# Optimizing a Trainium2 kernel written in Bass

```python
import math
import jax, jax.numpy as jnp
from jax import lax
import numpy as np

D_MODEL = 1024
BATCH = 1
SEQ = 256
DEPTH = 1

HEAD_DIM = 64
W_BR = D_MODEL // 2
N_BRANCH = 3
H_A = W_BR // HEAD_DIM
MOBA_BLOCK = 256
MOBA_TOPK = 3
MOBA_QCHUNK = 32
DIL_PAIRS = ((128, 1), (512, 4), (2048, 16))
N_DIL = len(DIL_PAIRS)
H_B = W_BR // HEAD_DIM
DIL_QCHUNK = 64
H_C = W_BR // HEAD_DIM
KV_C = 2
SWA_WINDOW = 128
N_BUCKETS = 32
REL_MAX_DIST = 2048
H_TOT = H_A + N_DIL * H_B + H_C
OFF_A = 0
OFF_B = H_A
OFF_C = H_A + N_DIL * H_B

EPS = 1e-6
NEG_INF = -1e30

SPLIT_SIZES = ([W_BR] * 4
               + [N_DIL * W_BR] * 3 + [W_BR]
               + [W_BR, KV_C * HEAD_DIM, KV_C * HEAD_DIM, W_BR]
               + [N_BRANCH * D_MODEL])
C_IN = int(sum(SPLIT_SIZES))
SPLIT_POINTS = [int(v) for v in np.cumsum(SPLIT_SIZES)[:-1]]


def rms_norm(x, g):
    x32 = x.astype(jnp.float32)
    y = x32 * lax.rsqrt(jnp.mean(x32 * x32, axis=-1, keepdims=True) + EPS)
    return (y * g.astype(jnp.float32)).astype(x.dtype)

def rel_bucket(dist):
    dist = jnp.maximum(dist, 0)
    max_exact = N_BUCKETS // 2
    log_ratio = jnp.log(jnp.maximum(dist, 1).astype(jnp.float32) / max_exact) / math.log(REL_MAX_DIST / max_exact)
    large = max_exact + (log_ratio * (N_BUCKETS - max_exact)).astype(jnp.int32)
    large = jnp.minimum(large, N_BUCKETS - 1)
    return jnp.where(dist < max_exact, dist, large)

def moba_attention(q, k, v, bias_tab):
    b, s, h, dh = q.shape
    s_pad = -(-s // MOBA_BLOCK) * MOBA_BLOCK
    pad = ((0, 0), (0, s_pad - s), (0, 0), (0, 0))
    qh, kh, vh = [jnp.pad(t, pad).transpose(0, 2, 1, 3) for t in (q, k, v)]
    nb = s_pad // MOBA_BLOCK
    kb = kh.reshape(b, h, nb, MOBA_BLOCK, dh)
    vb = vh.reshape(b, h, nb, MOBA_BLOCK, dh)
    k_mean = jnp.mean(kb.astype(jnp.float32), axis=3)
    gate = jnp.einsum('bhsd,bhnd->bhsn', qh.astype(jnp.float32), k_mean)
    q_blk = jnp.arange(s_pad) // MOBA_BLOCK
    past = jnp.arange(nb)[None, :] < q_blk[:, None]
    gate = jnp.where(past, gate, NEG_INF)
    n_sel = min(MOBA_TOPK, max(nb - 1, 1))
    _, top_idx = lax.top_k(gate, n_sel)
    sel_valid = jnp.arange(n_sel)[None, :] < jnp.minimum(q_blk, MOBA_TOPK)[:, None]
    scale = dh ** -0.5
    bias_tab = bias_tab.astype(jnp.float32)
    b_idx = jnp.arange(b)[:, None, None, None]
    h_idx = jnp.arange(h)[None, :, None, None]
    h_idx5 = jnp.arange(h)[None, :, None, None, None]
    blk_off = jnp.arange(MOBA_BLOCK)

    def chunk(c):
        t0 = c * MOBA_QCHUNK
        t = t0 + jnp.arange(MOBA_QCHUNK)
        q_c = lax.dynamic_slice_in_dim(qh, t0, MOBA_QCHUNK, axis=2)
        idx_c = lax.dynamic_slice_in_dim(top_idx, t0, MOBA_QCHUNK, axis=2)
        valid_c = lax.dynamic_slice_in_dim(sel_valid, t0, MOBA_QCHUNK, axis=0)
        k_sel = kb[b_idx, h_idx, idx_c]
        v_sel = vb[b_idx, h_idx, idx_c]
        s_sel = jnp.einsum('bhqd,bhqjkd->bhqjk', q_c, k_sel,
                           preferred_element_type=jnp.float32) * scale
        key_pos = idx_c[..., None] * MOBA_BLOCK + blk_off
        dist = t[:, None, None] - key_pos
        bias_sel = bias_tab[h_idx5, rel_bucket(dist)]
        s_sel = jnp.where(valid_c[:, :, None], s_sel + bias_sel, NEG_INF)
        n_own = t0 // MOBA_BLOCK
        k_own = lax.dynamic_index_in_dim(kb, n_own, axis=2, keepdims=False)
        v_own = lax.dynamic_index_in_dim(vb, n_own, axis=2, keepdims=False)
        s_own = jnp.einsum('bhqd,bhkd->bhqk', q_c, k_own,
                           preferred_element_type=jnp.float32) * scale
        dist_own = t[:, None] - (n_own * MOBA_BLOCK + blk_off)[None, :]
        s_own = jnp.where(dist_own >= 0, s_own + bias_tab[:, rel_bucket(dist_own)], NEG_INF)
        n_s = n_sel * MOBA_BLOCK
        logits = jnp.concatenate([s_sel.reshape(b, h, MOBA_QCHUNK, n_s), s_own], axis=-1)
        p = jax.nn.softmax(logits, axis=-1)
        p_sel = p[..., :n_s].reshape(b, h, MOBA_QCHUNK, n_sel, MOBA_BLOCK).astype(v.dtype)
        p_own = p[..., n_s:].astype(v.dtype)
        out = (jnp.einsum('bhqjk,bhqjkd->bhqd', p_sel, v_sel, preferred_element_type=jnp.float32)
               + jnp.einsum('bhqk,bhkd->bhqd', p_own, v_own, preferred_element_type=jnp.float32))
        return out.astype(v.dtype)

    out = lax.map(chunk, jnp.arange(s_pad // MOBA_QCHUNK))
    out = out.transpose(1, 0, 3, 2, 4).reshape(b, s_pad, h, dh)
    return out[:, :s]

def dilated_attention(q, k, v, bias_tab):
    b, s, _, h, dh = q.shape
    scale = dh ** -0.5
    bias_tab = bias_tab.astype(jnp.float32)
    n_keys = [w // d + 1 for (w, d) in DIL_PAIRS]
    k_pads = [jnp.pad(k[:, :, gi], ((0, 0), (w, 0), (0, 0), (0, 0))) for gi, (w, d) in enumerate(DIL_PAIRS)]
    v_pads = [jnp.pad(v[:, :, gi], ((0, 0), (w, 0), (0, 0), (0, 0))) for gi, (w, d) in enumerate(DIL_PAIRS)]
    bias_g = [bias_tab[gi * h:(gi + 1) * h][:, rel_bucket(d * jnp.arange(n_keys[gi]))]
              for gi, (w, d) in enumerate(DIL_PAIRS)]

    def chunk(c):
        t0 = c * DIL_QCHUNK
        t = t0 + jnp.arange(DIL_QCHUNK)
        q_c = lax.dynamic_slice_in_dim(q, t0, DIL_QCHUNK, axis=1)
        outs, lses = [], []
        for gi, (w, d) in enumerate(DIL_PAIRS):
            steps = jnp.arange(n_keys[gi]) * d
            idx = t[:, None] + w - steps[None, :]
            k_g = k_pads[gi][:, idx]
            v_g = v_pads[gi][:, idx]
            logits = jnp.einsum('bqhd,bqjhd->bhqj', q_c[:, :, gi], k_g,
                                preferred_element_type=jnp.float32) * scale + bias_g[gi][:, None, :]
            logits = jnp.where((t[:, None] - steps[None, :]) >= 0, logits, NEG_INF)
            lse = jax.nn.logsumexp(logits, axis=-1)
            p = jnp.exp(logits - lse[..., None]).astype(v.dtype)
            outs.append(jnp.einsum('bhqj,bqjhd->bqhd', p, v_g, preferred_element_type=jnp.float32))
            lses.append(lse)
        wts = jax.nn.softmax(jnp.stack(lses, axis=0), axis=0)
        out = sum(wts[gi].transpose(0, 2, 1)[..., None] * outs[gi] for gi in range(N_DIL))
        return out.astype(v.dtype)

    out = lax.map(chunk, jnp.arange(s // DIL_QCHUNK))
    return out.transpose(1, 0, 2, 3, 4).reshape(b, s, h, dh)

def swa_sink_attention(q, k, v, sinks, bias_tab):
    b, s, h, dh = q.shape
    kvh = k.shape[2]
    rep = h // kvh
    W = SWA_WINDOW
    nb = s // W
    scale = dh ** -0.5
    qb = q.reshape(b, nb, W, kvh, rep, dh)
    kb = k.reshape(b, nb, W, kvh, dh)
    vb = v.reshape(b, nb, W, kvh, dh)

    def with_prev(t):
        prev = jnp.pad(t, ((0, 0), (1, 0), (0, 0), (0, 0), (0, 0)))[:, :-1]
        return jnp.concatenate([prev, t], axis=2)

    kk, vv = with_prev(kb), with_prev(vb)
    logits = jnp.einsum('bnqgrd,bnkgd->bngrqk', qb, kk,
                        preferred_element_type=jnp.float32) * scale
    i = jnp.arange(W)
    j = jnp.arange(2 * W)
    dist = i[:, None] + W - j[None, :]
    key_pos = jnp.arange(nb)[:, None] * W - W + j[None, :]
    valid = ((dist >= 0) & (dist < W))[None] & (key_pos >= 0)[:, None, :]
    bias = bias_tab.astype(jnp.float32)[:, rel_bucket(dist)].reshape(kvh, rep, W, 2 * W)
    logits = jnp.where(valid[None, :, None, None], logits + bias, NEG_INF)
    sink = sinks.astype(jnp.float32).reshape(kvh, rep)[None, None, :, :, None, None]
    m = jnp.maximum(jnp.max(logits, axis=-1, keepdims=True), sink)
    e = jnp.exp(logits - m)
    p = e / (jnp.sum(e, axis=-1, keepdims=True) + jnp.exp(sink - m))
    out = jnp.einsum('bngrqk,bnkgd->bnqgrd', p.astype(v.dtype), vv, preferred_element_type=jnp.float32)
    return out.reshape(b, s, h, dh).astype(v.dtype)

def first_inputs(seed: int = 0) -> dict:
    key = jax.random.key(seed)
    ks = jax.random.split(key, 8)
    x = jax.random.normal(ks[0], (BATCH, SEQ, D_MODEL), jnp.float32)
    ln_g = 1.0 + 0.02 * jax.random.normal(ks[1], (DEPTH, D_MODEL), jnp.float32)
    w_in = jax.random.normal(ks[2], (DEPTH, D_MODEL, C_IN), jnp.float32) * D_MODEL ** -0.5
    qk_g = 1.0 + 0.02 * jax.random.normal(ks[3], (DEPTH, 6, HEAD_DIM), jnp.float32)
    sinks = 0.5 * jax.random.normal(ks[4], (DEPTH, H_C), jnp.float32)
    w_branch = jax.random.normal(ks[5], (DEPTH, N_BRANCH, W_BR, D_MODEL), jnp.float32) * W_BR ** -0.5
    w_out = jax.random.normal(ks[6], (DEPTH, D_MODEL, D_MODEL), jnp.float32) * D_MODEL ** -0.5
    rel_bias = 0.2 * jax.random.normal(ks[7], (H_TOT, N_BUCKETS), jnp.float32)
    return {"x": x, "ln_g": ln_g, "w_in": w_in, "qk_g": qk_g, "sinks": sinks,
            "w_branch": w_branch, "w_out": w_out, "rel_bias": rel_bias}

def first_block(x, ln_g, w_in, qk_g, sinks, w_branch, w_out, rel_bias):
    b, s, _ = x.shape
    for l in range(DEPTH):
        hn = rms_norm(x, ln_g[l])
        proj = jnp.einsum('bsd,dc->bsc', hn, w_in[l])
        (qa, ka, va, ga, qb, kb, vb, gb, qc, kc, vc, gc, gate_logits) = jnp.split(proj, SPLIT_POINTS, axis=-1)
        g = qk_g[l]
        qa = rms_norm(qa.reshape(b, s, H_A, HEAD_DIM), g[0])
        ka = rms_norm(ka.reshape(b, s, H_A, HEAD_DIM), g[1])
        o_a = moba_attention(qa, ka, va.reshape(b, s, H_A, HEAD_DIM), rel_bias[OFF_A:OFF_A + H_A])
        qb = rms_norm(qb.reshape(b, s, N_DIL, H_B, HEAD_DIM), g[2])
        kb = rms_norm(kb.reshape(b, s, N_DIL, H_B, HEAD_DIM), g[3])
        o_b = dilated_attention(qb, kb, vb.reshape(b, s, N_DIL, H_B, HEAD_DIM),
                                rel_bias[OFF_B:OFF_B + N_DIL * H_B])
        qc = rms_norm(qc.reshape(b, s, H_C, HEAD_DIM), g[4])
        kc = rms_norm(kc.reshape(b, s, KV_C, HEAD_DIM), g[5])
        o_c = swa_sink_attention(qc, kc, vc.reshape(b, s, KV_C, HEAD_DIM), sinks[l],
                                 rel_bias[OFF_C:OFF_C + H_C])
        branches = jnp.stack([o_a.reshape(b, s, W_BR) * jax.nn.silu(ga),
                              o_b.reshape(b, s, W_BR) * jax.nn.silu(gb),
                              o_c.reshape(b, s, W_BR) * jax.nn.silu(gc)], axis=2)
        br = jnp.einsum('bsiw,iwd->bsid', branches, w_branch[l])
        gates = jax.nn.sigmoid(gate_logits.reshape(b, s, N_BRANCH, D_MODEL))
        merged = jnp.sum(gates * br, axis=2)
        x = x + jnp.einsum('bsd,de->bse', merged, w_out[l])
    return x


D_MIX = D_MODEL
ATTN_HEADS = (D_MIX // 2) // HEAD_DIM
ATTN_DIM = ATTN_HEADS * HEAD_DIM
CONV_DIM = D_MIX - ATTN_DIM
CONV_K = 3
IDX_HEADS = 8
IDX_DIM = 64
IDX_SCALE = (IDX_DIM ** -0.5) * (IDX_HEADS ** -0.5)
TOPK_KEYS_MAX = 256
QUERY_BLOCK = 128
ROPE_THETA = 500000.0
ROPE_DIM = HEAD_DIM // 4
N_EXPERTS = 64
TOP_K_EXPERTS = 8
EXPERT_DIM = 256
SHARED_DIM = 256
ROUTED_SCALE = 2.5
DISPATCH_BLOCK = 128
IN_SPLITS = (CONV_DIM, CONV_DIM, CONV_DIM, ATTN_DIM, ATTN_DIM, ATTN_DIM,
             IDX_HEADS * IDX_DIM, IDX_DIM, IDX_HEADS)
IN_COLS = sum(IN_SPLITS)


def rms_norm_2(x, g):
    xf = x.astype(jnp.float32)
    y = xf * lax.rsqrt(jnp.mean(xf * xf, axis=-1, keepdims=True) + EPS)
    return y.astype(x.dtype) * g

def apply_partial_rope(x, positions):
    half = ROPE_DIM // 2
    inv_freq = ROPE_THETA ** (-jnp.arange(half, dtype=jnp.float32) / half)
    ang = positions.astype(jnp.float32)[..., None] * inv_freq
    ang = ang.reshape(ang.shape[:2] + (1,) * (x.ndim - 3) + (half,))
    cos, sin = jnp.cos(ang), jnp.sin(ang)
    x1 = x[..., :half].astype(jnp.float32)
    x2 = x[..., half:ROPE_DIM].astype(jnp.float32)
    rot = jnp.concatenate([x1 * cos - x2 * sin, x2 * cos + x1 * sin], axis=-1)
    return jnp.concatenate([rot.astype(x.dtype), x[..., ROPE_DIM:]], axis=-1)

def short_conv(u, w):
    up = jnp.pad(u, ((0, 0), (CONV_K - 1, 0), (0, 0)))
    return up[:, :-2] * w[0] + up[:, 1:-1] * w[1] + up[:, 2:] * w[2]

def dsa_attention(q, k, v, qi, ki, wi):
    B, S, H, Dh = q.shape
    n_sel = min(TOPK_KEYS_MAX, S // 4)
    n_blocks = S // QUERY_BLOCK
    key_pos = jnp.arange(S)

    def block(j):
        q0 = j * QUERY_BLOCK
        qb = lax.dynamic_slice_in_dim(q, q0, QUERY_BLOCK, axis=1)
        qib = lax.dynamic_slice_in_dim(qi, q0, QUERY_BLOCK, axis=1)
        wib = lax.dynamic_slice_in_dim(wi, q0, QUERY_BLOCK, axis=1)
        t_pos = q0 + jnp.arange(QUERY_BLOCK)
        rel = jax.nn.relu(jnp.einsum('bqhd,bsd->bqhs', qib, ki).astype(jnp.float32))
        score = jnp.einsum('bqhs,bqh->bqs', rel, wib.astype(jnp.float32)) * IDX_SCALE
        causal = key_pos[None, :] <= t_pos[:, None]
        score = jnp.where(causal[None], score, -jnp.inf)
        _, idx = lax.top_k(score, n_sel)
        valid = idx <= t_pos[None, :, None]
        flat = idx.reshape(B, QUERY_BLOCK * n_sel)
        ks = jax.vmap(lambda kb, ib: kb[ib])(k, flat).reshape(B, QUERY_BLOCK, n_sel, H, Dh)
        vs = jax.vmap(lambda vb, ib: vb[ib])(v, flat).reshape(B, QUERY_BLOCK, n_sel, H, Dh)
        s = jnp.einsum('bqhd,bqkhd->bhqk', qb, ks).astype(jnp.float32) * (Dh ** -0.5)
        s = jnp.where(valid[:, None], s, -jnp.inf)
        p = jax.nn.softmax(s, axis=-1).astype(vs.dtype)
        o = jnp.einsum('bhqk,bqkhd->bqhd', p, vs)
        return o.reshape(B, QUERY_BLOCK, H * Dh)

    out = lax.map(block, jnp.arange(n_blocks))
    return out.transpose(1, 0, 2, 3).reshape(B, S, H * Dh)

def swiglu(x, w1, w3, w2):
    return (jax.nn.silu(x @ w1) * (x @ w3)) @ w2

def moe(h, w_router, router_bias, w1, w3, w2, ws1, ws3, ws2):
    B, S, D = h.shape
    t = h.reshape(-1, D)
    n_tok = t.shape[0]
    scores = jax.nn.sigmoid((t @ w_router).astype(jnp.float32))
    _, eidx = lax.top_k(scores + router_bias.astype(jnp.float32), TOP_K_EXPERTS)
    g = jnp.take_along_axis(scores, eidx, axis=1)
    g = g / jnp.sum(g, axis=-1, keepdims=True) * ROUTED_SCALE
    n_pair = n_tok * TOP_K_EXPERTS
    flat_e = eidx.reshape(-1)
    flat_tok = jnp.arange(n_pair, dtype=jnp.int32) // TOP_K_EXPERTS
    flat_g = g.reshape(-1).astype(t.dtype)
    order = jnp.argsort(flat_e)
    se, stok, sg = flat_e[order], flat_tok[order], flat_g[order]
    counts = jnp.bincount(flat_e, length=N_EXPERTS)
    padded = (counts + DISPATCH_BLOCK - 1) // DISPATCH_BLOCK * DISPATCH_BLOCK
    start = jnp.cumsum(counts) - counts
    pend = jnp.cumsum(padded)
    pstart = pend - padded
    dest = pstart[se] + jnp.arange(n_pair) - start[se]
    rows = n_pair + N_EXPERTS * DISPATCH_BLOCK
    n_blk = rows // DISPATCH_BLOCK
    row_tok = jnp.zeros((rows,), jnp.int32).at[dest].set(stok)
    row_g = jnp.zeros((rows,), t.dtype).at[dest].set(sg)
    block_e = jnp.clip(jnp.searchsorted(pend, jnp.arange(n_blk) * DISPATCH_BLOCK, side='right'),
                       0, N_EXPERTS - 1)

    def expert_block(args):
        e, toks, gs = args
        xb = t[toks]
        return swiglu(xb, w1[e], w3[e], w2[e]) * gs[:, None]

    out = lax.map(expert_block, (block_e, row_tok.reshape(n_blk, DISPATCH_BLOCK),
                                 row_g.reshape(n_blk, DISPATCH_BLOCK)))
    routed = jax.ops.segment_sum(out.reshape(rows, D), row_tok, num_segments=n_tok)
    shared = swiglu(t, ws1, ws3, ws2)
    return (routed + shared).reshape(B, S, D)

def hybrid_layer(x, c, positions, norm1_g, norm2_g, w_ada, b_ada, w_in, conv_w,
                 q_norm_g, k_norm_g, kidx_norm_g, w_out, w_router, router_bias,
                 w1, w3, w2, ws1, ws3, ws2):
    B, S, D = x.shape
    ada = jax.nn.silu(c) @ w_ada + b_ada
    shift1, scale1, gate1, shift2, scale2, gate2 = [a[:, None, :] for a in jnp.split(ada, 6, axis=-1)]

    h = rms_norm_2(x, norm1_g) * (1 + scale1) + shift1
    proj = h @ w_in
    cuts = list(np.cumsum(IN_SPLITS)[:-1])
    xc, bg, cg, q, k, v, qi, ki, wi = jnp.split(proj, cuts, axis=-1)
    conv_out = bg * short_conv(cg * xc, conv_w)
    q = apply_partial_rope(rms_norm_2(q.reshape(B, S, ATTN_HEADS, HEAD_DIM), q_norm_g), positions)
    k = apply_partial_rope(rms_norm_2(k.reshape(B, S, ATTN_HEADS, HEAD_DIM), k_norm_g), positions)
    v = v.reshape(B, S, ATTN_HEADS, HEAD_DIM)
    qi = apply_partial_rope(qi.reshape(B, S, IDX_HEADS, IDX_DIM), positions)
    ki = apply_partial_rope(rms_norm_2(ki, kidx_norm_g), positions)
    attn_out = dsa_attention(q, k, v, qi, ki, wi)
    mix = jnp.concatenate([conv_out, attn_out], axis=-1) @ w_out
    x = x + gate1 * mix

    h2 = rms_norm_2(x, norm2_g) * (1 + scale2) + shift2
    x = x + gate2 * moe(h2, w_router, router_bias, w1, w3, w2, ws1, ws3, ws2)
    return x

def second_inputs(seed: int = 0) -> dict:
    key = jax.random.key(seed)
    ks = jax.random.split(key, 24)
    f32 = jnp.float32
    L, D, E, F, Fs = DEPTH, D_MODEL, N_EXPERTS, EXPERT_DIM, SHARED_DIM

    def nrm(k, shape, scale):
        return jax.random.normal(k, shape, f32) * scale

    positions = (jax.random.randint(ks[2], (BATCH, 1), 0, 1024, dtype=jnp.int32)
                 + jnp.arange(SEQ, dtype=jnp.int32)[None, :])
    return {
        "x": nrm(ks[0], (BATCH, SEQ, D), 1.0),
        "c": nrm(ks[1], (BATCH, D), 1.0),
        "positions": positions,
        "norm1_g": 1.0 + nrm(ks[3], (L, D), 0.02),
        "norm2_g": 1.0 + nrm(ks[4], (L, D), 0.02),
        "w_ada": nrm(ks[5], (L, D, 6 * D), 0.5 * D ** -0.5),
        "b_ada": nrm(ks[6], (L, 6 * D), 0.02),
        "w_in": nrm(ks[7], (L, D, IN_COLS), D ** -0.5),
        "conv_w": nrm(ks[8], (L, CONV_K, CONV_DIM), CONV_K ** -0.5),
        "q_norm_g": 1.0 + nrm(ks[9], (L, HEAD_DIM), 0.02),
        "k_norm_g": 1.0 + nrm(ks[10], (L, HEAD_DIM), 0.02),
        "kidx_norm_g": 1.0 + nrm(ks[11], (L, IDX_DIM), 0.02),
        "w_out": nrm(ks[12], (L, D_MIX, D), D_MIX ** -0.5),
        "w_router": nrm(ks[13], (L, D, E), D ** -0.5),
        "router_bias": nrm(ks[14], (L, E), 0.01),
        "w1": nrm(ks[15], (L, E, D, F), D ** -0.5),
        "w3": nrm(ks[16], (L, E, D, F), D ** -0.5),
        "w2": nrm(ks[17], (L, E, F, D), F ** -0.5),
        "ws1": nrm(ks[18], (L, D, Fs), D ** -0.5),
        "ws3": nrm(ks[19], (L, D, Fs), D ** -0.5),
        "ws2": nrm(ks[20], (L, Fs, D), Fs ** -0.5),
    }

def second_block(x, c, positions, norm1_g, norm2_g, w_ada, b_ada, w_in, conv_w,
              q_norm_g, k_norm_g, kidx_norm_g, w_out, w_router, router_bias,
              w1, w3, w2, ws1, ws3, ws2):
    for l in range(DEPTH):
        x = hybrid_layer(x, c, positions, norm1_g[l], norm2_g[l], w_ada[l], b_ada[l],
                         w_in[l], conv_w[l], q_norm_g[l], k_norm_g[l], kidx_norm_g[l],
                         w_out[l], w_router[l], router_bias[l], w1[l], w3[l], w2[l],
                         ws1[l], ws3[l], ws2[l])
    return x


def setup_inputs(seed=0):
    out = dict(first_inputs(seed))
    for name, value in second_inputs(seed + 1).items():
        if name != "x":
            out[name + "_2"] = value
    return out


def reference(
    x, ln_g, w_in, qk_g, sinks, w_branch, w_out, rel_bias, c_2, positions_2, norm1_g_2,
    norm2_g_2, w_ada_2, b_ada_2, w_in_2, conv_w_2, q_norm_g_2, k_norm_g_2, kidx_norm_g_2,
    w_out_2, w_router_2, router_bias_2, w1_2, w3_2, w2_2, ws1_2, ws3_2, ws2_2,
):
    x = first_block(
        x, ln_g, w_in, qk_g, sinks, w_branch, w_out, rel_bias,
    )
    return second_block(
        x, c_2, positions_2, norm1_g_2, norm2_g_2, w_ada_2, b_ada_2, w_in_2, conv_w_2,
        q_norm_g_2, k_norm_g_2, kidx_norm_g_2, w_out_2, w_router_2, router_bias_2, w1_2, w3_2,
        w2_2, ws1_2, ws3_2, ws2_2,
    )


_drawn_inputs = setup_inputs


def setup_inputs(seed=0):
    import zlib

    import numpy as np

    out = dict(_drawn_inputs(seed))
    spreads = {}
    factors = {'ln_g': 3.984,
     'qk_g': 5.259,
     'sinks': 56.136,
     'norm1_g_2': 8.825,
     'q_norm_g_2': 64.0,
     'k_norm_g_2': 64.0,
     'kidx_norm_g_2': 48.888,
     'norm2_g_2': 8.0,
     'w_router_2': 3.931,
     'router_bias_2': 8.0,
     'w1_2': 3.971,
     'w3_2': 3.718,
     'w2_2': 3.7,
     'ws1_2': 3.541,
     'ws3_2': 3.36,
     'ws2_2': 3.353}
    for name, (base, spread) in spreads.items():
        noise = np.random.default_rng([zlib.crc32(name.encode()), seed]).standard_normal(out[name].shape)
        drawn = base * np.exp(spread * noise) if base else spread * noise
        out[name] = __import__('jax').numpy.asarray(drawn.astype(out[name].dtype))
    for name, factor in factors.items():
        out[name] = (out[name] * factor).astype(out[name].dtype)
    return out
```

```python
import math

import numpy as np
import concourse.bass as bass
from concourse import mybir
from contextlib import ExitStack

F32 = mybir.dt.float32
I32 = mybir.dt.int32
ALU = mybir.AluOpType
ACT = mybir.ActivationFunctionType
AX = mybir.AxisListType

P = 128
TOK = 256
NT = TOK // P
DM = 1024
KT = DM // P
HD = 64
W_BR = 512
WK = W_BR // P
EPS = 1e-6
NEG = -1e30
TAKEN = -3e38
N_EXP = 64
ED = 256
FT = ED // P
TOP_KEYS = 64
SCALE = HD ** -0.5
IDX_SCALE = (64 ** -0.5) * (8 ** -0.5)
ROUTED = 2.5
NREL = 383
NREL_PAD = 384
CH = 512
N_ADA = 6 * DM // CH

C_ID, C_CAUS, C_FREQ, C_TRI, C_IOTA, C_COL, C_N = 0, 128, 384, 392, 456, 520, 521

CHUNKS = (
    [("q", 0, 512, 0), ("k", 512, 512, 0), ("v", 1024, 512, 0), ("silu", 1536, 512, 0)]
    + [("q", 2048 + 512 * g, 512, 4 + 4 * g) for g in range(3)]
    + [("k", 3584 + 512 * g, 512, 4 + 4 * g) for g in range(3)]
    + [("v", 5120 + 512 * g, 512, 512 + 512 * g) for g in range(3)]
    + [("silu", 6656, 512, 1)]
    + [("q", 7168, 512, 16), ("kv", 7680, 256, 16), ("silu", 7936, 512, 2)]
    + [("gate", 8448 + 512 * g, 512, 512 * g) for g in range(6)]
)
CHUNKS2 = [("qi", 3072, 512, 16), ("kiwi", 3584, 72, 24), ("q2", 1536, 512, 0), ("k2", 2048, 512, 8),
           ("v2", 2560, 512, 0), ("xc", 0, 512, 0), ("cg", 1024, 512, 0), ("bg", 512, 512, 0)]
N_QP, N_KP = 20, 18
V_COLS = 512 + 1536 + 128


def units_of(n):
    b, h = n // 8, n % 8
    if b == 0:
        return [(h // 2, h // 2, h % 2, 64 * h, h)]
    if b == 1:
        return [(4 + 4 * g + h // 2, 4 + 4 * g + h // 2, h % 2, 512 + 512 * g + 64 * h, 8 + 8 * g + h)
                for g in range(3)]
    return [(16 + h // 2, 16 + h // 4, h % 2, 2048 + 64 * (h // 4), 32 + h)]


def make_schedule():
    s = [("start",)]
    fill = []
    late = {}

    def project(c):
        for t in range(NT):
            fill.append(("proj", c, t))
            if CHUNKS[c][0] in ("q", "k", "kv"):
                late[len(fill) - 1] = ("turn", c, t)

    for c in range(len(CHUNKS)):
        project(c)
    seq = []
    pending = None
    for i, item in enumerate(fill):
        seq.append([item] + ([pending] if pending else []))
        pending = late.get(i)
    if pending:
        seq.append([pending])
    at = 0

    def take(k):
        nonlocal at
        for _ in range(k):
            if at < len(seq):
                s.extend(seq[at])
                at += 1

    take(9)
    ada = 0

    def head(n):
        s.append(("score", n))
        if n >= 1:
            s.append(("flip", n - 1))
            s.append(("value", n - 1))

    def modulation():
        nonlocal ada
        if ada < N_ADA:
            s.append(("ada", ada))
        if ada >= 1:
            s.append(("ada_out", ada - 1))
        ada += 1

    for n in range(8):
        head(n)
        take(3 if n < 4 else 2)
        if n >= 2:
            modulation()
    for n in range(8, 16):
        head(n)
        take(2 if n < 12 else 1)
        if n < 15:
            modulation()
        if n == 10:
            s.append(("turn_branch", 0))
    assert ada == N_ADA + 1
    for n in range(16, 24):
        head(n)
        take(1)
        if n == 18:
            s.append(("turn_branch", 1))
        if n == 17:
            s.extend(("branch", 0, hf, t) for hf in range(2) for t in range(NT))
        if n == 20:
            s.extend(("branch", 1, hf, t) for hf in range(2) for t in range(NT))
    take(99)
    s += [("flip", 23), ("value", 23), ("turn_branch", 2)]
    s.extend(("branch", 2, hf, t) for hf in range(2) for t in range(NT))
    s.append(("turn_merged",))
    s.extend(("out1", hf, t) for hf in range(2) for t in range(NT))
    s.append(("norm", 0))
    for c in range(5):
        s.extend(("proj2", c, t) for t in range(NT))
    s.append(("rope",))
    s.append(("turn2",))
    s.extend(("index", h) for h in range(8))
    s.append(("topk",))
    for c in range(5, 8):
        s.extend(("proj2", c, t) for t in range(NT))
    for h in range(8):
        s.append(("score", 24 + h))
        if h:
            s += [("flip", 23 + h), ("value", 23 + h)]
    s += [("flip", 31), ("value", 31), ("turn_branch", 3)]
    s.extend(("out2", hf, t) for hf in range(2) for t in range(NT))
    s.append(("norm", 1))
    s.append(("router",))
    return s


SCHEDULE = make_schedule()

RING = 3
WEIGHTS_OF = {"proj": "w_in", "ada": "w_ada", "branch": "w_branch", "out1": "w_out", "proj2": "w_in_2", "out2": "w_out_2"}
JOBS, JOB = [], {}
LAST_STEP = {}
for _it in SCHEDULE:
    if _it[0] in WEIGHTS_OF:
        _key = (WEIGHTS_OF[_it[0]], _it[1])
        if _key not in JOB:
            JOB[_key] = len(JOBS)
            JOBS.append(_key)
        LAST_STEP[JOB[_key]] = _it
for _key in (("shared_up",), ("shared_down",)):
    JOB[_key] = len(JOBS)
    JOBS.append(_key)

BANKED = [it for it in SCHEDULE if it[0] in ("proj", "branch", "out1", "proj2", "out2")]
USE = {it: n for n, it in enumerate(BANKED)}
HEADS = [it[1] for it in SCHEDULE if it[0] == "score"]
UNITS = [(n, g) for n in HEADS for g in range(len(units_of(n)) if n < 24 else 1)]
UNIT = {ng: u for u, ng in enumerate(UNITS)}
N_BIAS = sum(n < 24 for n, _ in UNITS)
BIAS_SLOTS = 6
TURNS = []
for _it in SCHEDULE:
    if _it[0] == "turn":
        TURNS.append(_it)
    if _it[0] == "turn_branch":
        TURNS += [_it + (t,) for t in range(NT)]
    if _it[0] in ("turn_merged", "norm", "start"):
        TURNS += [_it + (t, q) for t in range(NT) for q in range(2)]
    if _it[0] == "ada_out":
        TURNS.append(_it)
    if _it[0] == "turn2":
        TURNS += [_it + (g, t) for g in range(4) for t in range(NT)]
TURN = {it: n for n, it in enumerate(TURNS)}
NORMED = [it for it in BANKED if (it[0] == "proj" and CHUNKS[it[1]][0] in ("q", "k", "kv"))
          or (it[0] == "proj2" and CHUNKS2[it[1]][0] in ("q2", "k2", "kiwi"))]
NTH_NORM = {it: n for n, it in enumerate(NORMED)}
GATED = [it for it in BANKED if it[0] == "proj" and CHUNKS[it[1]][0] in ("silu", "gate")]
NTH_GATE = {it: n for n, it in enumerate(GATED)}
ESLOTS = 3
N_SMALL = 16
N_LATE = 6
ELOADS = 4


def build(nc, a, out):
    ctx = ExitStack()
    with ctx:
        def sb(name, shape, dt=F32, stack=ctx):
            return stack.enter_context(nc.sbuf_tensor(name, shape, dt))

        sems = {}

        def S(name):
            if name not in sems:
                sems[name] = ctx.enter_context(nc.semaphore(name))
            return sems[name]

        ctx.enter_context(nc.allow_non_contiguous_dma(reason="small vectors onto partitions"))
        rel_dram = nc.dram_tensor("rel_rows", (40, NREL_PAD), F32, kind="Internal").ap()
        gate_dram = nc.dram_tensor("expert_gates", (N_EXP, TOK), F32, kind="Internal").ap()

        ring = sb("ring", [P, RING, 4096])
        consts = sb("consts", [P, C_N])
        ident = consts[:, C_ID:C_ID + P]
        ones = sb("ones", [P, P])
        x = sb("x", [P, NT, DM])
        xT = sb("xT", [P, KT, TOK])
        ln_g = sb("ln_g_cols", [P, 3, KT])
        qk_g = sb("qk_g_cols", [P, 6])
        q_scale = sb("q_scale", [P, 3])
        g2 = sb("g2", [P, 3, HD])
        half_neg = sb("half_neg", [P, 8])
        c_col = sb("c_col", [P, 3, KT])
        b_ada = sb("b_ada_cols", [P, 6, KT])
        gate_bc = sb("gate_bc", [P, 2, DM])
        mod = sb("mod_cols", [P, 4, KT])
        ada_acc = sb("ada_acc", [P, 2, CH])
        sq = sb("squares", [P, CH])
        msum = sb("mean_squares", [P, 8])
        rstd = sb("rstd", [P, 8])
        xsum = sb("x_squares", [P, 1])
        L = sb("logits", [P, 2, 3, 386])
        PT = sb("probsT", [P, 2, 3, 384])
        nmax = sb("neg_max", [P, 2, 2])
        den = sb("den", [P, 2, 2])
        rden = sb("rden", [P, 2, 2])
        xn = PT[:, :, :, :].rearrange("p a g n -> p (a g n)")[:, 0:DM]
        spare = L[:, :, :, :].rearrange("p a g n -> p (a g n)")
        hot, relmask, relrow = spare[0:32, 0:384], spare[0:40, 384:768], spare[0:40, 768:1152]
        qn = sb("qn", [P, 2, CH])

        first = ExitStack()
        tabT = sb("tabT", [32, 40], F32, first)
        bias = sb("bias", [P, BIAS_SLOTS, 256], F32, first)
        qT = sb("qT", [P, N_QP, TOK], F32, first)
        kT = sb("kT", [P, N_KP, TOK], F32, first)
        V = sb("V", [P, NT, V_COLS], F32, first)
        O = sb("O", [P, 3, NT, W_BR], F32, first)
        OT = sb("OT", [P, WK, TOK], F32, first)
        G = sb("G", [P, NT, 3 * DM], F32, first)
        egate = sb("egate", [P, CH], F32, first)
        sinks = sb("sinks", [P, 8], F32, first)
        first.close()

        second = ExitStack()
        pos_i = sb("pos_i", [P, NT], I32, second)
        pos = sb("pos", [P, NT], F32, second)
        ang = sb("ang", [P, NT, 2, 8], F32, second)
        turns_f = sb("turns_f", [P, NT, 2, 8], F32, second)
        turns_i = sb("turns_i", [P, NT, 2, 8], I32, second)
        wrap = sb("wrap", [P, NT, 2, 8], F32, second)
        trig = sb("trig", [P, NT, 2, 8], F32, second)
        R = sb("rows2", [P, NT, 26, HD], F32, second)
        rt = sb("rope_tmp", [P, 4, 25, 8], F32, second)
        wi = sb("wi", [P, NT, 8], F32, second)
        V2 = sb("V2", [P, NT, CH], F32, second)
        T2 = sb("T2", [P, 13, TOK], F32, second)
        relu = sb("relu", [P, 2, 384], F32, second)
        score = sb("score", [P, 384], F32, second)
        top8 = sb("top8", [P, 2, 8], F32, second)
        selmask = sb("selmask", [P, 384], F32, second)
        xcT = sb("xcT", [P, WK, TOK], F32, second)
        uT = sb("uT", [P, WK, TOK + 2], F32, second)
        cv = sb("cv", [P, TOK], F32, second)
        conv_w = sb("conv_w_cols", [P, 3, WK], F32, second)
        O2 = sb("O2", [P, NT, W_BR], F32, second)
        mixT = sb("mixT", [P, KT, TOK], F32, second)
        w_router = sb("w_router", [P, KT, N_EXP], F32, second)
        rbias = sb("router_bias", [P, N_EXP], F32, second)
        sig = sb("sig", [P, NT, N_EXP], F32, second)
        rarg = sb("rarg", [P, 2, NT, N_EXP], F32, second)
        rexp = sb("rexp", [P, 2, NT, N_EXP], F32, second)
        sel = sb("sel", [P, NT, N_EXP], F32, second)
        gsum = sb("gsum", [P, NT], F32, second)
        gT = sb("gT", [N_EXP, TOK], F32, second)
        used = sb("used", [N_EXP, 1], F32, second)
        place = sb("place", [N_EXP, 1], F32, second)
        order = sb("order", [N_EXP, N_EXP], F32, second)
        elist = sb("elist", [1, N_EXP + 1 + ESLOTS], I32, second)
        hT = sb("hT", [P, FT, TOK], F32, second)
        hs = sb("hs", [P, FT, TOK], F32, second)
        gb = sb("gate_rows", [P, ESLOTS, TOK], F32, second)
        own = sb("expert_w", [P, 6144], F32, second)
        flat = ring[:, :, :].rearrange("p r n -> p (r n)")
        ew = [own[:, :], flat[:, 0:6144], flat[:, 6144:12288]]
        second.close()

        bank = [ctx.enter_context(nc.psum_tensor(f"bank{i}", [P, 512], F32)) for i in range(8)]
        proj_b, score_b, flip_b, value_b, turn_b = bank[0:2], bank[2:4], bank[4:6], bank[6], bank[7]
        acc_b, up_b = bank[0:4], bank[4:6]

        block = ctx.enter_context(nc.Block())

        def view(j, kind):
            slot = ring[:, j % RING, :]
            if kind == "k8":
                return slot.rearrange("p (k n) -> p k n", k=KT)
            if kind == "k4":
                return slot.rearrange("p (k n) -> p k n", k=WK)
            if kind == "kiwi":
                return slot[:, 0:KT * 72].rearrange("p (k n) -> p k n", k=KT)
            if kind == "kv":
                return slot[:, 0:KT * 256].rearrange("p (k n) -> p k n", k=KT)
            if kind == "up":
                return slot.rearrange("p (m k n) -> p m k n", m=2, k=KT)
            return slot[:, 0:FT * DM].rearrange("p (f n) -> p f n", f=FT)

        def job_ready(eng, j):
            eng.wait_ge(S(f"ring_loaded_{j % RING}"), 16 * (2 if JOBS[j][0] == "shared_up" else 1)
                        + 16 * sum(1 for i in range(j % RING, j, RING)))

        @block.sync
        def _(sp):
            d_rows = "(p k) n -> p k n"

            def load(j):
                kind, arg = JOBS[j][0], JOBS[j][1:]
                done = S(f"ring_loaded_{j % RING}")
                if j >= RING:
                    last = LAST_STEP[j - RING]
                    if last[0] == "ada":
                        sp.wait_ge(S("ada_summed"), last[1] + 1)
                    else:
                        sp.wait_ge(S("bank_full"), USE[last] + 1)
                if kind == "w_in":
                    _, c0, w, _ = CHUNKS[arg[0]]
                    src = a["w_in"][0].rearrange(d_rows, k=KT)[:, :, c0:c0 + w]
                    sp.dma_start(view(j, "kv" if w == 256 else "k8"), src).then_inc(done, 16)
                elif kind == "w_in_2":
                    _, c0, w, _ = CHUNKS2[arg[0]]
                    src = a["w_in_2"][0].rearrange(d_rows, k=KT)[:, :, c0:c0 + w]
                    sp.dma_start(view(j, "kiwi" if w == 72 else "k8"), src).then_inc(done, 16)
                elif kind == "w_ada":
                    src = a["w_ada_2"][0].rearrange(d_rows, k=KT)[:, :, CH * arg[0]:CH * arg[0] + CH]
                    sp.dma_start(view(j, "k8"), src).then_inc(done, 16)
                elif kind == "w_branch":
                    src = a["w_branch"][0, arg[0]].rearrange("(k p) n -> p k n", p=P)
                    sp.dma_start(view(j, "k4"), src).then_inc(done, 16)
                elif kind == "w_out":
                    src = a["w_out"][0].rearrange("(k p) n -> p k n", p=P)[:, :, CH * arg[0]:CH * arg[0] + CH]
                    sp.dma_start(view(j, "k8"), src).then_inc(done, 16)
                elif kind == "w_out_2":
                    src = a["w_out_2"][0].rearrange("(k p) n -> p k n", p=P)[:, :, CH * arg[0]:CH * arg[0] + CH]
                    sp.dma_start(view(j, "k8"), src).then_inc(done, 16)
                elif kind == "shared_up":
                    for m, name in enumerate(("ws1_2", "ws3_2")):
                        sp.dma_start(view(j, "up")[:, m], a[name][0].rearrange(d_rows, k=KT)).then_inc(done, 16)
                else:
                    sp.dma_start(view(j, "down"), a["ws2_2"][0].rearrange("(p f) n -> p f n", f=FT))\
                      .then_inc(done, 16)

            at = 0
            for it in SCHEDULE:
                if it[0] == "start":
                    for t in range(NT):
                        sp.dma_start(x[:, t, :], a["x"][0, t * P:(t + 1) * P, :]).then_inc(S(f"x_loaded_{t}"), 16)
                if it[0] == "score" and it[1] < 24:
                    for g, (_, _, _, _, row) in enumerate(units_of(it[1])):
                        u = UNIT[it[1], g]
                        if u == 0:
                            sp.wait_ge(S("rel_ready"), 1)
                            sp.dma_start(rel_dram, relrow).then_inc(S("rel_stored"), 16)
                            sp.wait_ge(S("rel_stored"), 16)
                        if u >= BIAS_SLOTS:
                            sp.wait_ge(S("logits"), u - BIAS_SLOTS + 1)
                        src = bass.AP(rel_dram.tensor, row * NREL_PAD, [[1, P], [1, 2 * P]])
                        sp.dma_start(bias[:, u % BIAS_SLOTS, :], src).then_inc(S(f"bias_loaded_{u % BIAS_SLOTS}"), 16)
                if it[0] in WEIGHTS_OF and (WEIGHTS_OF[it[0]], it[1]) == JOBS[at]:
                    load(at)
                    at += 1
            for j in range(at, len(JOBS)):
                load(j)

            sp.wait_ge(S("gT_ready"), 1)
            sp.dma_start(gate_dram, gT[:, :]).then_inc(S("gates_stored"), 16)
            sp.wait_ge(S("gates_stored"), 16)
            sp.wait_ge(S("elist_ready"), 2)
            n_used = sp.value_load(elist[0:1, 0:1], min_val=0, max_val=N_EXP)

            def load_expert(i, r):
                e = sp.value_load(elist[0:1, bass.ds(i + 1, 1)], min_val=0, max_val=N_EXP - 1)
                done = S(f"expert_loaded_{r}")
                for m, name in enumerate(("w1_2", "w3_2")):
                    src = a[name][0].rearrange("e (p k) n -> p e (k n)", k=KT)[:, bass.ds(e, 1), :]
                    sp.dma_start(ew[r][:, 2048 * m:2048 * m + 2048].unsqueeze(1), src).then_inc(done, 16)
                src = a["w2_2"][0].rearrange("e (p f) n -> p e (f n)", f=FT)[:, bass.ds(e, 1), :]
                sp.dma_start(ew[r][:, 4096:6144].unsqueeze(1), src).then_inc(done, 16)
                sp.dma_start(gb[:, r, :], gate_dram[bass.ds(e, 1), :].to_broadcast([P, TOK])).then_inc(done, 16)

            for r in range(ESLOTS):
                if r == 1:
                    sp.wait_ge(S("shared_done"), 1)
                with sp.If(n_used > r):
                    load_expert(r, r)
            with sp.Fori(1, -(-N_EXP // ESLOTS)) as m:
                for r in range(ESLOTS):
                    with sp.If(n_used > m * ESLOTS + r):
                        sp.wait_ge(S("expert_done"), (m - 1) * ESLOTS + r + 1)
                        load_expert(m * ESLOTS + r, r)
            for t in range(NT):
                sp.wait_ge(S("out_ready"), 2 * t + 2)
                sp.dma_start(out[0, t * P:(t + 1) * P, :], x[:, t, :]).then_inc(S("out_stored"), 16)
            sp.wait_ge(S("out_stored"), 16 * NT)

        @block.gpsimd
        def _(gp):
            gp.memset(half_neg[:, :], -0.5).then_inc(S("half_neg_set"), 1)
            gp.memset(ones[:, :], 1.0).then_inc(S("ones_set"), 1)
            small = S("small_loaded")
            gp.dma_start(consts[:, :], a["c_square"]).then_inc(S("consts_loaded"), 16)
            gp.dma_start(hot, a["c_hot"]).then_inc(small, 16)
            gp.dma_start(relmask, a["c_mask"]).then_inc(small, 16)
            gp.dma_start(tabT[:, :], a["rel_bias"].rearrange("h b -> b h")).then_inc(small, 16)
            for i, name in enumerate(("ln_g", "norm1_g_2", "norm2_g_2")):
                gp.dma_start(ln_g[:, i, :], a[name][0].rearrange("(p k) -> p k", k=KT)).then_inc(small, 16)
            gp.dma_start(c_col[:, 0, :], a["c_2"][0].rearrange("(p k) -> p k", k=KT)).then_inc(small, 16)
            gp.dma_start(b_ada[:, :, :], a["b_ada_2"][0].rearrange("(s p k) -> p s k", s=6, k=KT)).then_inc(small, 16)
            for h in range(2):
                gp.dma_start(qk_g[HD * h:HD * h + HD, :], a["qk_g"][0].rearrange("g d -> d g")).then_inc(small, 16)
            gp.dma_start(sinks[:, :], a["sinks"].to_broadcast([P, 8])).then_inc(small, 16)
            for i, name in enumerate(("q_norm_g_2", "k_norm_g_2", "kidx_norm_g_2")):
                gp.dma_start(g2[:, i, :], a[name].to_broadcast([P, HD])).then_inc(small, 16)
            for i, s in enumerate((2, 5)):
                gp.dma_start(gate_bc[:, i, :], a["b_ada_2"][0:1, s * DM:(s + 1) * DM].to_broadcast([P, DM])).then_inc(small, 16)
            gp.wait_ge(S("half_neg_set"), 1)

            def inverse_root(width, count, ready, nth, done):
                gp.wait_ge(S(ready), nth)
                gp.tensor_scalar(msum[:, 0:width], msum[:, 0:width], 1.0 / count, EPS, ALU.mult, ALU.add)\
                  .then_inc(S("mean_eps"), 1)
                inverse_root.n += 1
                gp.wait_ge(S("mean_eps"), inverse_root.n)
                gp.tensor_tensor(rstd[:, 0:width], msum[:, 0:width], half_neg[:, 0:width], ALU.pow)\
                  .then_inc(S(done), 1)
            inverse_root.n = 0
            nx = 0
            for it in SCHEDULE:
                if it[0] in ("start", "norm"):
                    for t in range(NT):
                        nx += 1
                        inverse_root(1, DM, "x_squared", nx, "x_rstd")
                if it in NTH_NORM:
                    kind = CHUNKS[it[1]][0] if it[0] == "proj" else CHUNKS2[it[1]][0]
                    inverse_root({"kv": 2, "kiwi": 1}.get(kind, 8), HD, "head_sums", NTH_NORM[it] + 1, "head_rstd")
                if it[0] == "out1" and it[1:] == (1, 1):
                    gp.wait_ge(S("bank_free"), USE[it] + 1)
                    late = S("late_loaded")
                    gp.dma_start(pos_i[:, :], a["positions_2"][0].rearrange("(t p) -> p t", p=P)).then_inc(late, 16)
                    for j in range(3):
                        gp.dma_start(conv_w[:, j, :], a["conv_w_2"][0, j].rearrange("(k p) -> p k", p=P)).then_inc(late, 16)
                    gp.dma_start(w_router[:, :, :], a["w_router_2"][0].rearrange("(p k) n -> p k n", k=KT)).then_inc(late, 16)
                    gp.dma_start(rbias[:, :], a["router_bias_2"].to_broadcast([P, N_EXP])).then_inc(late, 16)

        @block.scalar
        def _(act):
            def x_square(t, nth):
                if nth >= 1:
                    act.wait_ge(S("x_rstd"), nth)
                    act.wait_ge(S("x_scaled"), nth)
                act.activation(qn[:, :, :].rearrange("p a n -> p (a n)"), x[:, t, :], ACT.Square, accum_out=msum[:, 0:1]).then_inc(S("x_squared"), 1)

            nx = 0
            n_silu_c = 0
            for it in SCHEDULE:
                if it[0] == "start":
                    for t in range(NT):
                        act.wait_ge(S(f"x_loaded_{t}"), 16)
                        x_square(t, nx)
                        nx += 1
                    act.wait_ge(S("small_loaded"), 16 * N_SMALL)
                    act.activation(c_col[:, 1, :], c_col[:, 0, :], ACT.Exp, scale=-1.0).then_inc(S("c_exp"), 1)
                if it[0] == "norm":
                    for t in range(NT):
                        act.wait_ge(S("bank_free"), USE[("out1" if it[1] == 0 else "out2", 1, 1)] + 1)
                        x_square(t, nx)
                        nx += 1
                if it[0] in ("proj", "proj2"):
                    n = USE[it]
                    kind, _, w, dst = (CHUNKS if it[0] == "proj" else CHUNKS2)[it[1]]
                    ps = proj_b[n % 2]
                    if it in NTH_NORM:
                        m = NTH_NORM[it]
                        w = {"kv": 128, "kiwi": 64}.get(kind, 512)
                        act.wait_ge(S("bank_full"), n + 1)
                        if m >= 1:
                            act.wait_ge(S("head_sums"), m)
                        act.activation(sq[:, 0:w], ps[:, 0:w], ACT.Square).then_inc(S("squared"), 1)
                    if it in NTH_GATE:
                        m = NTH_GATE[it]
                        act.wait_ge(S("bank_full"), n + 1)
                        if m >= 1:
                            act.wait_ge(S("gate_taken"), m)
                        act.activation(egate[:, :], ps[:, :], ACT.Exp, scale=-1.0).then_inc(S("gate_exp"), 1)
                if it[0] == "turn":
                    k = TURN[it]
                    kind, _, _, dst = CHUNKS[it[1]]
                    t = it[2]
                    act.wait_ge(S("turned"), k + 1)
                    src = turn_b[:, :].rearrange("p (b n) -> p b n", b=4)
                    if kind == "q":
                        br = 0 if dst < 4 else (1 if dst < 16 else 2)
                        act.wait_ge(S("q_scale_ready"), 2)
                        act.activation(qT[:, dst:dst + 4, t * P:(t + 1) * P], src, ACT.Copy,
                                       scale=q_scale[:, br:br + 1]).then_inc(S("turn_free"), 1)
                    elif kind == "k":
                        act.activation(kT[:, dst:dst + 4, t * P:(t + 1) * P], src, ACT.Copy).then_inc(S("turn_free"), 1)
                    else:
                        act.activation(kT[:, dst:dst + 2, t * P:(t + 1) * P], src[:, 0:2], ACT.Copy)\
                           .then_inc(S("turn_free"), 1)
                if it[0] == "turn_branch":
                    i = it[1]
                    dst = OT if i < 3 else mixT[:, WK:2 * WK, :]
                    for t in range(NT):
                        k = TURN[it + (t,)]
                        act.wait_ge(S("turned"), k + 1)
                        if i in (1, 2) and t == 0:
                            act.wait_ge(S("bank_full"), USE[("branch", i - 1, 1, 1)] + 1)
                        act.activation(dst[:, :, t * P:(t + 1) * P],
                                       turn_b[:, :].rearrange("p (b n) -> p b n", b=4), ACT.Copy)\
                           .then_inc(S("turn_free"), 1)
                if it[0] == "turn_merged":
                    for t in range(NT):
                        for q in range(2):
                            act.wait_ge(S("turned"), TURN[it + (t, q)] + 1)
                            act.activation(xT[:, 4 * q:4 * q + 4, t * P:(t + 1) * P],
                                           turn_b[:, :].rearrange("p (b n) -> p b n", b=4), ACT.Copy)\
                               .then_inc(S("turn_free"), 1)
                if it[0] == "turn2":
                    for g in range(4):
                        for t in range(NT):
                            act.wait_ge(S("turned"), TURN[it + (g, t)] + 1)
                            nb = 4 if g < 3 else 1
                            act.activation(T2[:, 4 * g:4 * g + nb, t * P:(t + 1) * P],
                                           turn_b[:, 0:P * nb].rearrange("p (b n) -> p b n", b=nb), ACT.Copy,
                                           scale=SCALE if g == 0 else 1.0).then_inc(S("turn_free"), 1)
                if it[0] == "rope":
                    act.wait_ge(S("angles_ready"), 1)
                    act.activation(trig[:, :, :, :], ang[:, :, :, :], ACT.Sin).then_inc(S("trig_ready"), 1)
                if it[0] == "index":
                    u = len(UNITS) + it[1]
                    h = it[1]
                    act.wait_ge(S("index_product"), h + 1)
                    if h >= 2:
                        act.wait_ge(S("index_added"), h - 1)
                    act.activation(relu[:, h % 2, :], score_b[h % 2][:, 0:384], ACT.Relu).then_inc(S("relu_done"), 1)
                if it[0] == "score":
                    n = it[1]
                    ng = len(units_of(n)) if n < 24 else 1
                    sink = 1 if 16 <= n < 24 else 0
                    i = HEADS.index(n)
                    act.wait_ge(S("maxed"), 2 * i + 2)
                    for t in range(NT):
                        lo, w = (0, P + sink) if t == 0 else (P + 1, 2 * P + sink)
                        v = L[:, i % 2, 0:ng, lo:lo + w]
                        act.activation(v, v, ACT.Exp, bias=nmax[:, i % 2, t:t + 1],
                                       accum_out=den[:, i % 2, t:t + 1]).then_inc(S("probs"), 1)
                if it[0] == "flip":
                    n = it[1]
                    ng = len(units_of(n)) if n < 24 else 1
                    i = HEADS.index(n)
                    for g in range(ng):
                        u = UNIT[n, g]
                        act.wait_ge(S("flipped"), u + 1)
                        if i >= 2:
                            act.wait_ge(S("value_product"), 2 * (i - 1))
                        act.activation(PT[:, i % 2, g, :], flip_b[u % 2][:, 0:384], ACT.Copy).then_inc(S("probsT"), 1)
                if it[0] == "router":
                    act.wait_ge(S("router_args"), 2)
                    act.activation(rexp[:, :, :, :], rarg[:, :, :, :], ACT.Exp).then_inc(S("router_exp"), 1)

            def silu_part(f, wait_on, value):
                act.wait_ge(wait_on, value)
                act.activation(hs[:, f, :], up_b[f][:, 0:TOK], ACT.Silu).then_inc(S(f"silu_{f}"), 1)

            for f in range(FT):
                silu_part(f, S(f"up_{f}"), 1)
            act.wait_ge(S("elist_ready"), 2)
            n_used = act.value_load(elist[0:1, 0:1], min_val=0, max_val=N_EXP)
            with act.Fori(0, N_EXP) as i:
                with act.If(n_used > i):
                    for f in range(FT):
                        act.wait_ge(S(f"h_ready_{f}"), i + 1)
                        silu_part(f, S(f"up_{f}"), i + 2)

        @block.vector
        def _(dve):
            n_scaled = 0

            def x_scale(t):
                nonlocal n_scaled
                dve.wait_ge(S("x_rstd"), n_scaled + 1)
                dve.tensor_scalar(xn, x[:, t, :], rstd[:, 0:1], None, ALU.mult).then_inc(S("x_scaled"), 1)
                n_scaled += 1

            def bc(ap2, n):
                return ap2.unsqueeze(2).to_broadcast([ap2.shape[0], ap2.shape[1], n])

            n_gt = 0
            n_idx = 0
            for it in SCHEDULE:
                kind0 = it[0]
                if kind0 in ("start", "norm"):
                    w = 0 if kind0 == "start" else 1 + it[1]
                    if kind0 == "start":
                        dve.wait_ge(S("small_loaded"), 16 * N_SMALL)
                    if kind0 == "norm":
                        m = it[1]
                        dve.wait_ge(S("turn_free"), TURN["ada_out", N_ADA - 1] + 1)
                        dve.tensor_tensor(mod[:, 2 * m + 1, :], mod[:, 2 * m + 1, :], ln_g[:, w, :], ALU.mult)\
                           .then_inc(S("mod_ready"), 1)
                    for t in range(NT):
                        x_scale(t)
                        for q in range(2):
                            dve.wait_ge(S("turned"), TURN[it + (t, q)] + 1)
                            src = turn_b[:, :].rearrange("p (b n) -> p b n", b=4)
                            if kind0 == "start":
                                dve.tensor_tensor(xT[:, 4 * q:4 * q + 4, t * P:(t + 1) * P], src,
                                                  bc(ln_g[:, 0, 4 * q:4 * q + 4], P), ALU.mult).then_inc(S("turn_free"), 1)
                            else:
                                dve.wait_ge(S("mod_ready"), m + 1)
                                for b in range(4):
                                    k = 4 * q + b
                                    last = dve.tensor_scalar(xT[:, k, t * P:(t + 1) * P], src[:, b],
                                                             mod[:, 2 * m + 1, k:k + 1], mod[:, 2 * m, k:k + 1],
                                                             ALU.mult, ALU.add)
                                last.then_inc(S("turn_free"), 1)
                if kind0 == "start":
                    dve.wait_ge(S("c_exp"), 1)
                    dve.tensor_scalar(c_col[:, 1, :], c_col[:, 1, :], 1.0, None, ALU.add).then_inc(S("c_step"), 1)
                    dve.wait_ge(S("c_step"), 1)
                    dve.reciprocal(c_col[:, 2, :], c_col[:, 1, :]).then_inc(S("c_step"), 1)
                    dve.wait_ge(S("c_step"), 2)
                    dve.tensor_tensor(c_col[:, 1, :], c_col[:, 0, :], c_col[:, 2, :], ALU.mult).then_inc(S("c_step"), 1)
                    gains = qk_g[:, :].rearrange("p (b two) -> p b two", two=2)
                    dve.tensor_tensor(q_scale[:, :], gains[:, :, 0], gains[:, :, 1], ALU.mult).then_inc(S("q_scale_ready"), 1)
                    dve.wait_ge(S("q_scale_ready"), 1)
                    dve.tensor_scalar(q_scale[:, :], q_scale[:, :], SCALE, None, ALU.mult).then_inc(S("q_scale_ready"), 1)
                    dve.wait_ge(S("rel_product"), 1)
                    dve.tensor_tensor(relrow, bank[6][0:40, 0:NREL_PAD], relmask, ALU.add)\
                       .then_inc(S("rel_ready"), 1)
                if kind0 in ("proj", "proj2"):
                    n, t = USE[it], it[2]
                    kind, _, w, dst = (CHUNKS if kind0 == "proj" else CHUNKS2)[it[1]]
                    ps = proj_b[n % 2]
                    free = S("bank_free")
                    if it in NTH_NORM:
                        m = NTH_NORM[it]
                        nh = {"kv": 2, "kiwi": 1}.get(kind, 8)
                        dve.wait_ge(S("squared"), m + 1)
                        if m >= 1:
                            dve.wait_ge(S("head_rstd"), m)
                        dve.tensor_reduce(msum[:, 0:nh], sq[:, 0:nh * HD].rearrange("p (h d) -> p h d", d=HD),
                                          AX.X, ALU.add).then_inc(S("head_sums"), 1)
                        dve.wait_ge(S("head_rstd"), m + 1)
                        heads = ps[:, 0:nh * HD].rearrange("p (h d) -> p h d", d=HD)
                        r8 = bc(rstd[:, 0:nh], HD)
                        if kind in ("q", "k"):
                            if m >= 2:
                                dve.wait_ge(S("turned"), TURN[("turn",) + NORMED[m - 2][1:]] + 1)
                            dve.tensor_tensor(qn[:, m % 2, :].rearrange("p (h d) -> p h d", d=HD), heads, r8, ALU.mult)\
                               .then_inc(free, 1)
                        elif kind == "kv":
                            dve.wait_ge(S("turned"), TURN[("turn",) + NORMED[m - 2][1:]] + 1)
                            o = qn[:, m % 2, 0:256].rearrange("p (g c d) -> p g c d", g=2, c=2)
                            for c in range(2):
                                dve.tensor_tensor(o[:, :, c, :], heads, r8, ALU.mult).then_inc(S("kv_step"), 1)
                            dve.tensor_copy(V[:, t, 2048:2176], ps[:, 128:256]).then_inc(free, 1)
                        else:
                            gi = {"q2": 0, "k2": 1, "kiwi": 2}[kind]
                            o = R[:, t, dst:dst + nh, :]
                            dve.tensor_tensor(o, heads, r8, ALU.mult).then_inc(S("r2_step"), 1)
                            n_gt += 1
                            dve.wait_ge(S("r2_step"), n_gt)
                            gains = g2[:, gi:gi + 1, :].to_broadcast([P, nh, HD])
                            if kind == "kiwi":
                                dve.tensor_copy(wi[:, t, :], ps[:, 64:72]).then_inc(S("wi_ready"), 1)
                            dve.tensor_tensor(o, o, gains, ALU.mult).then_inc(free, 1)
                    elif kind == "v":
                        dve.wait_ge(S("bank_full"), n + 1)
                        dve.tensor_copy(V[:, t, dst:dst + 512], ps[:, :]).then_inc(free, 1)
                    elif kind == "v2":
                        dve.wait_ge(S("bank_full"), n + 1)
                        dve.tensor_copy(V2[:, t, :], ps[:, :]).then_inc(free, 1)
                    elif kind == "qi":
                        dve.wait_ge(S("bank_full"), n + 1)
                        dve.tensor_copy(R[:, t, dst:dst + 8, :], ps[:, :].rearrange("p (h d) -> p h d", d=HD))\
                           .then_inc(free, 1)
                    elif kind in ("silu", "gate"):
                        m = NTH_GATE[it]
                        o = O[:, dst, t, :] if kind == "silu" else G[:, t, dst:dst + 512]
                        dve.wait_ge(S("gate_exp"), m + 1)
                        dve.tensor_scalar(o, egate[:, :], 1.0, None, ALU.add).then_inc(S("gate_taken"), 1)
                        dve.wait_ge(S("gate_taken"), m + 1)
                        if kind == "gate":
                            dve.reciprocal(o, o).then_inc(free, 1)
                        else:
                            dve.reciprocal(o, o).then_inc(S("silu_step"), 1)
                            dve.wait_ge(S("silu_step"), 2 * dst + t + 1)
                            dve.tensor_tensor(o, ps[:, :], o, ALU.mult).then_inc(free, 1)
                    else:
                        v = ps[:, :].rearrange("p (c n) -> p c n", c=2)
                        dve.wait_ge(S("bank_full"), n + 1)
                        if kind == "xc":
                            dve.tensor_copy(xcT[:, 2 * t:2 * t + 2, :], v).then_inc(free, 1)
                        elif kind == "cg":
                            dve.wait_ge(free, n)
                            if t == 0:
                                dve.memset(uT[:, :, 0:2], 0.0).then_inc(S("u_pad"), 1)
                            dve.tensor_tensor(uT[:, 2 * t:2 * t + 2, 2:TOK + 2], v, xcT[:, 2 * t:2 * t + 2, :], ALU.mult)\
                               .then_inc(free, 1)
                        else:
                            dve.wait_ge(free, n)
                            dve.wait_ge(S("late_loaded"), 16 * N_LATE)
                            dve.wait_ge(S("u_pad"), 1)
                            for c in range(2):
                                ct = 2 * t + c
                                s0 = 4 * ct - ct // 2
                                if ct:
                                    dve.wait_ge(S("conv_step"), s0)
                                dve.tensor_scalar(cv[:, :], uT[:, ct, 0:TOK], conv_w[:, 0, ct:ct + 1], None, ALU.mult)\
                                   .then_inc(S("conv_step"), 1)
                                for j in (1, 2):
                                    dve.wait_ge(S("conv_step"), s0 + j)
                                    dve.scalar_tensor_tensor(out=cv[:, :], in0=uT[:, ct, j:TOK + j],
                                                             scalar=conv_w[:, j, ct:ct + 1], in1=cv[:, :],
                                                             op0=ALU.mult, op1=ALU.add).then_inc(S("conv_step"), 1)
                                dve.wait_ge(S("conv_step"), s0 + 3)
                                dve.tensor_tensor(mixT[:, ct, :], v[:, c], cv[:, :], ALU.mult)\
                                   .then_inc(free if c else S("conv_step"), 1)
                if kind0 == "branch":
                    _, i, hf, t = it
                    n = USE[it]
                    g = G[:, t, i * DM + hf * CH:i * DM + hf * CH + CH]
                    g0 = G[:, t, hf * CH:hf * CH + CH]
                    dve.wait_ge(S("bank_full"), n + 1)
                    if i == 0:
                        dve.wait_ge(S("bank_free"), n)
                        dve.tensor_tensor(g, g, proj_b[n % 2][:, :], ALU.mult).then_inc(S("bank_free"), 1)
                    else:
                        dve.wait_ge(S("bank_free"), n)
                        dve.tensor_tensor(g, g, proj_b[n % 2][:, :], ALU.mult).then_inc(S("merge_step"), 1)
                        dve.wait_ge(S("merge_step"), 4 * (i - 1) + 2 * hf + t + 1)
                        dve.tensor_tensor(g0, g0, g, ALU.add).then_inc(S("bank_free"), 1)
                if kind0 == "out1":
                    _, hf, t = it
                    n = USE[it]
                    o = x[:, t, hf * CH:hf * CH + CH]
                    dve.wait_ge(S("bank_full"), n + 1)
                    dve.tensor_tensor(o, o, proj_b[n % 2][:, :], ALU.add).then_inc(S("bank_free"), 1)
                if kind0 == "out2":
                    _, hf, t = it
                    n = USE[it]
                    o = x[:, t, hf * CH:hf * CH + CH]
                    tmp = qn[:, n % 2, :]
                    dve.wait_ge(S("bank_full"), n + 1)
                    dve.tensor_tensor(tmp, proj_b[n % 2][:, :], gate_bc[:, 0, hf * CH:hf * CH + CH], ALU.mult)\
                       .then_inc(S("mix_step"), 1)
                    dve.wait_ge(S("mix_step"), 2 * hf + t + 1)
                    dve.tensor_tensor(o, o, tmp, ALU.add).then_inc(S("bank_free"), 1)
                if kind0 == "ada":
                    c = it[1]
                    j = JOB["w_ada", c]
                    o = ada_acc[:, c % 2, :]
                    w = view(j, "k8")
                    job_ready(dve, j)
                    if c >= 2:
                        dve.wait_ge(S("turned"), TURN["ada_out", c - 2] + 1)
                    if c == 0:
                        dve.wait_ge(S("c_step"), 3)
                    dve.tensor_scalar(o, w[:, 0], c_col[:, 1, 0:1], None, ALU.mult).then_inc(S("ada_step"), 1)
                    for k in range(1, KT):
                        dve.wait_ge(S("ada_step"), (KT - 1) * c + k)
                        dve.scalar_tensor_tensor(out=o, in0=w[:, k], scalar=c_col[:, 1, k:k + 1], in1=o,
                                                 op0=ALU.mult, op1=ALU.add)\
                           .then_inc(S("ada_step" if k < KT - 1 else "ada_summed"), 1)
                if kind0 == "ada_out":
                    c = it[1]
                    s, hf = c // 2, c % 2
                    k = TURN[it]
                    dve.wait_ge(S("turned"), k + 1)
                    dve.wait_ge(S("small_loaded"), 16 * N_SMALL)
                    if s in (2, 5):
                        o = gate_bc[:, s // 3, hf * CH:(hf + 1) * CH]
                        dve.tensor_tensor(o, o, turn_b[:, :], ALU.add).then_inc(S("turn_free"), 1)
                    else:
                        m = {0: 0, 1: 1, 3: 2, 4: 3}[s]
                        rows = slice(HD * hf, HD * hf + HD)
                        dve.scalar_tensor_tensor(out=mod[rows, m, :], in0=turn_b[rows, 0:KT], scalar=float(s in (1, 4)),
                                                 in1=b_ada[rows, s, :], op0=ALU.add, op1=ALU.add)\
                           .then_inc(S("turn_free"), 1)
                if kind0 == "score":
                    n = it[1]
                    i = HEADS.index(n)
                    ng = len(units_of(n)) if n < 24 else 1
                    sink = 1 if 16 <= n < 24 else 0
                    buf = L[:, i % 2]
                    for g in range(ng):
                        u = UNIT[n, g]
                        if i >= 2 and g == 0:
                            dve.wait_ge(S("flipped"), UNIT[HEADS[i - 2], 0] + (len(units_of(HEADS[i - 2])) if HEADS[i - 2] < 24 else 1))
                        dve.wait_ge(S("scored"), u + 1)
                        if n < 24:
                            dve.wait_ge(S(f"bias_loaded_{u % BIAS_SLOTS}"), 16 * (u // BIAS_SLOTS + 1))
                            back = bias[:, u % BIAS_SLOTS, ::-1]
                            add = [back[:, P:2 * P], back]
                        else:
                            dve.wait_ge(S("selmask_ready"), 1)
                            add = [selmask[:, 0:P], selmask[:, P:3 * P]]
                        ps = score_b[u % 2]
                        dve.tensor_tensor(buf[:, g, 0:P], ps[:, 0:P], add[0], ALU.add).then_inc(S("logits_half"), 1)
                        dve.tensor_tensor(buf[:, g, P + 1:3 * P + 1], ps[:, P:3 * P], add[1], ALU.add)\
                           .then_inc(S("logits"), 1)
                    if sink:
                        h = n - 16
                        for t in range(NT):
                            at = (P, 3 * P + 1)[t]
                            dve.tensor_copy(buf[:, 0, at:at + 1], sinks[:, h:h + 1]).then_inc(S("sink_set"), 1)
                        dve.wait_ge(S("sink_set"), 2 * h + 2)
                    dve.wait_ge(S("logits"), UNIT[n, ng - 1] + 1)
                    if i >= 2:
                        dve.wait_ge(S("probs"), 2 * i - 2)
                    for t in range(NT):
                        lo, w = (0, P + sink) if t == 0 else (P + 1, 2 * P + sink)
                        dve.tensor_reduce(nmax[:, i % 2, t:t + 1], buf[:, 0:ng, lo:lo + w],
                                          AX.XY, ALU.max, negate=True).then_inc(S("maxed"), 1)
                if kind0 == "value":
                    n = it[1]
                    i = HEADS.index(n)
                    dve.wait_ge(S("probs"), 2 * i + 2)
                    dve.reciprocal(rden[:, i % 2, :], den[:, i % 2, :]).then_inc(S("rden_ready"), 1)
                    dve.wait_ge(S("rden_ready"), i + 1)
                    for t in range(NT):
                        dve.wait_ge(S("value_product"), 2 * i + 2)
                        ps = value_b[:, 128 * (i % 2) + 64 * t:128 * (i % 2) + 64 * t + 64]
                        if n < 24:
                            o = O[:, n // 8, t, HD * (n % 8):HD * (n % 8) + HD]
                            if n % 8 == 0 and t == 0:
                                c = [k for k, ch in enumerate(CHUNKS) if ch[0] == "silu"][n // 8]
                                dve.wait_ge(S("bank_free"), USE["proj", c, 1] + 1)
                            dve.scalar_tensor_tensor(out=o, in0=ps, scalar=rden[:, i % 2, t:t + 1], in1=o,
                                                     op0=ALU.mult, op1=ALU.mult).then_inc(S("valued"), 1)
                        else:
                            o = O2[:, t, HD * (n - 24):HD * (n - 24) + HD]
                            dve.tensor_scalar(o, ps, rden[:, i % 2, t:t + 1], None, ALU.mult).then_inc(S("valued"), 1)
                if kind0 == "rope":
                    step = S("rope_step")
                    k = 0

                    def chain(ins):
                        nonlocal k
                        ins.then_inc(step, 1)
                        k += 1
                        dve.wait_ge(step, k)

                    dve.wait_ge(S("late_loaded"), 16 * N_LATE)
                    chain(dve.tensor_copy(pos[:, :], pos_i[:, :]))
                    for t in range(NT):
                        chain(dve.tensor_scalar(ang[:, t, 1, :], consts[:, C_FREQ:C_FREQ + 8], pos[:, t:t + 1], None,
                                                ALU.mult))
                    chain(dve.tensor_scalar(turns_f[:, :, 1, :], ang[:, :, 1, :], 1.0 / (2 * math.pi), None, ALU.mult))
                    chain(dve.tensor_scalar(turns_f[:, :, 0, :], turns_f[:, :, 1, :], 0.25, None, ALU.add))
                    chain(dve.tensor_copy(turns_i[:, :, :, :], turns_f[:, :, :, :]))
                    chain(dve.tensor_copy(turns_f[:, :, :, :], turns_i[:, :, :, :]))
                    chain(dve.tensor_copy(ang[:, :, 0, :], ang[:, :, 1, :]))
                    c1 = 6.28125
                    c2 = float(np.float32(np.floor((2 * math.pi - c1) * 2 ** 20) / 2 ** 20))
                    c3 = 2 * math.pi - c1 - c2
                    for c in (c1, c2, c3):
                        chain(dve.scalar_tensor_tensor(out=ang[:, :, :, :], in0=turns_f[:, :, :, :], scalar=-c,
                                                       in1=ang[:, :, :, :], op0=ALU.mult, op1=ALU.add))
                    chain(dve.tensor_scalar(ang[:, :, 0, :], ang[:, :, 0, :], math.pi / 2, None, ALU.add))
                    for op, lim, sign in ((ALU.is_gt, math.pi, -1.0), (ALU.is_lt, -math.pi, 1.0)):
                        chain(dve.tensor_scalar(wrap[:, :, :, :], ang[:, :, :, :], lim, sign * 2 * math.pi, op, ALU.mult))
                        chain(dve.tensor_tensor(ang[:, :, :, :], ang[:, :, :, :], wrap[:, :, :, :], ALU.add))
                    dve.tensor_scalar(ang[:, :, :, :], ang[:, :, :, :], 3.1415925, -3.1415925, ALU.min, ALU.max)\
                       .then_inc(S("angles_ready"), 1)
                    dve.wait_ge(S("trig_ready"), 1)
                    dve.wait_ge(S("bank_free"), USE["proj2", 3, 1] + 1)
                    for t in range(NT):
                        lo, hi = R[:, t, 0:25, 0:8], R[:, t, 0:25, 8:16]
                        cos = trig[:, t, 0:1, :].to_broadcast([P, 25, 8])
                        sin = trig[:, t, 1:2, :].to_broadcast([P, 25, 8])
                        for b, (src, f) in enumerate(((lo, cos), (hi, sin), (hi, cos), (lo, sin))):
                            chain(dve.tensor_tensor(rt[:, b], src, f, ALU.mult))
                        chain(dve.tensor_tensor(lo, rt[:, 0], rt[:, 1], ALU.subtract))
                        chain(dve.tensor_tensor(hi, rt[:, 2], rt[:, 3], ALU.add))
                        dve.tensor_copy(R[:, t, 25, :], R[:, t, 24, :]).then_inc(S("rows_ready"), 1)
                if kind0 == "index":
                    h = it[1]
                    dve.wait_ge(S("relu_done"), h + 1)
                    dve.wait_ge(S("wi_ready"), 2)
                    for t, (lo, w) in enumerate(((0, P), (P, 2 * P))):
                        o = score[:, lo:lo + w]
                        r = relu[:, h % 2, lo:lo + w]
                        done = S("index_half" if t == 0 else "index_added")
                        if h == 0:
                            dve.tensor_scalar(o, r, wi[:, t, h:h + 1], None, ALU.mult).then_inc(done, 1)
                        else:
                            dve.wait_ge(done, h)
                            dve.scalar_tensor_tensor(out=o, in0=r, scalar=wi[:, t, h:h + 1], in1=o,
                                                     op0=ALU.mult, op1=ALU.add).then_inc(done, 1)
                if kind0 == "topk":
                    step = S("topk_step")
                    k = 0

                    def chain(ins):
                        nonlocal k
                        ins.then_inc(step, 1)
                        k += 1
                        dve.wait_ge(step, k)

                    caus = [consts[:, C_CAUS + P:C_CAUS + 2 * P], consts[:, C_CAUS:C_CAUS + 2 * P]]
                    dve.wait_ge(S("index_added"), 8)
                    for t, (lo, w) in enumerate(((0, P), (P, 2 * P))):
                        o = score[:, lo:lo + w]
                        chain(dve.scalar_tensor_tensor(out=o, in0=o, scalar=IDX_SCALE, in1=caus[t],
                                                       op0=ALU.mult, op1=ALU.add))
                        for _ in range(TOP_KEYS // 8):
                            chain(dve.max(top8[:, t, :], o))
                            chain(dve.match_replace(out=o, in_to_replace=top8[:, t, :], in_values=o, imm_value=TAKEN))
                        chain(dve.tensor_scalar(o, o, TAKEN / 2, NEG, ALU.is_gt, ALU.mult))
                        last = dve.tensor_tensor(selmask[:, lo:lo + w], o, caus[t], ALU.add)
                        if t == 0:
                            chain(last)
                        else:
                            last.then_inc(S("selmask_ready"), 1)
                if kind0 == "router":
                    step = S("router_step")
                    k = 0

                    def chain(ins):
                        nonlocal k
                        ins.then_inc(step, 1)
                        k += 1
                        dve.wait_ge(step, k)

                    dve.wait_ge(S("router_product"), 1)
                    z = turn_b[:, 0:NT * N_EXP].rearrange("p (t e) -> p t e", t=NT)
                    dve.tensor_scalar(rarg[:, 0], z, 0.0, None, ALU.min).then_inc(S("router_args"), 1)
                    dve.wait_ge(S("router_args"), 1)
                    dve.scalar_tensor_tensor(out=rarg[:, 1], in0=rarg[:, 0], scalar=2.0, in1=z, op0=ALU.mult,
                                             op1=ALU.subtract)\
                       .then_inc(S("router_args"), 1)
                    dve.wait_ge(S("router_exp"), 1)
                    chain(dve.tensor_scalar(rexp[:, 1], rexp[:, 1], 1.0, None, ALU.add))
                    chain(dve.reciprocal(rexp[:, 1], rexp[:, 1]))
                    chain(dve.tensor_tensor(sig[:, :, :], rexp[:, 0], rexp[:, 1], ALU.mult))
                    chain(dve.tensor_tensor(sel[:, :, :], sig[:, :, :],
                                            rbias[:, :].unsqueeze(1).to_broadcast([P, NT, N_EXP]), ALU.add))
                    for t in range(NT):
                        chain(dve.max(top8[:, t, :], sel[:, t, :]))
                        chain(dve.match_replace(out=sel[:, t, :], in_to_replace=top8[:, t, :], in_values=sel[:, t, :],
                                                imm_value=TAKEN))
                    chain(dve.tensor_scalar(sel[:, :, :], sel[:, :, :], TAKEN / 2, None, ALU.is_lt))
                    chain(dve.tensor_tensor(sig[:, :, :], sig[:, :, :], sel[:, :, :], ALU.mult))
                    chain(dve.tensor_reduce(gsum[:, :], sig[:, :, :], AX.X, ALU.add))
                    chain(dve.reciprocal(gsum[:, :], gsum[:, :]))
                    for t in range(NT):
                        ins = dve.tensor_scalar(sig[:, t, :], sig[:, t, :], gsum[:, t:t + 1], ROUTED, ALU.mult, ALU.mult)
                        ins.then_inc(S("gates_ready"), 1)
                    dve.wait_ge(S("gates_turned"), 1)
                    dve.tensor_copy(gT[:, :], bank[6][0:N_EXP, 0:TOK]).then_inc(S("gT_ready"), 1)
                    dve.wait_ge(S("gT_ready"), 1)
                    chain(dve.tensor_reduce(used[:, :], gT[:, :], AX.X, ALU.max))
                    dve.tensor_scalar(used[:, :], used[:, :], 0.0, None, ALU.is_gt).then_inc(S("used_ready"), 1)
                    dve.wait_ge(S("places_counted"), 1)
                    chain(dve.tensor_copy(place[:, :], bank[7][0:N_EXP, 0:1]))
                    dve.wait_ge(S("used_ready"), 1)
                    dve.tensor_scalar(order[:, :], consts[0:N_EXP, C_IOTA:C_IOTA + N_EXP], place[:, 0:1],
                                      used[:, 0:1], ALU.is_equal, ALU.mult).then_inc(S("order_ready"), 1)
                    dve.wait_ge(S("list_product"), 1)
                    dve.tensor_copy(elist[0:1, 1:N_EXP + 1], bank[6][0:1, 0:N_EXP]).then_inc(S("elist_ready"), 1)
                    dve.tensor_copy(elist[0:1, 0:1], bank[6][0:1, N_EXP:N_EXP + 1])\
                       .then_inc(S("elist_ready"), 1)

            for f in range(FT):
                dve.wait_ge(S(f"silu_{f}"), 1)
                dve.tensor_tensor(hT[:, f, :], hs[:, f, :], up_b[f][:, TOK:2 * TOK], ALU.mult).then_inc(S(f"h_ready_{f}"), 1)
            dve.wait_ge(S("elist_ready"), 2)
            n_used = dve.value_load(elist[0:1, 0:1], min_val=0, max_val=N_EXP)
            with dve.Fori(0, -(-N_EXP // ESLOTS)) as m:
                for r in range(ESLOTS):
                    i = m * ESLOTS + r
                    with dve.If(n_used > i):
                        dve.wait_ge(S(f"expert_loaded_{r}"), 16 * ELOADS * (m + 1))
                        for f in range(FT):
                            dve.wait_ge(S(f"silu_{f}"), i + 2)
                            dve.tensor_tensor(hs[:, f, :], hs[:, f, :], gb[:, r, :], ALU.mult).then_inc(S(f"gated_{f}"), 1)
                            dve.wait_ge(S(f"gated_{f}"), i + 1)
                            dve.tensor_tensor(hT[:, f, :], hs[:, f, :], up_b[f][:, TOK:2 * TOK], ALU.mult)\
                               .then_inc(S(f"h_ready_{f}"), 1)
            dve.wait_ge(S("experts_summed"), 1)
            for t in range(NT):
                for hf in range(2):
                    tmp = qn[:, hf, :]
                    o = x[:, t, hf * CH:hf * CH + CH]
                    dve.tensor_tensor(tmp, acc_b[2 * t + hf][:, :], gate_bc[:, 1, hf * CH:hf * CH + CH], ALU.mult)\
                       .then_inc(S("final_step"), 1)
                    dve.wait_ge(S("final_step"), 2 * t + hf + 1)
                    dve.tensor_tensor(o, o, tmp, ALU.add).then_inc(S("out_ready"), 1)

        @block.tensor
        def _(pe):
            def turn_bank(k):
                if k >= 1:
                    pe.wait_ge(S("turn_free"), k)

            def use_bank(n):
                if n >= 2:
                    pe.wait_ge(S("bank_free"), n - 1)
                return proj_b[n % 2]

            for it in SCHEDULE:
                kind0 = it[0]
                if kind0 == "start":
                    pe.wait_ge(S("consts_loaded"), 16)
                    pe.wait_ge(S("ones_set"), 1)
                if kind0 in ("start", "norm"):
                    base = {("start",): 0, ("norm", 0): NT, ("norm", 1): 2 * NT}[it]
                    for t in range(NT):
                        pe.wait_ge(S("x_scaled"), base + t + 1)
                        for q in range(2):
                            turn_bank(TURN[it + (t, q)])
                            for b in range(4):
                                k = 4 * q + b
                                mm = pe.transpose(turn_b[:, b * P:(b + 1) * P], xn[:, k:DM:KT], ident)
                            mm.then_inc(S("turned"), 1)
                if kind0 == "start":
                    pe.wait_ge(S("small_loaded"), 16 * N_SMALL)
                    pe.matmul(bank[6][0:40, 0:NREL_PAD], tabT[:, :], hot, start=True, stop=True)\
                      .then_inc(S("rel_product"), 1)
                if kind0 == "proj":
                    _, c, t = it
                    n = USE[it]
                    kind, _, w, _ = CHUNKS[c]
                    j = JOB["w_in", c]
                    ps = use_bank(n)
                    if n == 0:
                        pe.wait_ge(S("turn_free"), 4)
                    if t == 0:
                        job_ready(pe, j)
                    wv = view(j, "kv" if w == 256 else "k8")
                    for k in range(KT):
                        mm = pe.matmul(ps[:, 0:w], xT[:, k, t * P:(t + 1) * P], wv[:, k, :], start=(k == 0), stop=(k == KT - 1))
                    mm.then_inc(S("bank_full"), 1)
                if kind0 == "proj2":
                    _, c, t = it
                    n = USE[it]
                    kind, _, w, _ = CHUNKS2[c]
                    j = JOB["w_in_2", c]
                    ps = use_bank(n)
                    if c == 0 and t == 0:
                        pe.wait_ge(S("turn_free"), TURN["norm", 0, 1, 1] + 1)
                    if t == 0:
                        job_ready(pe, j)
                    wv = view(j, "kiwi" if w == 72 else "k8")
                    if kind in ("xc", "cg", "bg"):
                        for q in range(2):
                            ct = 2 * t + q
                            for k in range(KT):
                                mm = pe.matmul(ps[:, q * TOK:(q + 1) * TOK], wv[:, k, ct * P:(ct + 1) * P], xT[:, k, :],
                                               start=(k == 0), stop=(k == KT - 1))
                    else:
                        for k in range(KT):
                            mm = pe.matmul(ps[:, 0:w], xT[:, k, t * P:(t + 1) * P], wv[:, k, :], start=(k == 0), stop=(k == KT - 1))
                    mm.then_inc(S("bank_full"), 1)
                if kind0 in ("branch", "out1", "out2"):
                    n = USE[it]
                    ps = use_bank(n)
                    if kind0 == "branch":
                        _, i, hf, t = it
                        j = JOB["w_branch", i]
                        if hf == 0 and t == 0:
                            job_ready(pe, j)
                            pe.wait_ge(S("turn_free"), TURN["turn_branch", i, 1] + 1)
                        wv, lhs, nk, cols = view(j, "k4"), OT, WK, slice(hf * CH, hf * CH + CH)
                    else:
                        _, hf, t = it
                        j = JOB["w_out" if kind0 == "out1" else "w_out_2", hf]
                        if t == 0:
                            job_ready(pe, j)
                        if hf == 0 and t == 0:
                            pe.wait_ge(S("turn_free"), (TURN["turn_merged", 1, 1] if kind0 == "out1"
                                                        else TURN["turn_branch", 3, 1]) + 1)
                            pe.wait_ge(S("bank_free"), n)
                        wv, lhs, nk, cols = view(j, "k8"), (xT if kind0 == "out1" else mixT), KT, slice(0, CH)
                    for k in range(nk):
                        mm = pe.matmul(ps[:, :], lhs[:, k, t * P:(t + 1) * P], wv[:, k, cols], start=(k == 0), stop=(k == nk - 1))
                    mm.then_inc(S("bank_full"), 1)
                if kind0 == "turn":
                    _, c, t = it
                    k = TURN[it]
                    m = NTH_NORM["proj", c, t]
                    pe.wait_ge(S("bank_free"), USE["proj", c, t] + 1)
                    turn_bank(k)
                    nb = 2 if CHUNKS[c][0] == "kv" else 4
                    for b in range(nb):
                        mm = pe.transpose(turn_b[:, b * P:(b + 1) * P], qn[:, m % 2, b * P:(b + 1) * P], ident)
                    mm.then_inc(S("turned"), 1)
                if kind0 == "turn_branch":
                    i = it[1]
                    pe.wait_ge(S("valued"), 2 * (8 * i + 8))
                    for t in range(NT):
                        turn_bank(TURN[it + (t,)])
                        for b in range(4):
                            src = O[:, i, t, b * P:(b + 1) * P] if i < 3 else O2[:, t, b * P:(b + 1) * P]
                            mm = pe.transpose(turn_b[:, b * P:(b + 1) * P], src, ident)
                        mm.then_inc(S("turned"), 1)
                if kind0 == "turn_merged":
                    pe.wait_ge(S("bank_free"), USE["branch", 2, 1, 1] + 1)
                    for t in range(NT):
                        for q in range(2):
                            turn_bank(TURN[it + (t, q)])
                            for b in range(4):
                                k = 4 * q + b
                                mm = pe.transpose(turn_b[:, b * P:(b + 1) * P], G[:, t, k * P:(k + 1) * P], ident)
                            mm.then_inc(S("turned"), 1)
                if kind0 == "turn2":
                    pe.wait_ge(S("rows_ready"), NT)
                    for g in range(4):
                        for t in range(NT):
                            turn_bank(TURN[it + (g, t)])
                            for b in range(4 if g < 3 else 1):
                                r0 = 8 * g + 2 * b
                                mm = pe.transpose(turn_b[:, b * P:(b + 1) * P],
                                                  R[:, t, r0:r0 + 2, :].rearrange("p h d -> p (h d)"), ident)
                            mm.then_inc(S("turned"), 1)
                if kind0 == "ada_out":
                    c = it[1]
                    s, hf = c // 2, c % 2
                    pe.wait_ge(S("ada_summed"), c + 1)
                    turn_bank(TURN[it])
                    acc = ada_acc[:, c % 2, :]
                    if s in (2, 5):
                        mm = pe.matmul(turn_b[:, :], ones[:, :], acc, start=True, stop=True)
                    else:
                        for k in range(KT):
                            mm = pe.matmul(turn_b[HD * hf:HD * hf + HD, k:k + 1], acc[:, k:CH:KT], ones[:, 0:1],
                                           start=True, stop=True)
                    mm.then_inc(S("turned"), 1)
                if kind0 == "score":
                    n = it[1]
                    for g in range(len(units_of(n)) if n < 24 else 1):
                        u = UNIT[n, g]
                        if u >= 2:
                            pe.wait_ge(S("logits"), u - 1)
                        if n < 24:
                            qp, kp, half, _, _ = units_of(n)[g]
                            q, kk = qT[HD * half:HD * half + HD, qp, :], kT[HD * half:HD * half + HD, kp, :]
                            if n % 8 == 0 and g == 0:
                                c = {0: 1, 1: 9, 2: 15}[n // 8]
                                pe.wait_ge(S("turn_free"), TURN["turn", c, 1] + 1)
                        else:
                            h = n - 24
                            half = h % 2
                            q, kk = T2[HD * half:HD * half + HD, h // 2, :], T2[HD * half:HD * half + HD, 4 + h // 2, :]
                            if h == 0:
                                pe.wait_ge(S("relu_done"), 8)
                        ps = score_b[u % 2]
                        pe.matmul(ps[:, 0:P], q[:, 0:P], kk[:, 0:P], start=True, stop=True)
                        pe.matmul(ps[:, P:3 * P], q[:, P:2 * P], kk, start=True, stop=True).then_inc(S("scored"), 1)
                if kind0 == "index":
                    h = it[1]
                    half = h % 2
                    if h == 0:
                        pe.wait_ge(S("turn_free"), TURN["turn2", 3, 1] + 1)
                        pe.wait_ge(S("logits"), N_BIAS)
                    if h >= 2:
                        pe.wait_ge(S("relu_done"), h - 1)
                    q, kk = T2[HD * half:HD * half + HD, 8 + h // 2, :], T2[HD * half:HD * half + HD, 12, :]
                    ps = score_b[h % 2]
                    pe.matmul(ps[:, 0:P], q[:, 0:P], kk[:, 0:P], start=True, stop=True)
                    pe.matmul(ps[:, P:3 * P], q[:, P:2 * P], kk, start=True, stop=True).then_inc(S("index_product"), 1)
                if kind0 == "flip":
                    n = it[1]
                    i = HEADS.index(n)
                    for g in range(len(units_of(n)) if n < 24 else 1):
                        u = UNIT[n, g]
                        pe.wait_ge(S("probs"), 2 * i + 2)
                        if u >= 2:
                            pe.wait_ge(S("probsT"), u - 1)
                        for b, lo in enumerate((0, P + 1, 2 * P + 1)):
                            mm = pe.transpose(flip_b[u % 2][:, b * P:(b + 1) * P], L[:, i % 2, g, lo:lo + P], ident)
                        mm.then_inc(S("flipped"), 1)
                if kind0 == "value":
                    n = it[1]
                    i = HEADS.index(n)
                    ng = len(units_of(n)) if n < 24 else 1
                    pe.wait_ge(S("probsT"), UNIT[n, ng - 1] + 1)
                    if n in (0, 8, 16):
                        c = {0: 2, 8: 12, 16: 15}[n]
                        pe.wait_ge(S("bank_free"), USE["proj", c, 1] + 1)
                    if n == 0:
                        pe.wait_ge(S("rel_ready"), 1)
                    if n == 24:
                        pe.wait_ge(S("bank_free"), USE["proj2", 4, 1] + 1)
                    if i >= 1:
                        pe.wait_ge(S("valued"), 2 * i)
                    for t in range(NT):
                        o = value_b[:, 128 * (i % 2) + 64 * t:128 * (i % 2) + 64 * t + 64]
                        parts = [(g, kb) for g in range(ng) for kb in range(t + 1)]
                        for z, (g, kb) in enumerate(parts):
                            v = V[:, kb, units_of(n)[g][3]:units_of(n)[g][3] + HD] if n < 24 \
                                else V2[:, kb, HD * (n - 24):HD * (n - 24) + HD]
                            lo = 0 if t == 0 else P + P * kb
                            mm = pe.matmul(o, PT[:, i % 2, g, lo:lo + P], v, start=(z == 0), stop=(z == len(parts) - 1))
                        mm.then_inc(S("value_product"), 1)
                if kind0 == "router":
                    pe.wait_ge(S("turn_free"), TURN["norm", 1, 1, 1] + 1)
                    pe.wait_ge(S("late_loaded"), 16 * N_LATE)
                    for t in range(NT):
                        for k in range(KT):
                            mm = pe.matmul(turn_b[:, N_EXP * t:N_EXP * t + N_EXP], xT[:, k, t * P:(t + 1) * P], w_router[:, k, :],
                                           start=(k == 0), stop=(k == KT - 1))
                    mm.then_inc(S("router_product"), 1)

            def up(w1, w3, f):
                for m, w in enumerate((w1, w3)):
                    for k in range(KT):
                        mm = pe.matmul(up_b[f][:, m * TOK:(m + 1) * TOK], w[:, k, f:ED:FT], xT[:, k, :],
                                       start=(k == 0), stop=(k == KT - 1))
                mm.then_inc(S(f"up_{f}"), 1)

            def down(w2, f, first_of_all):
                for t in range(NT):
                    for hf in range(2):
                        mm = pe.matmul(acc_b[2 * t + hf][:, :], hT[:, f, t * P:(t + 1) * P], w2[:, f, hf * CH:hf * CH + CH],
                                       start=first_of_all, stop=False, skip_group_check=True)
                return mm

            j = JOB["shared_up",]
            job_ready(pe, j)
            pe.wait_ge(S("probsT"), len(UNITS))
            wv = view(j, "up")
            for f in range(FT):
                up(wv[:, 0], wv[:, 1], f)
            pe.wait_ge(S("bank_free"), len(BANKED))
            pe.wait_ge(S("logits"), len(UNITS))
            pe.wait_ge(S("gates_ready"), NT)
            pe.wait_ge(S("valued"), 64)
            for t in range(NT):
                mm = pe.transpose(bank[6][0:N_EXP, t * P:(t + 1) * P], sig[:, t, :], ident)
            mm.then_inc(S("gates_turned"), 1)
            pe.wait_ge(S("used_ready"), 1)
            pe.wait_ge(S("router_exp"), 1)
            pe.matmul(bank[7][0:N_EXP, 0:1], consts[0:N_EXP, C_TRI:C_TRI + N_EXP], used[:, :], start=True, stop=True)\
              .then_inc(S("places_counted"), 1)
            pe.wait_ge(S("order_ready"), 1)
            pe.matmul(bank[6][0:1, 0:N_EXP], consts[0:N_EXP, C_COL:C_COL + 1], order[:, :], start=True, stop=True)
            pe.matmul(bank[6][0:1, N_EXP:N_EXP + 1], used[:, :], ones[0:N_EXP, 0:1], start=True, stop=True)\
              .then_inc(S("list_product"), 1)
            j = JOB["shared_down",]
            job_ready(pe, j)
            for f in range(FT):
                pe.wait_ge(S(f"h_ready_{f}"), 1)
                mm = down(view(j, "down"), f, f == 0)
            mm.then_inc(S("shared_done"), 1)

            pe.wait_ge(S("elist_ready"), 2)
            n_used = pe.value_load(elist[0:1, 0:1], min_val=0, max_val=N_EXP)
            with pe.Fori(0, -(-N_EXP // ESLOTS)) as m:
                for r in range(ESLOTS):
                    i = m * ESLOTS + r
                    with pe.If(n_used > i):
                        pe.wait_ge(S(f"expert_loaded_{r}"), 16 * ELOADS * (m + 1))
                        w1 = ew[r][:, 0:2048].rearrange("p (k n) -> p k n", k=KT)
                        w3 = ew[r][:, 2048:4096].rearrange("p (k n) -> p k n", k=KT)
                        w2 = ew[r][:, 4096:6144].rearrange("p (f n) -> p f n", f=FT)
                        for f in range(FT):
                            up(w1, w3, f)
                        for f in range(FT):
                            pe.wait_ge(S(f"h_ready_{f}"), i + 2)
                            mm = down(w2, f, False)
                        mm.then_inc(S("expert_done"), 1)
            pe.matmul(bank[6][0:1, 0:1], ones[:, 0:1], ones[:, 0:1], start=True, stop=True).then_inc(S("experts_summed"), 1)


def rel_bucket(dist):
    dist = np.maximum(dist, 0)
    ratio = (np.log(np.maximum(dist, 1).astype(np.float32) / np.float32(16)) / np.float32(math.log(2048 / 16)))
    large = np.minimum(16 + (ratio * np.float32(16)).astype(np.int32), 31)
    return np.where(dist < 16, dist, large)


def shape_constants():
    sq = np.zeros((P, C_N), np.float32)
    p = np.arange(P)[:, None]
    sq[:, C_ID:C_ID + P] = np.eye(P)
    sq[:, C_CAUS:C_CAUS + 2 * P] = np.where(P + p - np.arange(2 * P)[None, :] >= 0, 0.0, NEG)
    sq[:, C_FREQ:C_FREQ + 8] = (np.float32(500000.0) ** (-np.arange(8, dtype=np.float32) / np.float32(8)))[None, :]
    sq[:N_EXP, C_TRI:C_TRI + N_EXP] = np.arange(N_EXP)[:, None] < np.arange(N_EXP)[None, :]
    sq[:, C_IOTA:C_IOTA + N_EXP] = np.arange(N_EXP)[None, :]
    sq[:, C_COL] = np.arange(P)
    dist = np.arange(NREL_PAD) - 127
    hot = (np.arange(32)[:, None] == rel_bucket(dist)[None, :]).astype(np.float32)
    mask = np.zeros((40, NREL_PAD), np.float32)
    for row in range(40):
        ok = dist >= 0
        if 8 <= row < 32:
            w, d = ((128, 1), (512, 4), (2048, 16))[(row - 8) // 8]
            ok = ok & (dist <= w) & (dist % d == 0)
        if row >= 32:
            ok = ok & (dist < 128)
        mask[row] = np.where(ok, 0.0, NEG)
    return {"c_square": sq, "c_hot": hot, "c_mask": mask}


_INS = ["x", "ln_g", "w_in", "qk_g", "sinks", "w_branch", "w_out", "rel_bias", "c_2", "positions_2", "norm1_g_2",
        "norm2_g_2", "w_ada_2", "b_ada_2", "w_in_2", "conv_w_2", "q_norm_g_2", "k_norm_g_2", "kidx_norm_g_2",
        "w_out_2", "w_router_2", "router_bias_2", "w1_2", "w3_2", "w2_2", "ws1_2", "ws3_2", "ws2_2"]


def kernel(**inputs):
    import concourse.bacc as _bacc
    from concourse.bass_utils import run_bass_kernel_spmd as _run

    nc = _bacc.Bacc("TRN2", target_bir_lowering=False, num_devices=1)
    arrays, args = {}, {}
    given = {name: inputs[name] for name in _INS}
    given.update(shape_constants())
    for name, value in given.items():
        v = np.ascontiguousarray(value)
        arrays[f"in_{name}_dram"] = v
        args[name] = nc.dram_tensor(f"in_{name}_dram", v.shape, mybir.dt.from_np(v.dtype), kind="ExternalInput").ap()
    out = nc.dram_tensor("out_0_dram", (1, TOK, DM), F32, kind="ExternalOutput").ap()
    build(nc, args, out)
    r = _run(nc, [arrays], core_ids=[0])
    return r.results[0]["out_0_dram"]
```

```python
import math

import numpy as np
import concourse.bass as bass
from concourse import mybir
from contextlib import ExitStack

F32 = mybir.dt.float32
F32R = mybir.dt.float32r
I32 = mybir.dt.int32
ALU = mybir.AluOpType
ACT = mybir.ActivationFunctionType
AX = mybir.AxisListType

P = 128
TOK = 256
NT = TOK // P
DM = 1024
KT = DM // P
HD = 64
W_BR = 512
WK = W_BR // P
EPS = 1e-6
NEG = -1e30
TAKEN = -3e38
N_EXP = 64
ED = 256
FT = ED // P
TOP_KEYS = 64
SCALE = HD ** -0.5
IDX_SCALE = (64 ** -0.5) * (8 ** -0.5)
ROUTED = 2.5
NREL = 383
NREL_PAD = 384
CH = 512
N_ADA = 6 * DM // CH

C_ID, C_CAUS, C_FREQ, C_TRI, C_IOTA, C_THR_ROW = 0, 128, 384, 392, 520, 648
C_COL, C_EXP, C_THR, C_N = 776, 777, 778, 779
FAR = 1000.0

CHUNKS = (
    [("q", 0, 512, 0), ("k", 512, 512, 0), ("v", 1024, 512, 0), ("silu", 1536, 512, 0)]
    + [("q", 2048 + 512 * g, 512, 4 + 4 * g) for g in range(3)]
    + [("k", 3584 + 512 * g, 512, 4 + 4 * g) for g in range(3)]
    + [("v", 5120 + 512 * g, 512, 512 + 512 * g) for g in range(3)]
    + [("silu", 6656, 512, 1)]
    + [("q", 7168, 512, 16), ("kv", 7680, 256, 16), ("silu", 7936, 512, 2)]
    + [("gate", 8448 + 512 * g, 512, 512 * g) for g in range(6)]
)
CHUNKS2 = [("qi", 3072, 512, 16), ("kiwi", 3584, 72, 24), ("q2", 1536, 512, 0), ("k2", 2048, 512, 8),
           ("v2", 2560, 512, 0), ("xc", 0, 512, 0), ("cg", 1024, 512, 0), ("bg", 512, 512, 0)]
N_QP, N_KP = 20, 18
V_COLS = 512 + 1536 + 128


def units_of(n):
    b, h = n // 8, n % 8
    if b == 0:
        return [(h // 2, h // 2, h % 2, 64 * h, h)]
    if b == 1:
        return [(4 + 4 * g + h // 2, 4 + 4 * g + h // 2, h % 2, 512 + 512 * g + 64 * h, 8 + 8 * g + h)
                for g in range(3)]
    return [(16 + h // 2, 16 + h // 4, h % 2, 2048 + 64 * (h // 4), 32 + h)]


FILL = [3] * 4 + [2] * 8 + [1] * 12


def make_schedule():
    s = [("start",)]
    fill = []
    late = {}

    def project(c):
        for t in range(NT):
            fill.append(("proj", c, t))
            if CHUNKS[c][0] in ("q", "k", "kv"):
                late[len(fill) - 1] = ("turn", c, t)

    for c in range(len(CHUNKS)):
        project(c)
    seq = []
    pending = None
    for i, item in enumerate(fill):
        seq.append([item] + ([pending] if pending else []))
        pending = late.get(i)
    if pending:
        seq.append([pending])
    at = 0

    def take(k):
        nonlocal at
        for _ in range(k):
            if at < len(seq):
                s.extend(seq[at])
                at += 1

    take(9)
    ada = [("ada", c, part) for c in range(N_ADA) for part in range(KT // 2)]

    def modulation(k):
        for _ in range(k):
            if ada:
                _, c, part = ada.pop(0)
                s.append(("ada", c, part))
                if part == 0 and c:
                    s.append(("ada_out", c - 1))
                if not ada:
                    s.append(("ada_out", c))

    def head(n, k, m=0):
        s.append(("score", n))
        take(1 if k > 0 else 0)
        modulation(m - m // 2)
        if n >= 1:
            s.append(("flip", n - 1))
        take(1 if k > 1 else 0)
        modulation(m // 2)
        if n >= 1:
            s.append(("value", n - 1))
        take(k - 2)

    for n in range(8):
        head(n, FILL[n], 3 if n >= 2 else 0)
    for n in range(8, 16):
        head(n, FILL[n], 4 if n < 15 else 3)
        if n == 10:
            s.append(("turn_branch", 0))
    assert not ada
    for n in range(16, 24):
        head(n, FILL[n])
        if n == 18:
            s.append(("turn_branch", 1))
        if n == 17:
            s.extend(("branch", 0, hf, t) for hf in range(2) for t in range(NT))
        if n == 20:
            s.extend(("branch", 1, hf, t) for hf in range(2) for t in range(NT))
    take(99)
    s += [("flip", 23), ("value", 23), ("turn_branch", 2)]
    s.extend(("branch", 2, hf, t) for hf in range(2) for t in range(NT))
    s.append(("turn_merged",))
    s.extend(("out1", hf, t) for hf in range(2) for t in range(NT))
    s.append(("norm", 0))
    for c in range(5):
        s.extend(("proj2", c, t) for t in range(NT))
    s.append(("rope",))
    s.append(("turn2",))
    s.extend(("index", h) for h in range(8))
    s.append(("topk",))
    for c in range(5, 8):
        s.extend(("proj2", c, t) for t in range(NT))
    for h in range(8):
        s.append(("score", 24 + h))
        if h:
            s += [("flip", 23 + h), ("value", 23 + h)]
    s += [("flip", 31), ("value", 31), ("turn_branch", 3)]
    s.extend(("out2", hf, t) for hf in range(2) for t in range(NT))
    s.append(("norm", 1))
    s.append(("router",))
    return s


SCHEDULE = make_schedule()

RING = 3
WEIGHTS_OF = {"proj": "w_in", "ada": "w_ada", "branch": "w_branch", "out1": "w_out", "proj2": "w_in_2", "out2": "w_out_2"}
JOBS, JOB = [], {}
LAST_STEP = {}
for _it in SCHEDULE:
    if _it[0] in WEIGHTS_OF:
        _key = (WEIGHTS_OF[_it[0]], _it[1])
        if _key not in JOB:
            JOB[_key] = len(JOBS)
            JOBS.append(_key)
        LAST_STEP[JOB[_key]] = _it
for _key in (("shared_up",), ("shared_down",)):
    JOB[_key] = len(JOBS)
    JOBS.append(_key)

BANKED = [it for it in SCHEDULE if it[0] in ("proj", "branch", "out1", "proj2", "out2")]
USE = {it: n for n, it in enumerate(BANKED)}
HEADS = [it[1] for it in SCHEDULE if it[0] == "score"]
UNITS = [(n, g) for n in HEADS for g in range(len(units_of(n)) if n < 24 else 1)]
UNIT = {ng: u for u, ng in enumerate(UNITS)}
N_BIAS = sum(n < 24 for n, _ in UNITS)
BIAS_SLOTS = 5
TURNS = []
for _it in SCHEDULE:
    if _it[0] == "turn":
        TURNS.append(_it)
    if _it[0] == "turn_branch":
        TURNS += [_it + (t,) for t in range(NT)]
    if _it[0] in ("turn_merged", "norm", "start"):
        TURNS += [_it + (t, q) for t in range(NT) for q in range(2)]
    if _it[0] == "ada_out":
        TURNS.append(_it)
    if _it[0] == "turn2":
        TURNS += [_it + (g, t) for g in range(4) for t in range(NT)]
TURN = {it: n for n, it in enumerate(TURNS)}
NORMED = [it for it in BANKED if (it[0] == "proj" and CHUNKS[it[1]][0] in ("q", "k", "kv"))
          or (it[0] == "proj2" and CHUNKS2[it[1]][0] in ("q2", "k2", "kiwi"))]
NTH_NORM = {it: n for n, it in enumerate(NORMED)}
GATED = [it for it in BANKED if it[0] == "proj" and CHUNKS[it[1]][0] == "silu"]
NTH_GATE = {it: n for n, it in enumerate(GATED)}
ESLOTS = 3
N_SMALL = 15
N_LATE = 6
NV = 2 * N_EXP
MAX_WORK = N_EXP + TOK * 8 // (P + 1)


def build(nc, a, out):
    ctx = ExitStack()
    with ctx:
        def sb(name, shape, dt=F32, stack=ctx):
            return stack.enter_context(nc.sbuf_tensor(name, shape, dt))

        sems = {}

        def S(name):
            if name not in sems:
                sems[name] = ctx.enter_context(nc.semaphore(name))
            return sems[name]

        ctx.enter_context(nc.allow_non_contiguous_dma(reason="small vectors onto partitions"))
        rel_dram = nc.dram_tensor("rel_rows", (40, NREL_PAD), F32, kind="Internal").ap()
        place_rows = nc.dram_tensor("place_rows", (NV, TOK), F32, kind="Internal").ap()
        place_cols = nc.dram_tensor("place_cols", (P, NV, 2 * NT), F32, kind="Internal").ap()

        ring = sb("ring", [P, RING, 4096])
        consts = sb("consts", [P, C_N])
        ident = consts[:, C_ID:C_ID + P]
        ones = sb("ones", [P, P])
        x = sb("x", [P, NT, DM])
        xT = sb("xT", [P, KT, TOK])
        ln_g = sb("ln_g_cols", [P, 3, KT])
        qk_g = sb("qk_g_cols", [P, 6])
        q_scale = sb("q_scale", [P, 3])
        g2 = sb("g2", [P, 3, HD])
        half_neg = sb("half_neg", [P, 8])
        c_col = sb("c_col", [P, 3, KT])
        b_ada = sb("b_ada_cols", [P, 6, KT])
        gate_bc = sb("gate_bc", [P, 2, DM])
        mod = sb("mod_cols", [P, 4, KT])
        ada_acc = sb("ada_acc", [P, 2, CH])
        sq = sb("squares", [P, CH])
        msum = sb("mean_squares", [P, 8])
        rstd = sb("rstd", [P, 8])
        xsum = sb("x_squares", [P, 1])
        L = sb("logits", [P, 2, 3, 386])
        PT = sb("probsT", [P, 2, 3, 384])
        nmax = sb("neg_max", [P, 2, 2])
        den = sb("den", [P, 2, 2])
        rden = sb("rden", [P, 2, 2])
        xn = PT[:, :, :, :].rearrange("p a g n -> p (a g n)")[:, 0:DM]
        spare = L[:, :, :, :].rearrange("p a g n -> p (a g n)")
        hot, relmask, relrow = spare[0:32, 0:384], spare[0:40, 384:768], spare[0:40, 768:1152]
        qn = sb("qn", [P, 2, CH])

        first = ExitStack()
        tabT = sb("tabT", [32, 40], F32, first)
        bias = sb("bias", [P, BIAS_SLOTS, 256], F32, first)
        qT = sb("qT", [P, N_QP, TOK], F32, first)
        kT = sb("kT", [P, N_KP, TOK], F32, first)
        V = sb("V", [P, NT, V_COLS], F32, first)
        O = sb("O", [P, 3, NT, W_BR], F32, first)
        OT = sb("OT", [P, WK, TOK], F32, first)
        G = sb("G", [P, NT, 3 * DM], F32, first)
        egate = sb("egate", [P, CH], F32, first)
        sinks = sb("sinks", [P, 8], F32, first)
        first.close()

        second = ExitStack()
        w_router = sb("w_router", [P, KT, N_EXP], F32, second)
        rbias = sb("router_bias", [P, N_EXP], F32, second)
        rarg = sb("rarg", [P, 2, NT, N_EXP], F32, second)
        rexp = sb("rexp", [P, 2, NT, N_EXP], F32, second)
        sig = sb("sig", [P, NT, N_EXP], F32, second)
        sel = sb("sel", [P, NT, N_EXP], F32, second)
        taken = sb("taken", [P, NT, NV], F32, second)
        ranks = sb("ranks", [P, NT, NV], F32, second)
        pcol = sb("pcol", [P, NV, 2 * NT], F32, second)
        prow = sb("prow", [NV, TOK], F32, second)
        gsum = sb("gsum", [P, NT], F32, second)
        used = sb("used", [NV, 1], F32, second)
        place = sb("place", [NV, 1], F32, second)
        order = sb("order", [NV, NV], F32, second)
        top8 = sb("top8", [P, 2, 8], F32, second)
        work = sb("work", [1, 1 + 2 * NV], I32, second)

        mixer = ExitStack()
        pos_i = sb("pos_i", [P, NT], I32, mixer)
        conv_w = sb("conv_w_cols", [P, 3, WK], F32, mixer)
        pos = sb("pos", [P, NT], F32, mixer)
        ang = sb("ang", [P, NT, 2, 8], F32, mixer)
        turns_f = sb("turns_f", [P, NT, 2, 8], F32, mixer)
        turns_i = sb("turns_i", [P, NT, 2, 8], I32, mixer)
        wrap = sb("wrap", [P, NT, 2, 8], F32, mixer)
        trig = sb("trig", [P, NT, 2, 8], F32, mixer)
        R = sb("rows2", [P, NT, 26, HD], F32, mixer)
        rt = sb("rope_tmp", [P, 4, 25, 8], F32, mixer)
        wi = sb("wi", [P, NT, 8], F32, mixer)
        V2 = sb("V2", [P, NT, CH], F32, mixer)
        T2 = sb("T2", [P, 13, TOK], F32, mixer)
        relu = sb("relu", [P, 2, 384], F32, mixer)
        score = sb("score", [P, 384], F32, mixer)
        selmask = sb("selmask", [P, 384], F32, mixer)
        xcT = sb("xcT", [P, WK, TOK], F32, mixer)
        uT = sb("uT", [P, WK, TOK + 2], F32, mixer)
        cv = sb("cv", [P, TOK], F32, mixer)
        O2 = sb("O2", [P, NT, W_BR], F32, mixer)
        mixT = sb("mixT", [P, KT, TOK], F32, mixer)
        mixer.close()

        moe = ExitStack()
        hs = sb("hs", [P, FT, TOK], F32, moe)
        hT = sb("hT", [P, FT, TOK], F32, moe)
        x_hi = sb("x_hi", [P, NT, KT, P], F32R, moe)
        x_lo = sb("x_lo", [P, NT, KT, P], F32R, moe)
        xe = sb("x_block", [P, KT, P], F32, moe)
        col3 = sb("block_cols", [P, ESLOTS, 2 * NT], F32, moe)
        row3 = sb("block_rows", [P, ESLOTS, TOK], F32, moe)
        pick = sb("pick", [P, ESLOTS, NT, P], F32R, moe)
        put = sb("put", [P, ESLOTS, TOK], F32R, moe)
        gcol = sb("block_gates", [P, 1], F32, moe)
        y_hi = sb("y_hi", [P, DM], F32R, moe)
        y_lo = sb("y_lo", [P, DM], F32R, moe)
        own = sb("expert_w", [P, 6144], F32, moe)
        moe.close()
        second.close()
        flat = ring[:, :, :].rearrange("p r n -> p (r n)")
        ew = [own[:, :], flat[:, 0:6144], flat[:, 6144:12288]]

        bank = [ctx.enter_context(nc.psum_tensor(f"bank{i}", [P, 512], F32)) for i in range(8)]
        proj_b, score_b, flip_b, value_b, turn_b = bank[0:2], bank[2:4], bank[4:6], bank[6], bank[7]
        acc_b, up_b, y_b = bank[0:4], bank[4:6], bank[6:8]

        block = ctx.enter_context(nc.Block())

        def view(j, kind):
            slot = ring[:, j % RING, :]
            if kind == "k8":
                return slot.rearrange("p (k n) -> p k n", k=KT)
            if kind == "k4":
                return slot.rearrange("p (k n) -> p k n", k=WK)
            if kind == "kiwi":
                return slot[:, 0:KT * 72].rearrange("p (k n) -> p k n", k=KT)
            if kind == "kv":
                return slot[:, 0:KT * 256].rearrange("p (k n) -> p k n", k=KT)
            if kind == "up":
                return slot.rearrange("p (m k n) -> p m k n", m=2, k=KT)
            return slot[:, 0:FT * DM].rearrange("p (f n) -> p f n", f=FT)

        def bank_taken(eng, n):
            eng.wait_ge(S(f"bank_free_{n % 2}"), n // 2 + 1)

        def job_ready(eng, j):
            eng.wait_ge(S(f"ring_loaded_{j % RING}"), 16 * (2 if JOBS[j][0] == "shared_up" else 1)
                        + 16 * sum(1 for i in range(j % RING, j, RING)))

        @block.sync
        def _(sp):
            d_rows = "(p k) n -> p k n"

            def load(j):
                kind, arg = JOBS[j][0], JOBS[j][1:]
                done = S(f"ring_loaded_{j % RING}")
                if j >= RING:
                    last = LAST_STEP[j - RING]
                    if last[0] == "ada":
                        sp.wait_ge(S("ada_summed"), last[1] + 1)
                    else:
                        sp.wait_ge(S("bank_full"), USE[last] + 1)
                if kind == "w_in":
                    _, c0, w, _ = CHUNKS[arg[0]]
                    src = a["w_in"][0].rearrange(d_rows, k=KT)[:, :, c0:c0 + w]
                    sp.dma_start(view(j, "kv" if w == 256 else "k8"), src).then_inc(done, 16)
                elif kind == "w_in_2":
                    _, c0, w, _ = CHUNKS2[arg[0]]
                    src = a["w_in_2"][0].rearrange(d_rows, k=KT)[:, :, c0:c0 + w]
                    sp.dma_start(view(j, "kiwi" if w == 72 else "k8"), src).then_inc(done, 16)
                elif kind == "w_ada":
                    src = a["w_ada_2"][0].rearrange(d_rows, k=KT)[:, :, CH * arg[0]:CH * arg[0] + CH]
                    sp.dma_start(view(j, "k8"), src).then_inc(done, 16)
                elif kind == "w_branch":
                    src = a["w_branch"][0, arg[0]].rearrange("(k p) n -> p k n", p=P)
                    sp.dma_start(view(j, "k4"), src).then_inc(done, 16)
                elif kind == "w_out":
                    src = a["w_out"][0].rearrange("(k p) n -> p k n", p=P)[:, :, CH * arg[0]:CH * arg[0] + CH]
                    sp.dma_start(view(j, "k8"), src).then_inc(done, 16)
                elif kind == "w_out_2":
                    src = a["w_out_2"][0].rearrange("(k p) n -> p k n", p=P)[:, :, CH * arg[0]:CH * arg[0] + CH]
                    sp.dma_start(view(j, "k8"), src).then_inc(done, 16)
                elif kind == "shared_up":
                    for m, name in enumerate(("ws1_2", "ws3_2")):
                        sp.dma_start(view(j, "up")[:, m], a[name][0].rearrange(d_rows, k=KT)).then_inc(done, 16)
                else:
                    sp.dma_start(view(j, "down"), a["ws2_2"][0].rearrange("(p f) n -> p f n", f=FT))\
                      .then_inc(done, 16)

            at = 0
            for it in SCHEDULE:
                if it[0] == "start":
                    for t in range(NT):
                        sp.dma_start(x[:, t, :], a["x"][0, t * P:(t + 1) * P, :]).then_inc(S(f"x_loaded_{t}"), 16)
                if it[0] == "score" and it[1] < 24:
                    for g, (_, _, _, _, row) in enumerate(units_of(it[1])):
                        u = UNIT[it[1], g]
                        if u == 0:
                            sp.wait_ge(S("rel_ready"), 1)
                            sp.dma_start(rel_dram, relrow).then_inc(S("rel_stored"), 16)
                            sp.wait_ge(S("rel_stored"), 16)
                        if u >= BIAS_SLOTS:
                            sp.wait_ge(S("logits"), u - BIAS_SLOTS + 1)
                        src = bass.AP(rel_dram.tensor, row * NREL_PAD, [[1, P], [1, 2 * P]])
                        sp.dma_start(bias[:, u % BIAS_SLOTS, :], src).then_inc(S(f"bias_loaded_{u % BIAS_SLOTS}"), 16)
                if it[0] in WEIGHTS_OF and (WEIGHTS_OF[it[0]], it[1]) == JOBS[at]:
                    load(at)
                    at += 1
            for j in range(at, len(JOBS)):
                load(j)

            sp.wait_ge(S("rows_turned"), 1)
            sp.dma_start(place_rows, prow[:, :]).then_inc(S("places_stored"), 16)
            sp.dma_start(place_cols, pcol[:, :, :]).then_inc(S("places_stored"), 16)
            sp.wait_ge(S("places_stored"), 32)
            sp.wait_ge(S("work_ready"), 2)
            n_work = sp.value_load(work[0:1, 0:1], min_val=0, max_val=MAX_WORK)

            def load_block(i, r):
                v = sp.value_load(work[0:1, bass.ds(i + 1 + NV, 1)], min_val=0, max_val=NV - 1)
                done = S(f"block_loaded_{r}")
                sp.dma_start(col3[:, r, :].unsqueeze(1), place_cols[:, bass.ds(v, 1), :]).then_inc(done, 16)
                sp.dma_start(row3[:, r, :], place_rows[bass.ds(v, 1), :].to_broadcast([P, TOK])).then_inc(done, 16)

            def load_expert(i, r):
                e = sp.value_load(work[0:1, bass.ds(i + 1, 1)], min_val=0, max_val=N_EXP - 1)
                for m, name in enumerate(("w1_2", "w3_2")):
                    src = a[name][0].rearrange("e (p k) n -> p e (k n)", k=KT)[:, bass.ds(e, 1), :]
                    sp.dma_start(ew[r][:, 2048 * m:2048 * m + 2048].unsqueeze(1), src).then_inc(S(f"up_loaded_{r}"), 16)
                src = a["w2_2"][0].rearrange("e (p f) n -> p e (f n)", f=FT)[:, bass.ds(e, 1), :]
                sp.dma_start(ew[r][:, 4096:6144].unsqueeze(1), src).then_inc(S(f"down_loaded_{r}"), 16)

            for r in range(ESLOTS):
                if r == 1:
                    sp.wait_ge(S("shared_done"), 1)
                with sp.If(n_work > r - 1):
                    load_block(r, r)
                with sp.If(n_work > r):
                    load_expert(r, r)
            with sp.Fori(1, -(-MAX_WORK // ESLOTS)) as m:
                for r in range(ESLOTS):
                    with sp.If(n_work > m * ESLOTS + r - 1):
                        sp.wait_ge(S("block_done"), (m - 1) * ESLOTS + r + 1)
                        load_block(m * ESLOTS + r, r)
                    with sp.If(n_work > m * ESLOTS + r):
                        load_expert(m * ESLOTS + r, r)
            for t in range(NT):
                sp.wait_ge(S("out_ready"), 2 * t + 2)
                sp.dma_start(out[0, t * P:(t + 1) * P, :], x[:, t, :]).then_inc(S("out_stored"), 16)
            sp.wait_ge(S("out_stored"), 16 * NT)

        @block.gpsimd
        def _(gp):
            gp.memset(half_neg[:, :], -0.5).then_inc(S("half_neg_set"), 1)
            gp.memset(ones[:, :], 1.0).then_inc(S("ones_set"), 1)
            small = S("small_loaded")
            gp.dma_start(hot, a["c_hot"]).then_inc(small, 16)
            gp.dma_start(relmask, a["c_mask"]).then_inc(small, 16)
            gp.dma_start(tabT[:, :], a["rel_bias"].rearrange("h b -> b h")).then_inc(small, 16)
            for i, name in ((1, "norm1_g_2"), (2, "norm2_g_2")):
                gp.dma_start(ln_g[:, i, :], a[name][0].rearrange("(p k) -> p k", k=KT)).then_inc(small, 16)
            gp.dma_start(c_col[:, 0, :], a["c_2"][0].rearrange("(p k) -> p k", k=KT)).then_inc(small, 16)
            gp.dma_start(b_ada[:, :, :], a["b_ada_2"][0].rearrange("(s p k) -> p s k", s=6, k=KT)).then_inc(small, 16)
            for h in range(2):
                gp.dma_start(qk_g[HD * h:HD * h + HD, :], a["qk_g"][0].rearrange("g d -> d g")).then_inc(small, 16)
            gp.dma_start(sinks[:, :], a["sinks"].to_broadcast([P, 8])).then_inc(small, 16)
            for i, name in enumerate(("q_norm_g_2", "k_norm_g_2", "kidx_norm_g_2")):
                gp.dma_start(g2[:, i, :], a[name].to_broadcast([P, HD])).then_inc(small, 16)
            for i, s in enumerate((2, 5)):
                gp.dma_start(gate_bc[:, i, :], a["b_ada_2"][0:1, s * DM:(s + 1) * DM].to_broadcast([P, DM])).then_inc(small, 16)
            gp.wait_ge(S("half_neg_set"), 1)

            def inverse_root(width, count, ready, nth, done):
                gp.wait_ge(S(ready), nth)
                gp.tensor_scalar(msum[:, 0:width], msum[:, 0:width], 1.0 / count, EPS, ALU.mult, ALU.add)\
                  .then_inc(S("mean_eps"), 1)
                inverse_root.n += 1
                gp.wait_ge(S("mean_eps"), inverse_root.n)
                gp.tensor_tensor(rstd[:, 0:width], msum[:, 0:width], half_neg[:, 0:width], ALU.pow)\
                  .then_inc(S(done), 1)
            inverse_root.n = 0
            nx = 0
            for it in SCHEDULE:
                if it[0] in ("start", "norm"):
                    for t in range(NT):
                        nx += 1
                        inverse_root(1, DM, "x_squared", nx, "x_rstd")
                if it in NTH_NORM:
                    kind = CHUNKS[it[1]][0] if it[0] == "proj" else CHUNKS2[it[1]][0]
                    inverse_root({"kv": 2, "kiwi": 1}.get(kind, 8), HD, "head_sums", NTH_NORM[it] + 1, "head_rstd")
                if it[0] == "out1" and it[1:] == (1, 1):
                    bank_taken(gp, USE[it])
                    late = S("late_loaded")
                    gp.dma_start(pos_i[:, :], a["positions_2"][0].rearrange("(t p) -> p t", p=P)).then_inc(late, 16)
                    for j in range(3):
                        gp.dma_start(conv_w[:, j, :], a["conv_w_2"][0, j].rearrange("(k p) -> p k", p=P)).then_inc(late, 16)
                    gp.dma_start(w_router[:, :, :], a["w_router_2"][0].rearrange("(p k) n -> p k n", k=KT)).then_inc(late, 16)
                    gp.dma_start(rbias[:, :], a["router_bias_2"].to_broadcast([P, N_EXP])).then_inc(late, 16)

        @block.scalar
        def _(act):
            def x_square(t, nth):
                if nth >= 1:
                    act.wait_ge(S("x_rstd"), nth)
                    act.wait_ge(S("x_scaled"), nth)
                act.activation(qn[:, :, :].rearrange("p a n -> p (a n)"), x[:, t, :], ACT.Square, accum_out=msum[:, 0:1]).then_inc(S("x_squared"), 1)

            act.dma_start(consts[:, :], a["c_square"]).then_inc(S("consts_loaded"), 16)
            act.dma_start(ln_g[:, 0, :], a["ln_g"][0].rearrange("(p k) -> p k", k=KT)).then_inc(S("ln_g_loaded"), 16)
            nx = 0
            for it in SCHEDULE:
                if it[0] == "start":
                    for t in range(NT):
                        act.wait_ge(S(f"x_loaded_{t}"), 16)
                        x_square(t, nx)
                        nx += 1
                    act.wait_ge(S("small_loaded"), 16 * N_SMALL)
                    act.activation(c_col[:, 1, :], c_col[:, 0, :], ACT.Exp, scale=-1.0).then_inc(S("c_exp"), 1)
                if it[0] == "norm":
                    for t in range(NT):
                        bank_taken(act, USE[("out1" if it[1] == 0 else "out2", 1, 1)])
                        x_square(t, nx)
                        nx += 1
                if it[0] in ("proj", "proj2"):
                    n = USE[it]
                    kind, _, w, dst = (CHUNKS if it[0] == "proj" else CHUNKS2)[it[1]]
                    ps = proj_b[n % 2]
                    if it in NTH_NORM:
                        m = NTH_NORM[it]
                        w = {"kv": 128, "kiwi": 64}.get(kind, 512)
                        act.wait_ge(S("bank_full"), n + 1)
                        if m >= 1:
                            act.wait_ge(S("head_sums"), m)
                        act.activation(sq[:, 0:w], ps[:, 0:w], ACT.Square).then_inc(S("squared"), 1)
                    if kind in ("silu", "gate"):
                        act.wait_ge(S("bank_full"), n + 1)
                        if kind == "gate":
                            act.activation(G[:, it[2], dst:dst + 512], ps[:, :], ACT.Tanh, scale=0.5)\
                               .then_inc(S(f"bank_free_{n % 2}"), 1)
                        else:
                            m = NTH_GATE[it]
                            if m >= 1:
                                bank_taken(act, USE[GATED[m - 1]])
                            act.activation(egate[:, :], ps[:, :], ACT.Tanh, scale=0.5).then_inc(S("gate_tanh"), 1)
                if it[0] == "turn":
                    k = TURN[it]
                    kind, _, _, dst = CHUNKS[it[1]]
                    t = it[2]
                    act.wait_ge(S("turned"), k + 1)
                    src = turn_b[:, :].rearrange("p (b n) -> p b n", b=4)
                    if kind == "q":
                        br = 0 if dst < 4 else (1 if dst < 16 else 2)
                        act.wait_ge(S("q_scale_ready"), 2)
                        act.activation(qT[:, dst:dst + 4, t * P:(t + 1) * P], src, ACT.Copy,
                                       scale=q_scale[:, br:br + 1]).then_inc(S("turn_free"), 1)
                    elif kind == "k":
                        act.activation(kT[:, dst:dst + 4, t * P:(t + 1) * P], src, ACT.Copy).then_inc(S("turn_free"), 1)
                    else:
                        act.activation(kT[:, dst:dst + 2, t * P:(t + 1) * P], src[:, 0:2], ACT.Copy)\
                           .then_inc(S("turn_free"), 1)
                if it[0] == "turn_branch":
                    i = it[1]
                    dst = OT if i < 3 else mixT[:, WK:2 * WK, :]
                    for t in range(NT):
                        k = TURN[it + (t,)]
                        act.wait_ge(S("turned"), k + 1)
                        if i in (1, 2) and t == 0:
                            act.wait_ge(S("bank_full"), USE[("branch", i - 1, 1, 1)] + 1)
                        act.activation(dst[:, :, t * P:(t + 1) * P],
                                       turn_b[:, :].rearrange("p (b n) -> p b n", b=4), ACT.Copy,
                                       scale=0.5 if i < 3 else 1.0).then_inc(S("turn_free"), 1)
                if it[0] == "turn_merged":
                    for t in range(NT):
                        for q in range(2):
                            act.wait_ge(S("turned"), TURN[it + (t, q)] + 1)
                            act.activation(xT[:, 4 * q:4 * q + 4, t * P:(t + 1) * P],
                                           turn_b[:, :].rearrange("p (b n) -> p b n", b=4), ACT.Copy, scale=0.5)\
                               .then_inc(S("turn_free"), 1)
                if it[0] == "turn2":
                    for g in range(4):
                        for t in range(NT):
                            act.wait_ge(S("turned"), TURN[it + (g, t)] + 1)
                            nb = 4 if g < 3 else 1
                            act.activation(T2[:, 4 * g:4 * g + nb, t * P:(t + 1) * P],
                                           turn_b[:, 0:P * nb].rearrange("p (b n) -> p b n", b=nb), ACT.Copy,
                                           scale=SCALE if g == 0 else 1.0).then_inc(S("turn_free"), 1)
                if it[0] == "rope":
                    act.wait_ge(S("angles_ready"), 1)
                    act.activation(trig[:, :, :, :], ang[:, :, :, :], ACT.Sin).then_inc(S("trig_ready"), 1)
                if it[0] == "index":
                    u = len(UNITS) + it[1]
                    h = it[1]
                    act.wait_ge(S("index_product"), h + 1)
                    if h >= 2:
                        act.wait_ge(S("index_added"), h - 1)
                    act.activation(relu[:, h % 2, :], score_b[h % 2][:, 0:384], ACT.Relu).then_inc(S("relu_done"), 1)
                if it[0] == "score":
                    n = it[1]
                    ng = len(units_of(n)) if n < 24 else 1
                    sink = 1 if 16 <= n < 24 else 0
                    i = HEADS.index(n)
                    act.wait_ge(S("maxed"), 2 * i + 2)
                    for t in range(NT):
                        lo, w = (0, P + sink) if t == 0 else (P + 1, 2 * P + sink)
                        v = L[:, i % 2, 0:ng, lo:lo + w]
                        act.activation(v, v, ACT.Exp, bias=nmax[:, i % 2, t:t + 1],
                                       accum_out=den[:, i % 2, t:t + 1]).then_inc(S("probs"), 1)
                if it[0] == "flip":
                    n = it[1]
                    ng = len(units_of(n)) if n < 24 else 1
                    i = HEADS.index(n)
                    for g in range(ng):
                        u = UNIT[n, g]
                        act.wait_ge(S("flipped"), u + 1)
                        if i >= 2:
                            act.wait_ge(S("value_product"), 2 * (i - 1))
                        act.activation(PT[:, i % 2, g, :], flip_b[u % 2][:, 0:384], ACT.Copy).then_inc(S("probsT"), 1)
                if it[0] == "router":
                    act.wait_ge(S("router_args"), 2)
                    act.activation(rexp[:, :, :, :], rarg[:, :, :, :], ACT.Exp).then_inc(S("router_exp"), 1)

            for k in range(KT // 2):
                for t in range(NT):
                    n = 2 * k + t
                    act.wait_ge(S("h2_turned"), n + 1)
                    act.activation(x_hi[:, t, 2 * k:2 * k + 2, :],
                                   y_b[t][:, 0:2 * P].rearrange("p (b n) -> p b n", b=2), ACT.Copy)\
                       .then_inc(S("x_hi_ready"), 1)
            for f in range(FT):
                act.wait_ge(S(f"up_{f}"), 1)
                act.activation(hs[:, f, :], up_b[f][:, 0:TOK], ACT.Silu).then_inc(S(f"silu_{f}"), 1)

            def copy_block(nth, q):
                act.wait_ge(S(f"gathered_{q}"), nth)
                act.activation(xe[:, 4 * q:4 * q + 4, :], up_b[q][:, :].rearrange("p (b n) -> p b n", b=4), ACT.Copy)\
                   .then_inc(S(f"block_ready_{q}"), 1)

            for q in range(2):
                copy_block(1, q)
            act.wait_ge(S("work_ready"), 2)
            n_work = act.value_load(work[0:1, 0:1], min_val=0, max_val=MAX_WORK)
            with act.Fori(0, MAX_WORK) as i:
                with act.If(n_work > i):
                    for f in range(FT):
                        act.wait_ge(S(f"h_ready_{f}"), i + 1)
                        act.wait_ge(S(f"up_{f}"), i + 2)
                        if f == 0:
                            act.wait_ge(S("gates_gathered"), i + 1)
                        act.activation(hs[:, f, 0:P], up_b[f][:, 0:P], ACT.Silu).then_inc(S(f"silu_{f}"), 1)
                    copy_block(i + 2, 0)
                    for hf in range(2):
                        act.wait_ge(S(f"down_{hf}"), i + 1)
                        act.activation(y_hi[:, hf * CH:(hf + 1) * CH], y_b[hf][:, :], ACT.Copy, scale=gcol[:, 0:1])\
                           .then_inc(S(f"y_hi_{hf}"), 1)
                    copy_block(i + 2, 1)

        @block.vector
        def _(dve):
            n_scaled = 0

            def x_scale(t):
                nonlocal n_scaled
                dve.wait_ge(S("x_rstd"), n_scaled + 1)
                dve.tensor_scalar(xn, x[:, t, :], rstd[:, 0:1], None, ALU.mult).then_inc(S("x_scaled"), 1)
                n_scaled += 1

            def bc(ap2, n):
                return ap2.unsqueeze(2).to_broadcast([ap2.shape[0], ap2.shape[1], n])

            n_gt = 0
            for it in SCHEDULE:
                kind0 = it[0]
                if kind0 in ("start", "norm"):
                    w = 0 if kind0 == "start" else 1 + it[1]
                    if kind0 == "start":
                        dve.wait_ge(S("ln_g_loaded"), 16)
                    if kind0 == "norm":
                        m = it[1]
                        dve.wait_ge(S("turn_free"), TURN["ada_out", N_ADA - 1] + 1)
                        dve.tensor_tensor(mod[:, 2 * m + 1, :], mod[:, 2 * m + 1, :], ln_g[:, w, :], ALU.mult)\
                           .then_inc(S("mod_ready"), 1)
                    for t in range(NT):
                        x_scale(t)
                        for q in range(2):
                            dve.wait_ge(S("turned"), TURN[it + (t, q)] + 1)
                            src = turn_b[:, :].rearrange("p (b n) -> p b n", b=4)
                            if kind0 == "start":
                                dve.tensor_tensor(xT[:, 4 * q:4 * q + 4, t * P:(t + 1) * P], src,
                                                  bc(ln_g[:, 0, 4 * q:4 * q + 4], P), ALU.mult).then_inc(S("turn_free"), 1)
                            else:
                                dve.wait_ge(S("mod_ready"), m + 1)
                                for b in range(4):
                                    k = 4 * q + b
                                    last = dve.tensor_scalar(xT[:, k, t * P:(t + 1) * P], src[:, b],
                                                             mod[:, 2 * m + 1, k:k + 1], mod[:, 2 * m, k:k + 1],
                                                             ALU.mult, ALU.add)
                                last.then_inc(S("turn_free"), 1)
                if kind0 == "start":
                    dve.wait_ge(S("small_loaded"), 16 * N_SMALL)
                    dve.wait_ge(S("c_exp"), 1)
                    dve.tensor_scalar(c_col[:, 1, :], c_col[:, 1, :], 1.0, None, ALU.add).then_inc(S("c_step"), 1)
                    dve.wait_ge(S("c_step"), 1)
                    dve.reciprocal(c_col[:, 2, :], c_col[:, 1, :]).then_inc(S("c_step"), 1)
                    dve.wait_ge(S("c_step"), 2)
                    dve.tensor_tensor(c_col[:, 1, :], c_col[:, 0, :], c_col[:, 2, :], ALU.mult).then_inc(S("c_step"), 1)
                    gains = qk_g[:, :].rearrange("p (b two) -> p b two", two=2)
                    dve.tensor_tensor(q_scale[:, :], gains[:, :, 0], gains[:, :, 1], ALU.mult).then_inc(S("q_scale_ready"), 1)
                    dve.wait_ge(S("q_scale_ready"), 1)
                    dve.tensor_scalar(q_scale[:, :], q_scale[:, :], SCALE, None, ALU.mult).then_inc(S("q_scale_ready"), 1)
                    dve.wait_ge(S("rel_product"), 1)
                    dve.tensor_tensor(relrow, bank[6][0:40, 0:NREL_PAD], relmask, ALU.add)\
                       .then_inc(S("rel_ready"), 1)
                if kind0 in ("proj", "proj2"):
                    n, t = USE[it], it[2]
                    kind, _, w, dst = (CHUNKS if kind0 == "proj" else CHUNKS2)[it[1]]
                    ps = proj_b[n % 2]
                    free = S(f"bank_free_{n % 2}")
                    if it in NTH_NORM:
                        m = NTH_NORM[it]
                        nh = {"kv": 2, "kiwi": 1}.get(kind, 8)
                        dve.wait_ge(S("squared"), m + 1)
                        if m >= 1:
                            dve.wait_ge(S("head_rstd"), m)
                        dve.tensor_reduce(msum[:, 0:nh], sq[:, 0:nh * HD].rearrange("p (h d) -> p h d", d=HD),
                                          AX.X, ALU.add).then_inc(S("head_sums"), 1)
                        dve.wait_ge(S("head_rstd"), m + 1)
                        heads = ps[:, 0:nh * HD].rearrange("p (h d) -> p h d", d=HD)
                        r8 = bc(rstd[:, 0:nh], HD)
                        if kind in ("q", "k"):
                            if m >= 2:
                                dve.wait_ge(S("turned"), TURN[("turn",) + NORMED[m - 2][1:]] + 1)
                            dve.tensor_tensor(qn[:, m % 2, :].rearrange("p (h d) -> p h d", d=HD), heads, r8, ALU.mult)\
                               .then_inc(free, 1)
                        elif kind == "kv":
                            dve.wait_ge(S("turned"), TURN[("turn",) + NORMED[m - 2][1:]] + 1)
                            o = qn[:, m % 2, 0:256].rearrange("p (g c d) -> p g c d", g=2, c=2)
                            for c in range(2):
                                dve.tensor_tensor(o[:, :, c, :], heads, r8, ALU.mult).then_inc(S("kv_step"), 1)
                            dve.tensor_copy(V[:, t, 2048:2176], ps[:, 128:256]).then_inc(free, 1)
                        else:
                            gi = {"q2": 0, "k2": 1, "kiwi": 2}[kind]
                            o = R[:, t, dst:dst + nh, :]
                            dve.tensor_tensor(o, heads, r8, ALU.mult).then_inc(S("r2_step"), 1)
                            n_gt += 1
                            dve.wait_ge(S("r2_step"), n_gt)
                            gains = g2[:, gi:gi + 1, :].to_broadcast([P, nh, HD])
                            if kind == "kiwi":
                                dve.tensor_copy(wi[:, t, :], ps[:, 64:72]).then_inc(S("wi_ready"), 1)
                            dve.tensor_tensor(o, o, gains, ALU.mult).then_inc(free, 1)
                    elif kind == "v":
                        dve.wait_ge(S("bank_full"), n + 1)
                        dve.tensor_copy(V[:, t, dst:dst + 512], ps[:, :]).then_inc(free, 1)
                    elif kind == "v2":
                        dve.wait_ge(S("bank_full"), n + 1)
                        dve.tensor_copy(V2[:, t, :], ps[:, :]).then_inc(free, 1)
                    elif kind == "qi":
                        dve.wait_ge(S("bank_full"), n + 1)
                        dve.tensor_copy(R[:, t, dst:dst + 8, :], ps[:, :].rearrange("p (h d) -> p h d", d=HD))\
                           .then_inc(free, 1)
                    elif kind == "gate":
                        pass
                    elif kind == "silu":
                        dve.wait_ge(S("gate_tanh"), NTH_GATE[it] + 1)
                        dve.scalar_tensor_tensor(out=O[:, dst, t, :], in0=egate[:, :], scalar=1.0, in1=ps[:, :],
                                                 op0=ALU.add, op1=ALU.mult).then_inc(free, 1)
                    else:
                        v = ps[:, :].rearrange("p (c n) -> p c n", c=2)
                        dve.wait_ge(S("bank_full"), n + 1)
                        if kind == "xc":
                            dve.tensor_copy(xcT[:, 2 * t:2 * t + 2, :], v).then_inc(free, 1)
                        elif kind == "cg":
                            bank_taken(dve, USE["proj2", it[1] - 1, t])
                            if t == 0:
                                dve.memset(uT[:, :, 0:2], 0.0).then_inc(S("u_pad"), 1)
                            dve.tensor_tensor(uT[:, 2 * t:2 * t + 2, 2:TOK + 2], v, xcT[:, 2 * t:2 * t + 2, :], ALU.mult)\
                               .then_inc(free, 1)
                        else:
                            bank_taken(dve, USE["proj2", it[1] - 1, t])
                            dve.wait_ge(S("late_loaded"), 16 * N_LATE)
                            dve.wait_ge(S("u_pad"), 1)
                            for c in range(2):
                                ct = 2 * t + c
                                s0 = 4 * ct - ct // 2
                                if ct % 2:
                                    dve.wait_ge(S("conv_step"), s0)
                                elif t:
                                    bank_taken(dve, n - 1)
                                dve.tensor_scalar(cv[:, :], uT[:, ct, 0:TOK], conv_w[:, 0, ct:ct + 1], None, ALU.mult)\
                                   .then_inc(S("conv_step"), 1)
                                for j in (1, 2):
                                    dve.wait_ge(S("conv_step"), s0 + j)
                                    dve.scalar_tensor_tensor(out=cv[:, :], in0=uT[:, ct, j:TOK + j],
                                                             scalar=conv_w[:, j, ct:ct + 1], in1=cv[:, :],
                                                             op0=ALU.mult, op1=ALU.add).then_inc(S("conv_step"), 1)
                                dve.wait_ge(S("conv_step"), s0 + 3)
                                dve.tensor_tensor(mixT[:, ct, :], v[:, c], cv[:, :], ALU.mult)\
                                   .then_inc(free if c else S("conv_step"), 1)
                if kind0 == "branch":
                    _, i, hf, t = it
                    n = USE[it]
                    g = G[:, t, i * DM + hf * CH:i * DM + hf * CH + CH]
                    g0 = G[:, t, hf * CH:hf * CH + CH]
                    dve.wait_ge(S("bank_full"), n + 1)
                    c = [k for k, ch in enumerate(CHUNKS) if ch[0] == "gate"][2 * i + hf]
                    bank_taken(dve, USE["proj", c, t])
                    done = S("merge_step" if i else f"bank_free_{n % 2}")
                    dve.scalar_tensor_tensor(out=g, in0=g, scalar=1.0, in1=proj_b[n % 2][:, :], op0=ALU.add, op1=ALU.mult)\
                       .then_inc(done, 1)
                    if i:
                        dve.wait_ge(S("merge_step"), 4 * (i - 1) + 2 * hf + t + 1)
                        bank_taken(dve, USE["branch", i - 1, hf, t])
                        dve.tensor_tensor(g0, g0, g, ALU.add).then_inc(S(f"bank_free_{n % 2}"), 1)
                if kind0 == "out1":
                    _, hf, t = it
                    n = USE[it]
                    o = x[:, t, hf * CH:hf * CH + CH]
                    dve.wait_ge(S("bank_full"), n + 1)
                    dve.tensor_tensor(o, o, proj_b[n % 2][:, :], ALU.add).then_inc(S(f"bank_free_{n % 2}"), 1)
                if kind0 == "out2":
                    _, hf, t = it
                    n = USE[it]
                    o = x[:, t, hf * CH:hf * CH + CH]
                    tmp = qn[:, n % 2, :]
                    dve.wait_ge(S("bank_full"), n + 1)
                    dve.tensor_tensor(tmp, proj_b[n % 2][:, :], gate_bc[:, 0, hf * CH:hf * CH + CH], ALU.mult)\
                       .then_inc(S("mix_step"), 1)
                    dve.wait_ge(S("mix_step"), 2 * hf + t + 1)
                    dve.tensor_tensor(o, o, tmp, ALU.add).then_inc(S(f"bank_free_{n % 2}"), 1)
                if kind0 == "ada":
                    _, c, part = it
                    j = JOB["w_ada", c]
                    o = ada_acc[:, c % 2, :]
                    w = view(j, "k8")
                    if part == 0:
                        job_ready(dve, j)
                        if c >= 2:
                            dve.wait_ge(S("turned"), TURN["ada_out", c - 2] + 1)
                        if c == 0:
                            dve.wait_ge(S("c_step"), 3)
                        dve.tensor_scalar(o, w[:, 0], c_col[:, 1, 0:1], None, ALU.mult).then_inc(S("ada_step"), 1)
                    for k in range(max(1, 2 * part), 2 * part + 2):
                        dve.wait_ge(S("ada_step"), (KT - 1) * c + k)
                        dve.scalar_tensor_tensor(out=o, in0=w[:, k], scalar=c_col[:, 1, k:k + 1], in1=o,
                                                 op0=ALU.mult, op1=ALU.add)\
                           .then_inc(S("ada_step" if k < KT - 1 else "ada_summed"), 1)
                if kind0 == "ada_out":
                    c = it[1]
                    s, hf = c // 2, c % 2
                    k = TURN[it]
                    dve.wait_ge(S("turned"), k + 1)
                    dve.wait_ge(S("small_loaded"), 16 * N_SMALL)
                    if s in (2, 5):
                        o = gate_bc[:, s // 3, hf * CH:(hf + 1) * CH]
                        dve.tensor_tensor(o, o, turn_b[:, :], ALU.add).then_inc(S("turn_free"), 1)
                    else:
                        m = {0: 0, 1: 1, 3: 2, 4: 3}[s]
                        rows = slice(HD * hf, HD * hf + HD)
                        dve.scalar_tensor_tensor(out=mod[rows, m, :], in0=turn_b[rows, 0:KT], scalar=float(s in (1, 4)),
                                                 in1=b_ada[rows, s, :], op0=ALU.add, op1=ALU.add)\
                           .then_inc(S("turn_free"), 1)
                if kind0 == "score":
                    n = it[1]
                    i = HEADS.index(n)
                    ng = len(units_of(n)) if n < 24 else 1
                    sink = 1 if 16 <= n < 24 else 0
                    buf = L[:, i % 2]
                    for g in range(ng):
                        u = UNIT[n, g]
                        if i >= 2 and g == 0:
                            dve.wait_ge(S("flipped"), UNIT[HEADS[i - 2], 0] + (len(units_of(HEADS[i - 2])) if HEADS[i - 2] < 24 else 1))
                        dve.wait_ge(S("scored"), u + 1)
                        if n < 24:
                            dve.wait_ge(S(f"bias_loaded_{u % BIAS_SLOTS}"), 16 * (u // BIAS_SLOTS + 1))
                            back = bias[:, u % BIAS_SLOTS, ::-1]
                            add = [back[:, P:2 * P], back]
                        else:
                            dve.wait_ge(S("selmask_ready"), 1)
                            add = [selmask[:, 0:P], selmask[:, P:3 * P]]
                        ps = score_b[u % 2]
                        dve.tensor_tensor(buf[:, g, 0:P], ps[:, 0:P], add[0], ALU.add).then_inc(S("logits_half"), 1)
                        dve.tensor_tensor(buf[:, g, P + 1:3 * P + 1], ps[:, P:3 * P], add[1], ALU.add)\
                           .then_inc(S("logits"), 1)
                    if sink:
                        h = n - 16
                        for t in range(NT):
                            at = (P, 3 * P + 1)[t]
                            dve.tensor_copy(buf[:, 0, at:at + 1], sinks[:, h:h + 1]).then_inc(S("sink_set"), 1)
                        dve.wait_ge(S("sink_set"), 2 * h + 2)
                    dve.wait_ge(S("logits"), UNIT[n, ng - 1] + 1)
                    if i >= 2:
                        dve.wait_ge(S("probs"), 2 * i - 2)
                    for t in range(NT):
                        lo, w = (0, P + sink) if t == 0 else (P + 1, 2 * P + sink)
                        dve.tensor_reduce(nmax[:, i % 2, t:t + 1], buf[:, 0:ng, lo:lo + w],
                                          AX.XY, ALU.max, negate=True).then_inc(S("maxed"), 1)
                if kind0 == "value":
                    n = it[1]
                    i = HEADS.index(n)
                    dve.wait_ge(S("probs"), 2 * i + 2)
                    dve.reciprocal(rden[:, i % 2, :], den[:, i % 2, :]).then_inc(S("rden_ready"), 1)
                    dve.wait_ge(S("rden_ready"), i + 1)
                    for t in range(NT):
                        dve.wait_ge(S("value_product"), 2 * i + 2)
                        ps = value_b[:, 128 * (i % 2) + 64 * t:128 * (i % 2) + 64 * t + 64]
                        if n < 24:
                            o = O[:, n // 8, t, HD * (n % 8):HD * (n % 8) + HD]
                            if n % 8 == 0 and t == 0:
                                c = [k for k, ch in enumerate(CHUNKS) if ch[0] == "silu"][n // 8]
                                bank_taken(dve, USE["proj", c, 1])
                            dve.scalar_tensor_tensor(out=o, in0=ps, scalar=rden[:, i % 2, t:t + 1], in1=o,
                                                     op0=ALU.mult, op1=ALU.mult).then_inc(S("valued"), 1)
                        else:
                            o = O2[:, t, HD * (n - 24):HD * (n - 24) + HD]
                            dve.tensor_scalar(o, ps, rden[:, i % 2, t:t + 1], None, ALU.mult).then_inc(S("valued"), 1)
                if kind0 == "rope":
                    step = S("rope_step")
                    k = 0

                    def chain(ins):
                        nonlocal k
                        ins.then_inc(step, 1)
                        k += 1
                        dve.wait_ge(step, k)

                    dve.wait_ge(S("late_loaded"), 16 * N_LATE)
                    chain(dve.tensor_copy(pos[:, :], pos_i[:, :]))
                    for t in range(NT):
                        chain(dve.tensor_scalar(ang[:, t, 1, :], consts[:, C_FREQ:C_FREQ + 8], pos[:, t:t + 1], None,
                                                ALU.mult))
                    chain(dve.tensor_scalar(turns_f[:, :, 1, :], ang[:, :, 1, :], 1.0 / (2 * math.pi), None, ALU.mult))
                    chain(dve.tensor_scalar(turns_f[:, :, 0, :], turns_f[:, :, 1, :], 0.25, None, ALU.add))
                    chain(dve.tensor_copy(turns_i[:, :, :, :], turns_f[:, :, :, :]))
                    chain(dve.tensor_copy(turns_f[:, :, :, :], turns_i[:, :, :, :]))
                    chain(dve.tensor_copy(ang[:, :, 0, :], ang[:, :, 1, :]))
                    c1 = 6.28125
                    c2 = float(np.float32(np.floor((2 * math.pi - c1) * 2 ** 20) / 2 ** 20))
                    c3 = 2 * math.pi - c1 - c2
                    for c in (c1, c2, c3):
                        chain(dve.scalar_tensor_tensor(out=ang[:, :, :, :], in0=turns_f[:, :, :, :], scalar=-c,
                                                       in1=ang[:, :, :, :], op0=ALU.mult, op1=ALU.add))
                    chain(dve.tensor_scalar(ang[:, :, 0, :], ang[:, :, 0, :], math.pi / 2, None, ALU.add))
                    for op, lim, sign in ((ALU.is_gt, math.pi, -1.0), (ALU.is_lt, -math.pi, 1.0)):
                        chain(dve.tensor_scalar(wrap[:, :, :, :], ang[:, :, :, :], lim, sign * 2 * math.pi, op, ALU.mult))
                        chain(dve.tensor_tensor(ang[:, :, :, :], ang[:, :, :, :], wrap[:, :, :, :], ALU.add))
                    dve.tensor_scalar(ang[:, :, :, :], ang[:, :, :, :], 3.1415925, -3.1415925, ALU.min, ALU.max)\
                       .then_inc(S("angles_ready"), 1)
                    dve.wait_ge(S("trig_ready"), 1)
                    bank_taken(dve, USE["proj2", 3, 1])
                    for t in range(NT):
                        lo, hi = R[:, t, 0:25, 0:8], R[:, t, 0:25, 8:16]
                        cos = trig[:, t, 0:1, :].to_broadcast([P, 25, 8])
                        sin = trig[:, t, 1:2, :].to_broadcast([P, 25, 8])
                        for b, (src, f) in enumerate(((lo, cos), (hi, sin), (hi, cos), (lo, sin))):
                            chain(dve.tensor_tensor(rt[:, b], src, f, ALU.mult))
                        chain(dve.tensor_tensor(lo, rt[:, 0], rt[:, 1], ALU.subtract))
                        chain(dve.tensor_tensor(hi, rt[:, 2], rt[:, 3], ALU.add))
                        dve.tensor_copy(R[:, t, 25, :], R[:, t, 24, :]).then_inc(S("rows_ready"), 1)
                if kind0 == "index":
                    h = it[1]
                    dve.wait_ge(S("relu_done"), h + 1)
                    dve.wait_ge(S("wi_ready"), 2)
                    for t, (lo, w) in enumerate(((0, P), (P, 2 * P))):
                        o = score[:, lo:lo + w]
                        r = relu[:, h % 2, lo:lo + w]
                        done = S("index_half" if t == 0 else "index_added")
                        if h == 0:
                            dve.tensor_scalar(o, r, wi[:, t, h:h + 1], None, ALU.mult).then_inc(done, 1)
                        else:
                            dve.wait_ge(done, h)
                            dve.scalar_tensor_tensor(out=o, in0=r, scalar=wi[:, t, h:h + 1], in1=o,
                                                     op0=ALU.mult, op1=ALU.add).then_inc(done, 1)
                if kind0 == "topk":
                    step = S("topk_step")
                    k = 0

                    def chain(ins):
                        nonlocal k
                        ins.then_inc(step, 1)
                        k += 1
                        dve.wait_ge(step, k)

                    caus = [consts[:, C_CAUS + P:C_CAUS + 2 * P], consts[:, C_CAUS:C_CAUS + 2 * P]]
                    dve.wait_ge(S("index_added"), 8)
                    for t, (lo, w) in enumerate(((0, P), (P, 2 * P))):
                        o = score[:, lo:lo + w]
                        chain(dve.scalar_tensor_tensor(out=o, in0=o, scalar=IDX_SCALE, in1=caus[t],
                                                       op0=ALU.mult, op1=ALU.add))
                        for _ in range(TOP_KEYS // 8):
                            chain(dve.max(top8[:, t, :], o))
                            chain(dve.match_replace(out=o, in_to_replace=top8[:, t, :], in_values=o, imm_value=TAKEN))
                        chain(dve.tensor_scalar(o, o, TAKEN / 2, NEG, ALU.is_gt, ALU.mult))
                        last = dve.tensor_tensor(selmask[:, lo:lo + w], o, caus[t], ALU.add)
                        if t == 0:
                            chain(last)
                        else:
                            last.then_inc(S("selmask_ready"), 1)
                if kind0 == "router":
                    step = S("router_step")
                    k = 0

                    def chain(ins):
                        nonlocal k
                        ins.then_inc(step, 1)
                        k += 1
                        dve.wait_ge(step, k)

                    dve.wait_ge(S("router_product"), 1)
                    z = turn_b[:, 0:NT * N_EXP].rearrange("p (t e) -> p t e", t=NT)
                    dve.tensor_scalar(rarg[:, 0], z, 0.0, None, ALU.min).then_inc(S("router_args"), 1)
                    dve.wait_ge(S("router_args"), 1)
                    dve.scalar_tensor_tensor(out=rarg[:, 1], in0=rarg[:, 0], scalar=2.0, in1=z, op0=ALU.mult,
                                             op1=ALU.subtract)\
                       .then_inc(S("router_args"), 1)
                    dve.wait_ge(S("router_exp"), 1)
                    chain(dve.tensor_scalar(rexp[:, 1], rexp[:, 1], 1.0, None, ALU.add))
                    chain(dve.reciprocal(rexp[:, 1], rexp[:, 1]))
                    chain(dve.tensor_tensor(sig[:, :, :], rexp[:, 0], rexp[:, 1], ALU.mult))
                    chain(dve.tensor_tensor(sel[:, :, :], sig[:, :, :],
                                            rbias[:, :].unsqueeze(1).to_broadcast([P, NT, N_EXP]), ALU.add))
                    for t in range(NT):
                        chain(dve.max(top8[:, t, :], sel[:, t, :]))
                        chain(dve.match_replace(out=sel[:, t, :], in_to_replace=top8[:, t, :], in_values=sel[:, t, :],
                                                imm_value=TAKEN))
                    chain(dve.tensor_scalar(sel[:, :, :], sel[:, :, :], TAKEN / 2, None, ALU.is_lt))
                    chain(dve.tensor_tensor(sig[:, :, :], sig[:, :, :], sel[:, :, :], ALU.mult))
                    chain(dve.tensor_reduce(gsum[:, :], sig[:, :, :], AX.X, ALU.add))
                    chain(dve.reciprocal(gsum[:, :], gsum[:, :]))
                    for j in range(2):
                        ins = dve.tensor_copy(taken[:, :, N_EXP * j:N_EXP * j + N_EXP], sel[:, :, :])
                        ins.then_inc(S("taken_ready"), 1)
                    for t in range(NT):
                        for j in range(2):
                            chain(dve.tensor_scalar(pcol[:, N_EXP * j:N_EXP * j + N_EXP, NT + t], sig[:, t, :],
                                                    gsum[:, t:t + 1], ROUTED, ALU.mult, ALU.mult))
                    dve.wait_ge(S("ranked"), 1)
                    counted = y_b[0][:, 2 * NV:2 * NV + 1]
                    dve.tensor_scalar(used[:, :], counted, consts[:, C_THR:C_THR + 1], None, ALU.is_gt)\
                       .then_inc(S("used_ready"), 1)
                    for t in range(NT):
                        chain(dve.tensor_tensor(ranks[:, t, :], y_b[0][:, NV * t:NV * t + NV],
                                                consts[:, C_THR_ROW:C_THR_ROW + NV], ALU.subtract))
                        chain(dve.tensor_tensor(ranks[:, t, :], ranks[:, t, :], taken[:, t, :], ALU.mult))
                        dve.tensor_scalar(ranks[:, t, :], ranks[:, t, :], -FAR, None, ALU.add)\
                           .then_inc(S("ranks_ready"), 1)
                    dve.wait_ge(S("places_counted"), 1)
                    chain(dve.tensor_copy(place[:, :], y_b[1][:, 0:1]))
                    dve.wait_ge(S("used_ready"), 1)
                    dve.tensor_scalar(order[:, :], consts[:, C_IOTA:C_IOTA + NV], place[:, 0:1],
                                      used[:, 0:1], ALU.is_equal, ALU.mult).then_inc(S("order_ready"), 1)
                    dve.wait_ge(S("ranks_ready"), NT)
                    for t in range(NT):
                        chain(dve.tensor_copy(pcol[:, :, t], ranks[:, t, :]))
                    dve.wait_ge(S("ranks_turned"), 1)
                    dve.tensor_copy(prow[:, :], y_b[0][:, 0:TOK]).then_inc(S("rows_turned"), 1)
                    dve.wait_ge(S("list_product"), 1)
                    dve.tensor_copy(work[0:1, 1:1 + 2 * NV], y_b[1][0:1, 0:2 * NV]).then_inc(S("work_ready"), 1)
                    dve.tensor_copy(work[0:1, 0:1], y_b[1][0:1, 2 * NV:2 * NV + 1]).then_inc(S("work_ready"), 1)

            for k in range(KT // 2):
                for t in range(NT):
                    n = 2 * k + t
                    dve.wait_ge(S("x_hi_ready"), n + 1)
                    sl = x_hi[:, t, 2 * k:2 * k + 2, :]
                    dve.tensor_tensor(x_lo[:, t, 2 * k:2 * k + 2, :],
                                      y_b[t][:, 0:2 * P].rearrange("p (b n) -> p b n", b=2), sl.bitcast(F32),
                                      ALU.subtract).then_inc(S("x_lo_ready"), 1)
            for f in range(FT):
                dve.wait_ge(S(f"silu_{f}"), 1)
                dve.tensor_tensor(hT[:, f, :], hs[:, f, :], up_b[f][:, TOK:2 * TOK], ALU.mult).then_inc(S(f"h_ready_{f}"), 1)

            def make_picks(r, loads):
                dve.wait_ge(S(f"block_loaded_{r}"), loads)
                dve.tensor_tensor(pick[:, r], consts[:, C_IOTA:C_IOTA + P].unsqueeze(1).to_broadcast([P, NT, P]),
                                  bc(col3[:, r, 0:NT], P), ALU.is_equal).then_inc(S("pick_ready"), 1)
                dve.tensor_scalar(put[:, r, :], row3[:, r, :], consts[:, C_COL:C_COL + 1], None, ALU.is_equal)\
                   .then_inc(S("put_ready"), 1)

            make_picks(0, 32)
            dve.wait_ge(S("work_ready"), 2)
            n_work = dve.value_load(work[0:1, 0:1], min_val=0, max_val=MAX_WORK)
            with dve.Fori(0, -(-MAX_WORK // ESLOTS)) as m:
                for r in range(ESLOTS):
                    i = m * ESLOTS + r
                    with dve.If(n_work > i):
                        make_picks((r + 1) % ESLOTS, 32 * (m + 1 + (r + 1) // ESLOTS))
                        dve.wait_ge(S("up_0"), i + 2)
                        dve.tensor_copy(gcol[:, :], up_b[0][:, 2 * P:2 * P + 1]).then_inc(S("gates_gathered"), 1)
                        for f in range(FT):
                            dve.wait_ge(S(f"silu_{f}"), i + 2)
                            dve.tensor_tensor(hT[:, f, 0:P], hs[:, f, 0:P], up_b[f][:, P:2 * P], ALU.mult)\
                               .then_inc(S(f"h_ready_{f}"), 1)
                        dve.wait_ge(S("gates_gathered"), i + 1)
                        for hf in range(2):
                            dve.wait_ge(S(f"y_hi_{hf}"), i + 1)
                            c = slice(hf * CH, (hf + 1) * CH)
                            dve.scalar_tensor_tensor(out=y_lo[:, c], in0=y_b[hf][:, :], scalar=gcol[:, 0:1],
                                                     in1=y_hi[:, c].bitcast(F32), op0=ALU.mult, op1=ALU.subtract)\
                               .then_inc(S(f"y_lo_{hf}"), 1)
            dve.wait_ge(S("experts_summed"), 1)
            for t in range(NT):
                for hf in range(2):
                    tmp = qn[:, hf, :]
                    o = x[:, t, hf * CH:hf * CH + CH]
                    dve.tensor_tensor(tmp, acc_b[2 * t + hf][:, :], gate_bc[:, 1, hf * CH:hf * CH + CH], ALU.mult)\
                       .then_inc(S("final_step"), 1)
                    dve.wait_ge(S("final_step"), 2 * t + hf + 1)
                    dve.tensor_tensor(o, o, tmp, ALU.add).then_inc(S("out_ready"), 1)

        @block.tensor
        def _(pe):
            def turn_bank(k):
                if k >= 1:
                    pe.wait_ge(S("turn_free"), k)

            def use_bank(n):
                if n >= 2:
                    bank_taken(pe, n - 2)
                return proj_b[n % 2]

            for it in SCHEDULE:
                kind0 = it[0]
                if kind0 == "start":
                    pe.wait_ge(S("consts_loaded"), 16)
                    pe.wait_ge(S("ones_set"), 1)
                if kind0 in ("start", "norm"):
                    base = {("start",): 0, ("norm", 0): NT, ("norm", 1): 2 * NT}[it]
                    for t in range(NT):
                        pe.wait_ge(S("x_scaled"), base + t + 1)
                        for q in range(2):
                            turn_bank(TURN[it + (t, q)])
                            for b in range(4):
                                k = 4 * q + b
                                mm = pe.transpose(turn_b[:, b * P:(b + 1) * P], xn[:, k:DM:KT], ident)
                            mm.then_inc(S("turned"), 1)
                if kind0 == "start":
                    pe.wait_ge(S("small_loaded"), 16 * N_SMALL)
                    pe.matmul(bank[6][0:40, 0:NREL_PAD], tabT[:, :], hot, start=True, stop=True)\
                      .then_inc(S("rel_product"), 1)
                if kind0 == "proj":
                    _, c, t = it
                    n = USE[it]
                    kind, _, w, _ = CHUNKS[c]
                    j = JOB["w_in", c]
                    ps = use_bank(n)
                    if n == 0:
                        pe.wait_ge(S("turn_free"), 4)
                    if t == 0:
                        job_ready(pe, j)
                    wv = view(j, "kv" if w == 256 else "k8")
                    for k in range(KT):
                        mm = pe.matmul(ps[:, 0:w], xT[:, k, t * P:(t + 1) * P], wv[:, k, :], start=(k == 0), stop=(k == KT - 1))
                    mm.then_inc(S("bank_full"), 1)
                if kind0 == "proj2":
                    _, c, t = it
                    n = USE[it]
                    kind, _, w, _ = CHUNKS2[c]
                    j = JOB["w_in_2", c]
                    ps = use_bank(n)
                    if c == 0 and t == 0:
                        pe.wait_ge(S("turn_free"), TURN["norm", 0, 1, 1] + 1)
                    if t == 0:
                        job_ready(pe, j)
                    wv = view(j, "kiwi" if w == 72 else "k8")
                    if kind in ("xc", "cg", "bg"):
                        for q in range(2):
                            ct = 2 * t + q
                            for k in range(KT):
                                mm = pe.matmul(ps[:, q * TOK:(q + 1) * TOK], wv[:, k, ct * P:(ct + 1) * P], xT[:, k, :],
                                               start=(k == 0), stop=(k == KT - 1))
                    else:
                        for k in range(KT):
                            mm = pe.matmul(ps[:, 0:w], xT[:, k, t * P:(t + 1) * P], wv[:, k, :], start=(k == 0), stop=(k == KT - 1))
                    mm.then_inc(S("bank_full"), 1)
                if kind0 in ("branch", "out1", "out2"):
                    n = USE[it]
                    ps = use_bank(n)
                    if kind0 == "branch":
                        _, i, hf, t = it
                        j = JOB["w_branch", i]
                        if hf == 0 and t == 0:
                            job_ready(pe, j)
                            pe.wait_ge(S("turn_free"), TURN["turn_branch", i, 1] + 1)
                        wv, lhs, nk, cols = view(j, "k4"), OT, WK, slice(hf * CH, hf * CH + CH)
                    else:
                        _, hf, t = it
                        j = JOB["w_out" if kind0 == "out1" else "w_out_2", hf]
                        if t == 0:
                            job_ready(pe, j)
                        if hf == 0 and t == 0:
                            pe.wait_ge(S("turn_free"), (TURN["turn_merged", 1, 1] if kind0 == "out1"
                                                        else TURN["turn_branch", 3, 1]) + 1)
                        wv, lhs, nk, cols = view(j, "k8"), (xT if kind0 == "out1" else mixT), KT, slice(0, CH)
                    for k in range(nk):
                        mm = pe.matmul(ps[:, :], lhs[:, k, t * P:(t + 1) * P], wv[:, k, cols], start=(k == 0), stop=(k == nk - 1))
                    mm.then_inc(S("bank_full"), 1)
                if kind0 == "turn":
                    _, c, t = it
                    k = TURN[it]
                    m = NTH_NORM["proj", c, t]
                    bank_taken(pe, USE["proj", c, t])
                    turn_bank(k)
                    nb = 2 if CHUNKS[c][0] == "kv" else 4
                    for b in range(nb):
                        mm = pe.transpose(turn_b[:, b * P:(b + 1) * P], qn[:, m % 2, b * P:(b + 1) * P], ident)
                    mm.then_inc(S("turned"), 1)
                if kind0 == "turn_branch":
                    i = it[1]
                    pe.wait_ge(S("valued"), 2 * (8 * i + 8))
                    for t in range(NT):
                        turn_bank(TURN[it + (t,)])
                        for b in range(4):
                            src = O[:, i, t, b * P:(b + 1) * P] if i < 3 else O2[:, t, b * P:(b + 1) * P]
                            mm = pe.transpose(turn_b[:, b * P:(b + 1) * P], src, ident)
                        mm.then_inc(S("turned"), 1)
                if kind0 == "turn_merged":
                    bank_taken(pe, USE["branch", 2, 1, 0])
                    bank_taken(pe, USE["branch", 2, 1, 1])
                    for t in range(NT):
                        for q in range(2):
                            turn_bank(TURN[it + (t, q)])
                            for b in range(4):
                                k = 4 * q + b
                                mm = pe.transpose(turn_b[:, b * P:(b + 1) * P], G[:, t, k * P:(k + 1) * P], ident)
                            mm.then_inc(S("turned"), 1)
                if kind0 == "turn2":
                    pe.wait_ge(S("rows_ready"), NT)
                    for g in range(4):
                        for t in range(NT):
                            turn_bank(TURN[it + (g, t)])
                            for b in range(4 if g < 3 else 1):
                                r0 = 8 * g + 2 * b
                                mm = pe.transpose(turn_b[:, b * P:(b + 1) * P],
                                                  R[:, t, r0:r0 + 2, :].rearrange("p h d -> p (h d)"), ident)
                            mm.then_inc(S("turned"), 1)
                if kind0 == "ada_out":
                    c = it[1]
                    s, hf = c // 2, c % 2
                    pe.wait_ge(S("ada_summed"), c + 1)
                    turn_bank(TURN[it])
                    acc = ada_acc[:, c % 2, :]
                    if s in (2, 5):
                        mm = pe.matmul(turn_b[:, :], ones[:, :], acc, start=True, stop=True)
                    else:
                        for k in range(KT):
                            mm = pe.matmul(turn_b[HD * hf:HD * hf + HD, k:k + 1], acc[:, k:CH:KT], ones[:, 0:1],
                                           start=True, stop=True)
                    mm.then_inc(S("turned"), 1)
                if kind0 == "score":
                    n = it[1]
                    for g in range(len(units_of(n)) if n < 24 else 1):
                        u = UNIT[n, g]
                        if u >= 2:
                            pe.wait_ge(S("logits"), u - 1)
                        if n < 24:
                            qp, kp, half, _, _ = units_of(n)[g]
                            q, kk = qT[HD * half:HD * half + HD, qp, :], kT[HD * half:HD * half + HD, kp, :]
                            if n % 8 == 0 and g == 0:
                                c = {0: 1, 1: 9, 2: 15}[n // 8]
                                pe.wait_ge(S("turn_free"), TURN["turn", c, 1] + 1)
                        else:
                            h = n - 24
                            half = h % 2
                            q, kk = T2[HD * half:HD * half + HD, h // 2, :], T2[HD * half:HD * half + HD, 4 + h // 2, :]
                            if h == 0:
                                pe.wait_ge(S("relu_done"), 8)
                        ps = score_b[u % 2]
                        pe.matmul(ps[:, 0:P], q[:, 0:P], kk[:, 0:P], start=True, stop=True)
                        pe.matmul(ps[:, P:3 * P], q[:, P:2 * P], kk, start=True, stop=True).then_inc(S("scored"), 1)
                if kind0 == "index":
                    h = it[1]
                    half = h % 2
                    if h == 0:
                        pe.wait_ge(S("turn_free"), TURN["turn2", 3, 1] + 1)
                        pe.wait_ge(S("logits"), N_BIAS)
                    if h >= 2:
                        pe.wait_ge(S("relu_done"), h - 1)
                    q, kk = T2[HD * half:HD * half + HD, 8 + h // 2, :], T2[HD * half:HD * half + HD, 12, :]
                    ps = score_b[h % 2]
                    pe.matmul(ps[:, 0:P], q[:, 0:P], kk[:, 0:P], start=True, stop=True)
                    pe.matmul(ps[:, P:3 * P], q[:, P:2 * P], kk, start=True, stop=True).then_inc(S("index_product"), 1)
                if kind0 == "flip":
                    n = it[1]
                    i = HEADS.index(n)
                    for g in range(len(units_of(n)) if n < 24 else 1):
                        u = UNIT[n, g]
                        pe.wait_ge(S("probs"), 2 * i + 2)
                        if u >= 2:
                            pe.wait_ge(S("probsT"), u - 1)
                        for b, lo in enumerate((0, P + 1, 2 * P + 1)):
                            mm = pe.transpose(flip_b[u % 2][:, b * P:(b + 1) * P], L[:, i % 2, g, lo:lo + P], ident)
                        mm.then_inc(S("flipped"), 1)
                if kind0 == "value":
                    n = it[1]
                    i = HEADS.index(n)
                    ng = len(units_of(n)) if n < 24 else 1
                    pe.wait_ge(S("probsT"), UNIT[n, ng - 1] + 1)
                    if n in (0, 8, 16):
                        c = {0: 2, 8: 12, 16: 15}[n]
                        bank_taken(pe, USE["proj", c, 1])
                    if n == 0:
                        pe.wait_ge(S("rel_ready"), 1)
                    if n == 24:
                        bank_taken(pe, USE["proj2", 4, 1])
                    if i >= 1:
                        pe.wait_ge(S("valued"), 2 * i)
                    for t in range(NT):
                        o = value_b[:, 128 * (i % 2) + 64 * t:128 * (i % 2) + 64 * t + 64]
                        parts = [(g, kb) for g in range(ng) for kb in range(t + 1)]
                        for z, (g, kb) in enumerate(parts):
                            v = V[:, kb, units_of(n)[g][3]:units_of(n)[g][3] + HD] if n < 24 \
                                else V2[:, kb, HD * (n - 24):HD * (n - 24) + HD]
                            lo = 0 if t == 0 else P + P * kb
                            mm = pe.matmul(o, PT[:, i % 2, g, lo:lo + P], v, start=(z == 0), stop=(z == len(parts) - 1))
                        mm.then_inc(S("value_product"), 1)
                if kind0 == "router":
                    pe.wait_ge(S("turn_free"), TURN["norm", 1, 1, 1] + 1)
                    pe.wait_ge(S("late_loaded"), 16 * N_LATE)
                    for t in range(NT):
                        for k in range(KT):
                            mm = pe.matmul(turn_b[:, N_EXP * t:N_EXP * t + N_EXP], xT[:, k, t * P:(t + 1) * P], w_router[:, k, :],
                                           start=(k == 0), stop=(k == KT - 1))
                    mm.then_inc(S("router_product"), 1)

            def up(w1, w3, f):
                for m, w in enumerate((w1, w3)):
                    for k in range(KT):
                        mm = pe.matmul(up_b[f][:, m * TOK:(m + 1) * TOK], w[:, k, f:ED:FT], xT[:, k, :],
                                       start=(k == 0), stop=(k == KT - 1))
                mm.then_inc(S(f"up_{f}"), 1)

            def down(w2, f, first_of_all):
                for t in range(NT):
                    for hf in range(2):
                        mm = pe.matmul(acc_b[2 * t + hf][:, :], hT[:, f, t * P:(t + 1) * P], w2[:, f, hf * CH:hf * CH + CH],
                                       start=first_of_all, stop=False, skip_group_check=True)
                return mm

            j = JOB["shared_up",]
            job_ready(pe, j)
            pe.wait_ge(S("probsT"), len(UNITS))
            wv = view(j, "up")
            for f in range(FT):
                up(wv[:, 0], wv[:, 1], f)
            for n in (1, 2):
                bank_taken(pe, len(BANKED) - n)
            pe.wait_ge(S("logits"), len(UNITS))
            pe.wait_ge(S("taken_ready"), 2)
            pe.wait_ge(S("valued"), 64)
            tri = consts[:, C_TRI:C_TRI + P]
            pe.matmul(y_b[0][:, 0:NV], tri, taken[:, 0, :], start=True, stop=True)
            pe.matmul(y_b[0][:, NV:2 * NV], ones[:, :], taken[:, 0, :], start=True, stop=False)
            pe.matmul(y_b[0][:, NV:2 * NV], tri, taken[:, 1, :], start=False, stop=True)
            for t in range(NT):
                mm = pe.matmul(y_b[0][:, 2 * NV:2 * NV + 1], taken[:, t, :], ones[:, 0:1], start=(t == 0), stop=(t == 1))
            mm.then_inc(S("ranked"), 1)
            pe.wait_ge(S("used_ready"), 1)
            pe.wait_ge(S("router_exp"), 1)
            pe.matmul(y_b[1][:, 0:1], tri, used[:, :], start=True, stop=True).then_inc(S("places_counted"), 1)
            pe.wait_ge(S("ranks_ready"), NT)
            for t in range(NT):
                mm = pe.transpose(y_b[0][:, t * P:(t + 1) * P], ranks[:, t, :], ident)
            mm.then_inc(S("ranks_turned"), 1)
            pe.wait_ge(S("order_ready"), 1)
            pe.matmul(y_b[1][0:1, 0:NV], consts[:, C_EXP:C_EXP + 1], order[:, :], start=True, stop=True)
            pe.matmul(y_b[1][0:1, NV:2 * NV], consts[:, C_COL:C_COL + 1], order[:, :], start=True, stop=True)
            pe.matmul(y_b[1][0:1, 2 * NV:2 * NV + 1], used[:, :], ones[:, 0:1], start=True, stop=True)\
              .then_inc(S("list_product"), 1)
            pe.wait_ge(S("work_ready"), 2)
            for k in range(KT // 2):
                for t in range(NT):
                    if k >= 1:
                        pe.wait_ge(S("x_lo_ready"), 2 * (k - 1) + t + 1)
                    for b in range(2):
                        mm = pe.transpose(y_b[t][:, b * P:(b + 1) * P], xT[:, 2 * k + b, t * P:(t + 1) * P], ident)
                    mm.then_inc(S("h2_turned"), 1)
            j = JOB["shared_down",]
            job_ready(pe, j)
            for f in range(FT):
                pe.wait_ge(S(f"h_ready_{f}"), 1)
                mm = down(view(j, "down"), f, f == 0)
            mm.then_inc(S("shared_done"), 1)

            def gather(r, q):
                for b in range(4):
                    for z, part in enumerate((x_hi, x_lo)):
                        for t in range(NT):
                            mm = pe.matmul(up_b[q][:, b * P:(b + 1) * P], part[:, t, 4 * q + b, :], pick[:, r, t, :],
                                           start=(z == 0 and t == 0), stop=(z == 1 and t == 1))
                mm.then_inc(S(f"gathered_{q}"), 1)

            pe.wait_ge(S("x_lo_ready"), KT)
            pe.wait_ge(S("pick_ready"), 1)
            for q in range(2):
                gather(0, q)
            n_work = pe.value_load(work[0:1, 0:1], min_val=0, max_val=MAX_WORK)
            with pe.Fori(0, -(-MAX_WORK // ESLOTS)) as m:
                for r in range(ESLOTS):
                    i = m * ESLOTS + r
                    nxt = (r + 1) % ESLOTS
                    with pe.If(n_work > i):
                        w1 = ew[r][:, 0:2048].rearrange("p (k n) -> p k n", k=KT)
                        w3 = ew[r][:, 2048:4096].rearrange("p (k n) -> p k n", k=KT)
                        w2 = ew[r][:, 4096:6144].rearrange("p (f n) -> p f n", f=FT)
                        pe.wait_ge(S("block_ready_0"), i + 1)
                        for t in range(NT):
                            pe.matmul(up_b[0][:, 2 * P:2 * P + 1], pick[:, r, t, :].bitcast(F32),
                                      col3[:, r, NT + t:NT + t + 1], start=(t == 0), stop=(t == 1))
                        pe.wait_ge(S(f"up_loaded_{r}"), 32 * (m + 1))
                        pe.wait_ge(S("block_ready_1"), i + 1)
                        for f in range(FT):
                            for b, w in enumerate((w1, w3)):
                                for k in range(KT):
                                    mm = pe.matmul(up_b[f][:, b * P:(b + 1) * P], w[:, k, f:ED:FT], xe[:, k, :],
                                                   start=(k == 0), stop=(k == KT - 1))
                            mm.then_inc(S(f"up_{f}"), 1)
                        pe.wait_ge(S("pick_ready"), i + 2)
                        pe.wait_ge(S("h_ready_0"), i + 2)
                        pe.wait_ge(S("gates_gathered"), i + 1)
                        gather(nxt, 0)
                        pe.wait_ge(S(f"down_loaded_{r}"), 16 * (m + 1))
                        pe.wait_ge(S("h_ready_1"), i + 2)
                        for hf in range(2):
                            for f in range(FT):
                                mm = pe.matmul(y_b[hf][:, :], hT[:, f, 0:P], w2[:, f, hf * CH:hf * CH + CH],
                                               start=(f == 0), stop=(f == FT - 1))
                            mm.then_inc(S(f"down_{hf}"), 1)
                        gather(nxt, 1)
                        pe.wait_ge(S("put_ready"), i + 1)
                        for hf in range(2):
                            pe.wait_ge(S(f"y_lo_{hf}"), i + 1)
                            for t in range(NT):
                                for part in (y_hi, y_lo):
                                    mm = pe.matmul(acc_b[2 * t + hf][:, :], put[:, r, t * P:(t + 1) * P],
                                                   part[:, hf * CH:hf * CH + CH], start=False, stop=False,
                                                   skip_group_check=True)
                        mm.then_inc(S("block_done"), 1)
            pe.matmul(y_b[0][0:1, 0:1], ones[:, 0:1], ones[:, 0:1], start=True, stop=True).then_inc(S("experts_summed"), 1)


def rel_bucket(dist):
    dist = np.maximum(dist, 0)
    ratio = (np.log(np.maximum(dist, 1).astype(np.float32) / np.float32(16)) / np.float32(math.log(2048 / 16)))
    large = np.minimum(16 + (ratio * np.float32(16)).astype(np.int32), 31)
    return np.where(dist < 16, dist, large)


def shape_constants():
    sq = np.zeros((P, C_N), np.float32)
    p = np.arange(P)[:, None]
    sq[:, C_ID:C_ID + P] = np.eye(P)
    sq[:, C_CAUS:C_CAUS + 2 * P] = np.where(P + p - np.arange(2 * P)[None, :] >= 0, 0.0, NEG)
    sq[:, C_FREQ:C_FREQ + 8] = (np.float32(500000.0) ** (-np.arange(8, dtype=np.float32) / np.float32(8)))[None, :]
    sq[:, C_TRI:C_TRI + P] = p < np.arange(P)[None, :]
    sq[:, C_IOTA:C_IOTA + P] = np.arange(P)[None, :]
    sq[:, C_THR_ROW:C_THR_ROW + NV] = P * (np.arange(NV)[None, :] // N_EXP) - FAR
    sq[:, C_COL] = np.arange(P)
    sq[:, C_EXP] = np.arange(P) % N_EXP
    sq[:, C_THR] = P * (np.arange(P) // N_EXP)
    dist = np.arange(NREL_PAD) - 127
    hot = (np.arange(32)[:, None] == rel_bucket(dist)[None, :]).astype(np.float32)
    mask = np.zeros((40, NREL_PAD), np.float32)
    for row in range(40):
        ok = dist >= 0
        if 8 <= row < 32:
            w, d = ((128, 1), (512, 4), (2048, 16))[(row - 8) // 8]
            ok = ok & (dist <= w) & (dist % d == 0)
        if row >= 32:
            ok = ok & (dist < 128)
        mask[row] = np.where(ok, 0.0, NEG)
    return {"c_square": sq, "c_hot": hot, "c_mask": mask}


_INS = ["x", "ln_g", "w_in", "qk_g", "sinks", "w_branch", "w_out", "rel_bias", "c_2", "positions_2", "norm1_g_2",
        "norm2_g_2", "w_ada_2", "b_ada_2", "w_in_2", "conv_w_2", "q_norm_g_2", "k_norm_g_2", "kidx_norm_g_2",
        "w_out_2", "w_router_2", "router_bias_2", "w1_2", "w3_2", "w2_2", "ws1_2", "ws3_2", "ws2_2"]


def kernel(**inputs):
    import concourse.bacc as _bacc
    from concourse.bass_utils import run_bass_kernel_spmd as _run

    nc = _bacc.Bacc("TRN2", target_bir_lowering=False, num_devices=1)
    arrays, args = {}, {}
    given = {name: inputs[name] for name in _INS}
    given.update(shape_constants())
    for name, value in given.items():
        v = np.ascontiguousarray(value)
        arrays[f"in_{name}_dram"] = v
        args[name] = nc.dram_tensor(f"in_{name}_dram", v.shape, mybir.dt.from_np(v.dtype), kind="ExternalInput").ap()
    out = nc.dram_tensor("out_0_dram", (1, TOK, DM), F32, kind="ExternalOutput").ap()
    build(nc, args, out)
    r = _run(nc, [arrays], core_ids=[0])
    return r.results[0]["out_0_dram"]
```

```python
import math

import numpy as np
import concourse.bass as bass
from concourse import mybir
from contextlib import ExitStack

F32 = mybir.dt.float32
F32R = mybir.dt.float32r
I32 = mybir.dt.int32
ALU = mybir.AluOpType
ACT = mybir.ActivationFunctionType
AX = mybir.AxisListType

P = 128
TOK = 256
NT = TOK // P
DM = 1024
KT = DM // P
HD = 64
W_BR = 512
WK = W_BR // P
EPS = 1e-6
NEG = -1e30
TAKEN = -3e38
N_EXP = 64
ED = 256
FT = ED // P
TOP_KEYS = 64
TOPK_STEPS = 1 + 2 * TOP_KEYS // 8 + 2
SCALE = HD ** -0.5
IDX_SCALE = (64 ** -0.5) * (8 ** -0.5)
ROUTED = 2.5
NREL = 383
NREL_PAD = 384
CH = 512
N_ADA = 6 * DM // CH

C_ID, C_CAUS, C_FREQ, C_TRI, C_IOTA, C_THR_ROW = 0, 128, 384, 392, 520, 648
C_COL, C_EXP, C_THR, C_N = 776, 777, 778, 779
FAR = 1000.0

CHUNKS = (
    [("q", 0, 512, 0), ("k", 512, 512, 0), ("v", 1024, 512, 0), ("silu", 1536, 512, 0)]
    + [("q", 2048 + 512 * g, 512, 4 + 4 * g) for g in range(3)]
    + [("k", 3584 + 512 * g, 512, 4 + 4 * g) for g in range(3)]
    + [("v", 5120 + 512 * g, 512, 512 + 512 * g) for g in range(3)]
    + [("silu", 6656, 512, 1)]
    + [("q", 7168, 512, 16), ("kv", 7680, 256, 16), ("silu", 7936, 512, 2)]
    + [("gate", 8448 + 512 * g, 512, 512 * g) for g in range(6)]
)
CHUNKS2 = [("qi", 3072, 512, 16), ("kiwi", 3584, 72, 24), ("q2", 1536, 512, 0), ("k2", 2048, 512, 8),
           ("v2", 2560, 512, 0), ("xc", 0, 512, 0), ("cg", 1024, 512, 0), ("bg", 512, 512, 0)]
N_QP, N_KP = 20, 18
V_COLS = 512 + 1536 + 128


def units_of(n):
    b, h = n // 8, n % 8
    if b == 0:
        return [(h // 2, h // 2, h % 2, 64 * h, h)]
    if b == 1:
        return [(4 + 4 * g + h // 2, 4 + 4 * g + h // 2, h % 2, 512 + 512 * g + 64 * h, 8 + 8 * g + h)
                for g in range(3)]
    return [(16 + h // 2, 16 + h // 4, h % 2, 2048 + 64 * (h // 4), 32 + h)]


FILL = [3] * 4 + [2] * 4 + [2, 1, 2] + [2, 2, 2, 1, 1] + [0, 2, 1, 1, 1, 1, 1, 0]
SUMS = {n: 4 for n in range(1, 11)} | {16: 8}
FILL2 = [1, 1, 1, 1, 0, 0, 0, 0]
SPLIT_OF = {"proj": "w_in", "out1": "w_out", "proj2": "w_in_2", "out2": "w_out_2"}
PIECES = KT // 2


def fill_groups():
    groups, pending = [], None
    chunks = [2, 3, 0, 1] + [c for c, ch in enumerate(CHUNKS) if c > 3 and ch[0] != "gate"]
    for c in chunks:
        for t in range(NT):
            groups.append([("proj", c, t)] + ([pending] if pending else []))
            pending = ("turn", c, t) if CHUNKS[c][0] in ("q", "k", "kv") else None
    for i in range(3):
        for hf in range(2):
            for t in range(NT):
                groups.append([("proj", len(chunks) + 2 * i + hf, t)])
            for t in range(NT):
                groups.append([("branch", i, hf, t)])
    return groups


def with_splits(steps):
    jobs = []
    for it in steps:
        if it[0] in SPLIT_OF and (SPLIT_OF[it[0]], it[1]) not in jobs:
            jobs.append((SPLIT_OF[it[0]], it[1]))
    s = []
    for it in steps:
        s.append(it)
        if it[0] == "start":
            s += [("split",) + jobs[0] + (p,) for p in range(PIECES)]
        if it == ("norm", 0):
            s += held
        if it[0] not in SPLIT_OF and it[0] != "branch":
            continue
        nxt = None
        last_gate = it[0] == "proj" and CHUNKS[it[1]][0] == "gate" and CHUNKS[it[1]][3] % (2 * CH) == CH
        if (it[0] in SPLIT_OF and it[-1] == NT - 1 and not last_gate) or (it[0] == "branch" and it[2:] == (1, 1)):
            job = ("w_in", len(CHUNKS) - 5 + 2 * it[1]) if it[0] == "branch" else (SPLIT_OF[it[0]], it[1])
            at = jobs.index(job)
            nxt = jobs[at + 1] if at + 1 < len(jobs) else None
        ahead = PIECES // 2 if it == ("out1", 1, 1) else PIECES
        if nxt:
            s += [("split",) + nxt + (p,) for p in range(ahead)]
        s.append(("drain",) + it)
        if nxt and ahead < PIECES:
            held = [("split",) + nxt + (p,) for p in range(ahead, PIECES)]
    return s


def make_schedule():
    s = [("start",)]
    groups = fill_groups()

    def take(k):
        for _ in range(k):
            if groups:
                s.extend(groups.pop(0))

    take(4)
    s.append(("small",))
    ada = [("ada", c, part) for c in range(N_ADA) for part in range(KT // 2)]

    def modulation(k):
        for _ in range(k):
            if ada:
                _, c, part = ada.pop(0)
                s.append(("ada", c, part))
                if part == 2 and c:
                    s.append(("ada_out", c - 1))

    take(5)

    def head(n, k, m=0):
        s.append(("score", n))
        take(1 if k > 0 else 0)
        modulation(m - m // 2)
        s.append(("score_rest", n))
        if n % 24 >= 2:
            s.append(("value", n - 2))
        take(1 if k > 1 else 0)
        modulation(m // 2)
        if n % 24:
            s.append(("flip", n - 1))
        if n in (9, 17):
            s.append(("turn_branch", n // 8 - 1))
        take(k - 2)

    for n in range(24):
        head(n, FILL[n], SUMS.get(n, 0))
        if n == 17:
            s.append(("ada_out", N_ADA - 1))
    assert not ada
    s += [("flip", 23), ("value", 22)]
    take(2)
    s += [("value", 23), ("turn_branch", 2)]
    take(99)
    s.append(("turn_merged",))
    s.extend(("out1", hf, t) for hf in range(2) for t in range(NT))
    s.append(("norm", 0))
    for c in range(4):
        s.extend(("proj2", c, t) for t in range(NT))
        if c == 1:
            s.append(("angles",))
    s.append(("rope",))
    groups = [[("proj2", c, t)] for c in range(4, 8) for t in range(NT)]
    take(2)
    s.append(("turn2",))
    s.extend(("index", h) for h in range(8))
    s.append(("topk", 0))
    take(1)
    s.append(("topk", 1))
    take(1)
    for h in range(8):
        head(24 + h, FILL2[h])
    s.append(("mix_conv",))
    s += [("flip", 31), ("value", 30), ("value", 31), ("turn_branch", 3)]
    s.extend(("out2", hf, t) for hf in range(2) for t in range(NT))
    s.append(("norm", 1))
    s.append(("router",))
    return with_splits(s)


SCHEDULE = make_schedule()

RING = 2
JOBS, JOB = [], {}
LAST_STEP, FIRST_AT, LAST_AT = {}, {}, {}


def weights_used(it):
    if it[0] == "split":
        return it[1], it[2]
    return {"ada": ("w_ada", it[1]), "branch": ("w_branch", it[1])}[it[0]] if it[0] in ("ada", "branch") else None


for _at, _it in enumerate(SCHEDULE):
    _key = weights_used(_it)
    if _key:
        if _key not in JOB:
            JOB[_key] = len(JOBS)
            FIRST_AT[len(JOBS)] = _at
            JOBS.append(_key)
        LAST_STEP[JOB[_key]] = _it
        LAST_AT[JOB[_key]] = _at
for _j in FIRST_AT:
    assert _j < RING or FIRST_AT[_j] > LAST_AT[_j - RING], (JOBS[_j], JOBS[_j - RING])
SPLITS = [k for k in JOBS if k[0] not in ("w_ada", "w_branch")]
for _key in (("shared_up",), ("shared_down",)):
    JOB[_key] = len(JOBS)
    JOBS.append(_key)

RING_OFFSET = (RING - 1 - JOB["shared_up",]) % RING

BANKED = [it for it in SCHEDULE if it[0] in SPLIT_OF or it[0] == "branch"]
RESULTS = [it[1:] if it[0] == "drain" else it for it in SCHEDULE if it[0] not in SPLIT_OF and it[0] != "branch"]
USE = {it: n for n, it in enumerate(BANKED)}
HEADS = [it[1] for it in SCHEDULE if it[0] == "score"]
UNITS = [(n, g) for n in HEADS for g in range(len(units_of(n)) if n < 24 else 1)]
UNIT = {ng: u for u, ng in enumerate(UNITS)}
N_BIAS = sum(n < 24 for n, _ in UNITS)
BIAS_SLOTS = 5
LAST_USE = {(SPLIT_OF[it[0]], it[1]): n for n, it in enumerate(BANKED) if it[0] in SPLIT_OF}
TURNS = []
for _it in SCHEDULE:
    if _it[0] == "turn":
        TURNS.append(_it)
    if _it[0] == "turn_branch":
        TURNS += [_it + (t,) for t in range(NT)]
    if _it[0] in ("turn_merged", "norm", "start"):
        TURNS += [_it + (t, q) for t in range(NT) for q in range(2)]
    if _it[0] == "ada_out":
        TURNS.append(_it)
    if _it[0] == "turn2":
        TURNS += [_it + (g, t) for g in range(4) for t in range(NT)]
TURN = {it: n for n, it in enumerate(TURNS)}
NORMED = [it for it in BANKED if (it[0] == "proj" and CHUNKS[it[1]][0] in ("q", "k", "kv"))
          or (it[0] == "proj2" and CHUNKS2[it[1]][0] in ("q2", "k2", "kiwi"))]
NTH_NORM = {it: n for n, it in enumerate(NORMED)}
GATED = [it for it in BANKED if it[0] == "proj" and CHUNKS[it[1]][0] == "silu"]
NTH_GATE = {it: n for n, it in enumerate(GATED)}
SIGMOIDS = [it for it in BANKED if it[0] == "proj" and CHUNKS[it[1]][0] == "gate"]
BRANCHED = [it for it in BANKED if it[0] == "branch"]
BODY = 4
UP, DOWN = 2 * KT * ED, FT * DM
N_SMALL = 15
N_LATE = 6
NV = 2 * N_EXP
MAX_WORK = N_EXP + TOK * 8 // (P + 1)


def build(nc, a, out):
    ctx = ExitStack()
    with ctx:
        def sb(name, shape, dt=F32, stack=ctx):
            return stack.enter_context(nc.sbuf_tensor(name, shape, dt))

        sems = {}

        def S(name):
            if name not in sems:
                sems[name] = ctx.enter_context(nc.semaphore(name))
            return sems[name]

        ctx.enter_context(nc.allow_non_contiguous_dma(reason="small vectors onto partitions"))
        rel_dram = nc.dram_tensor("rel_rows", (40, NREL_PAD), F32, kind="Internal").ap()
        place_rows = nc.dram_tensor("place_rows", (NV, TOK), F32, kind="Internal").ap()
        place_cols = nc.dram_tensor("place_cols", (P, NV, 2 * NT), F32, kind="Internal").ap()

        consts = sb("consts", [P, C_N])
        ident = consts[:, C_ID:C_ID + P]
        ones = sb("ones", [P, P])
        ln_g = sb("ln_g_cols", [P, 3, KT])
        qk_g = sb("qk_g_cols", [P, 6])
        q_scale = sb("q_scale", [P, 3])
        g2 = sb("g2", [P, 3, HD])
        half_neg = sb("half_neg", [P, 8])
        c_col = sb("c_col", [P, 3, KT])
        b_ada = sb("b_ada_cols", [P, 6, KT])
        gate_bc = sb("gate_bc", [P, 2, DM])
        mod = sb("mod_cols", [P, 4, KT])
        msum = sb("mean_squares", [P, 8])
        rstd = sb("rstd", [P, 8])
        nmax = sb("neg_max", [P, 2, 2])
        den = sb("den", [P, 2, 2])
        rden = sb("rden", [P, 2, 2])
        qn = sb("qn", [P, 2, CH])

        attention = ExitStack()
        ring = sb("ring", [P, RING, 4096], F32, attention)
        w_parts = [sb(f"w_{z}", [P, KT, CH], F32R, attention) for z in ("hi", "lo")]
        a_parts = [sb(f"a_{z}", [P, KT, TOK], F32R, attention) for z in ("hi", "lo")]
        ada_acc = sb("ada_acc", [P, 2, CH], F32, attention)
        sq = sb("squares", [P, CH], F32, attention)
        L = sb("logits", [P, 2, 3, 386], F32, attention)
        PT = sb("probsT", [P, 2, 3, 384], F32, attention)
        xn = PT[:, :, :, :].rearrange("p a g n -> p (a g n)")[:, 0:DM]
        spare = L[:, :, :, :].rearrange("p a g n -> p (a g n)")
        hot, relmask, relrow = spare[0:32, 0:384], spare[0:40, 384:768], spare[0:40, 768:1152]
        turned_x = [spare[:, 1152 + CH * r:1152 + CH * (r + 1)] for r in range(2)]

        first = ExitStack()
        qT = sb("qT", [P, N_QP, TOK], F32, first)
        tabT = sb("tabT", [32, 40], F32, first)
        bias = sb("bias", [P, BIAS_SLOTS, 256], F32, first)
        kT = sb("kT", [P, N_KP, TOK], F32, first)
        V = sb("V", [P, NT, V_COLS], F32, first)
        O = sb("O", [P, 2, NT, W_BR], F32, first)
        OT = sb("OT", [P, WK, TOK], F32, first)
        G = sb("merged", [P, NT, DM], F32, first)
        egate = sb("silu_gate", [P, CH], F32, first)
        gates = sb("branch_gates", [P, 2, CH], F32, first)
        sinks = sb("sinks", [P, 8], F32, first)
        first.close()
        attention.close()

        operands = ExitStack()
        raw = sb("raw_weights", [P, 2, UP + DOWN], F32, operands)
        early = ExitStack()
        xT = sb("xT", [P, KT, TOK], F32, early)
        early.close()
        y_hi = sb("y_hi", [P, DM], F32R, operands)
        y_lo = sb("y_lo", [P, DM], F32R, operands)
        x_hi = sb("x_hi", [P, NT, KT, P], F32R, operands)
        x_lo = sb("x_lo", [P, NT, KT, P], F32R, operands)
        hs = sb("hs", [P, FT, TOK], F32, operands)
        hT = sb("hT", [P, FT, TOK], F32, operands)
        row4 = sb("block_rows", [P, BODY, TOK], F32, operands)
        col4 = sb("block_cols", [P, BODY, 2 * NT], F32, operands)
        down_lo = sb("down_lo", [P, FT, DM], F32R, operands)
        xe_hi = sb("x_block_hi", [P, KT, P], F32R, operands)
        xe_lo = sb("x_block_lo", [P, KT, P], F32R, operands)
        pick = sb("pick", [P, 2, NT, P], F32R, operands)
        put = sb("put", [P, 2, TOK], F32R, operands)
        sb("operands_end", [P, 1152], F32, operands)

        second = ExitStack()
        work = sb("work", [1, 1 + 2 * NV], I32, second)
        x = sb("x", [P, NT, DM], F32, second)

        routing = ExitStack()
        w_router = sb("w_router", [P, KT, N_EXP], F32, routing)
        rbias = sb("router_bias", [P, N_EXP], F32, routing)
        rarg = sb("rarg", [P, 2, NT, N_EXP], F32, routing)
        rexp = sb("rexp", [P, 2, NT, N_EXP], F32, routing)
        sig = sb("sig", [P, NT, N_EXP], F32, routing)
        sel = sb("sel", [P, NT, N_EXP], F32, routing)
        taken = sb("taken", [P, NT, NV], F32, routing)
        ranks = sb("ranks", [P, NT, NV], F32, routing)
        pcol = sb("pcol", [P, NV, 2 * NT], F32, routing)
        prow = sb("prow", [NV, TOK], F32, routing)
        gsum = sb("gsum", [P, NT], F32, routing)
        used = sb("used", [NV, 1], F32, routing)
        place = sb("place", [NV, 1], F32, routing)
        order = sb("order", [NV, NV], F32, routing)
        top8 = sb("top8", [P, 2, 8], F32, routing)

        mixer = ExitStack()
        pos_i = sb("pos_i", [P, NT], I32, mixer)
        conv_w = sb("conv_w_cols", [P, 3, WK], F32, mixer)
        pos = sb("pos", [P, NT], F32, mixer)
        ang = sb("ang", [P, NT, 2, 8], F32, mixer)
        turns_f = sb("turns_f", [P, NT, 2, 8], F32, mixer)
        turns_i = sb("turns_i", [P, NT, 2, 8], I32, mixer)
        wrap = sb("wrap", [P, NT, 2, 8], F32, mixer)
        trig = sb("trig", [P, NT, 2, 8], F32, mixer)
        R = sb("rows2", [P, NT, 26, HD], F32, mixer)
        rt = sb("rope_tmp", [P, 4, 25, 8], F32, mixer)
        wi = sb("wi", [P, NT, 8], F32, mixer)
        V2 = sb("V2", [P, NT, CH], F32, mixer)
        T2 = sb("T2", [P, 13, TOK], F32, mixer)
        relu = sb("relu", [P, 2, 384], F32, mixer)
        score = sb("score", [P, 384], F32, mixer)
        selmask = sb("selmask", [P, 384], F32, mixer)
        xcT = sb("xcT", [P, WK, TOK], F32, mixer)
        uT = sb("uT", [P, WK, TOK + 2], F32, mixer)
        cv = sb("cv", [P, TOK], F32, mixer)
        O2 = sb("O2", [P, NT, W_BR], F32, mixer)
        convT = sb("convT", [P, WK, TOK], F32, mixer)
        mixer.close()

        routing.close()

        moe = ExitStack()
        down_hi = sb("down_hi", [P, FT, DM], F32R, moe)
        h_hi = sb("h_hi", [P, FT, P], F32R, moe)
        h_lo = sb("h_lo", [P, FT, P], F32R, moe)
        gcol = sb("block_gates", [P, 1], F32, moe)
        sb("routing_end", [P, 224], F32, moe)
        he = hT[:, 0, :]
        up_hi = sb("up_hi", [P, 2, KT, 2, ED], F32R, moe)
        up_lo = sb("up_lo", [P, 2, KT, 2, ED], F32R, moe)
        moe.close()
        second.close()
        operands.close()
        raw_flat = raw[:, :, :].rearrange("p r n -> p (r n)")

        bank = [ctx.enter_context(nc.psum_tensor(f"bank{i}", [P, 512], F32)) for i in range(8)]
        proj_b, score_b, flip_b, value_b, turn_b = bank[0:2], bank[2:4], bank[4:6], bank[6], bank[7]
        wide_b = [turn_b, score_b[0]]
        acc_b, up_b, y_b = bank[0:4], bank[4:6], bank[6:8]
        hidden_b, turned_b = bank[4], bank[5]
        gather_b = [y_b[0], y_b[1], hidden_b, turned_b]

        block = ctx.enter_context(nc.Block())

        def view(j, kind):
            if kind == "down":
                return raw_flat[:, RING * 4096:RING * 4096 + DOWN].rearrange("p (f n) -> p f n", f=FT)
            slot = ring[:, (j + RING_OFFSET) % RING, :]
            if kind == "k8":
                return slot.rearrange("p (k n) -> p k n", k=KT)
            if kind == "k4":
                return slot.rearrange("p (k n) -> p k n", k=WK)
            if kind == "kiwi":
                return slot[:, 0:KT * 72].rearrange("p (k n) -> p k n", k=KT)
            if kind == "kv":
                return slot[:, 0:KT * 256].rearrange("p (k n) -> p k n", k=KT)
            assert kind == "up"
            return slot.rearrange("p (m k n) -> p m k n", m=2, k=KT)

        def split_kind(name, arg):
            w = {"w_in": CHUNKS, "w_in_2": CHUNKS2}[name][arg][2] if name in ("w_in", "w_in_2") else CH
            return {CH: "k8", 256: "kv", 72: "kiwi"}[w], w

        def raw_up(buf, kh, m):
            return buf[:, UP // 2 * m:UP // 2 * (m + 1)].rearrange("p (k n) -> p k n", k=KT)[:, 4 * kh:4 * kh + 4, :]

        def bank_taken(eng, n):
            eng.wait_ge(S(f"bank_free_{n % 2}"), n // 2 + 1)

        def job_ready(eng, j):
            eng.wait_ge(S(f"ring_loaded_{j % RING}"), 16 * (2 if JOBS[j][0] == "shared_up" else 1)
                        + 16 * sum(1 for i in range(j % RING, j, RING)))

        @block.sync
        def _(sp):
            d_rows = "(p k) n -> p k n"

            def load(j):
                kind, arg = JOBS[j][0], JOBS[j][1:]
                done = S(f"ring_loaded_{j % RING}")
                if j >= RING:
                    if kind == "shared_down":
                        sp.wait_ge(S("bank_full"), len(BANKED))
                    last = LAST_STEP.get(j - RING, ("none",))
                    if last[0] == "ada":
                        sp.wait_ge(S("ada_summed"), last[1] + 1)
                    elif last[0] == "branch":
                        sp.wait_ge(S("bank_full"), USE[last] + 1)
                    elif last[0] == "split":
                        sp.wait_ge(S("w_lo"), PIECES * (SPLITS.index(last[1:3]) + 1))
                if kind == "w_in":
                    _, c0, w, _ = CHUNKS[arg[0]]
                    src = a["w_in"][0].rearrange(d_rows, k=KT)[:, :, c0:c0 + w]
                    sp.dma_start(view(j, "kv" if w == 256 else "k8"), src).then_inc(done, 16)
                elif kind == "w_in_2":
                    _, c0, w, _ = CHUNKS2[arg[0]]
                    src = a["w_in_2"][0].rearrange(d_rows, k=KT)[:, :, c0:c0 + w]
                    sp.dma_start(view(j, "kiwi" if w == 72 else "k8"), src).then_inc(done, 16)
                elif kind == "w_ada":
                    src = a["w_ada_2"][0].rearrange(d_rows, k=KT)[:, :, CH * arg[0]:CH * arg[0] + CH]
                    sp.dma_start(view(j, "k8"), src).then_inc(done, 16)
                elif kind == "w_branch":
                    src = a["w_branch"][0, arg[0]].rearrange("(k p) n -> p k n", p=P)
                    sp.dma_start(view(j, "k4"), src).then_inc(done, 16)
                elif kind == "w_out":
                    src = a["w_out"][0].rearrange("(k p) n -> p k n", p=P)[:, :, CH * arg[0]:CH * arg[0] + CH]
                    sp.dma_start(view(j, "k8"), src).then_inc(done, 16)
                elif kind == "w_out_2":
                    src = a["w_out_2"][0].rearrange("(k p) n -> p k n", p=P)[:, :, CH * arg[0]:CH * arg[0] + CH]
                    sp.dma_start(view(j, "k8"), src).then_inc(done, 16)
                elif kind == "shared_up":
                    for m, name in enumerate(("ws1_2", "ws3_2")):
                        sp.dma_start(view(j, "up")[:, m], a[name][0].rearrange(d_rows, k=KT)).then_inc(done, 16)
                else:
                    sp.dma_start(view(j, "down"), a["ws2_2"][0].rearrange("(p f) n -> p f n", f=FT))\
                      .then_inc(done, 16)

            at = 0
            for it in SCHEDULE:
                if it[0] == "start":
                    for t in range(NT):
                        sp.dma_start(G[:, t, :], a["x"][0, t * P:(t + 1) * P, :]).then_inc(S(f"x_loaded_{t}"), 16)
                if it == ("out1", 0, 0):
                    sp.wait_ge(S("scored"), N_BIAS)
                    for t in range(NT):
                        sp.dma_start(x[:, t, :], a["x"][0, t * P:(t + 1) * P, :]).then_inc(S(f"x_loaded_{t}"), 16)
                if it[0] == "score" and it[1] < 24:
                    for g, (_, _, _, _, row) in enumerate(units_of(it[1])):
                        u = UNIT[it[1], g]
                        if u == 0:
                            sp.wait_ge(S("rel_ready"), 1)
                            sp.dma_start(rel_dram, relrow).then_inc(S("rel_stored"), 16)
                            sp.wait_ge(S("rel_stored"), 16)
                        if u >= BIAS_SLOTS:
                            sp.wait_ge(S("logits"), u - BIAS_SLOTS + 1)
                        src = bass.AP(rel_dram.tensor, row * NREL_PAD, [[1, P], [1, 2 * P]])
                        sp.dma_start(bias[:, u % BIAS_SLOTS, :], src).then_inc(S(f"bias_loaded_{u % BIAS_SLOTS}"), 16)
                if weights_used(it) == JOBS[at]:
                    load(at)
                    at += 1
            for j in range(at, len(JOBS)):
                load(j)

            sp.wait_ge(S("rows_turned"), 1)
            sp.dma_start(place_rows, prow[:, :]).then_inc(S("places_stored"), 16)
            sp.dma_start(place_cols, pcol[:, :, :]).then_inc(S("places_stored"), 16)
            sp.wait_ge(S("places_stored"), 32)
            sp.wait_ge(S("work_ready"), 2)
            n_work = sp.value_load(work[0:1, 0:1], min_val=0, max_val=MAX_WORK)

            def load_entry(i, r):
                v = sp.value_load(work[0:1, bass.ds(i + 1 + NV, 1)], min_val=0, max_val=NV - 1)
                done = S(f"places_loaded_{r}")
                sp.dma_start(col4[:, r, :].unsqueeze(1), place_cols[:, bass.ds(v, 1), :]).then_inc(done, 16)
                sp.dma_start(row4[:, r, :], place_rows[bass.ds(v, 1), :].to_broadcast([P, TOK])).then_inc(done, 16)
                e = sp.value_load(work[0:1, bass.ds(i + 1, 1)], min_val=0, max_val=N_EXP - 1)
                for m, name in enumerate(("w1_2", "w3_2")):
                    src = a[name][0].rearrange("e (p k) n -> p e (k n)", k=KT)[:, bass.ds(e, 1), :]
                    sp.dma_start(raw[:, r % 2][:, UP // 2 * m:UP // 2 * (m + 1)].unsqueeze(1), src)\
                      .then_inc(S(f"up_loaded_{r}"), 16)
                src = a["w2_2"][0].rearrange("e (p f) n -> p e (f n)", f=FT)[:, bass.ds(e, 1), :]
                sp.dma_start(raw[:, r % 2][:, UP:].unsqueeze(1), src).then_inc(S(f"down_loaded_{r}"), 16)

            for r in range(BODY):
                if r == 1:
                    sp.wait_ge(S("block_done"), 1)
                with sp.If(n_work > r - 1):
                    if r >= 2:
                        sp.wait_ge(S("down_lo"), 2 * (r - 1))
                    load_entry(r, r)
            with sp.Fori(1, -(-(MAX_WORK + 1) // BODY)) as m:
                for r in range(BODY):
                    i = m * BODY + r
                    with sp.If(n_work > i - 1):
                        sp.wait_ge(S("down_lo"), 2 * i - 2)
                        load_entry(i, r)
            for t in range(NT):
                sp.wait_ge(S("out_ready"), 2 * t + 2)
                sp.dma_start(out[0, t * P:(t + 1) * P, :], x[:, t, :]).then_inc(S("out_stored"), 16)
            sp.wait_ge(S("out_stored"), 16 * NT)

        @block.gpsimd
        def _(gp):
            gp.memset(half_neg[:, :], -0.5).then_inc(S("half_neg_set"), 1)
            gp.memset(ones[:, :], 1.0).then_inc(S("ones_set"), 1)
            gp.wait_ge(S("half_neg_set"), 1)

            def inverse_root(width, count, ready, nth, done):
                gp.wait_ge(S(ready), nth)
                gp.tensor_scalar(msum[:, 0:width], msum[:, 0:width], 1.0 / count, EPS, ALU.mult, ALU.add)\
                  .then_inc(S("mean_eps"), 1)
                inverse_root.n += 1
                gp.wait_ge(S("mean_eps"), inverse_root.n)
                gp.tensor_tensor(rstd[:, 0:width], msum[:, 0:width], half_neg[:, 0:width], ALU.pow)\
                  .then_inc(S(done), 1)
            inverse_root.n = 0
            nx = 0
            for it in RESULTS:
                if it[0] in ("start", "norm"):
                    for t in range(NT):
                        nx += 1
                        inverse_root(1, DM, "x_squared", nx, "x_rstd")
                if it[0] == "start":
                    small = S("small_loaded")
                    gp.dma_start(hot, a["c_hot"]).then_inc(small, 16)
                    gp.dma_start(relmask, a["c_mask"]).then_inc(small, 16)
                    gp.dma_start(tabT[:, :], a["rel_bias"].rearrange("h b -> b h")).then_inc(small, 16)
                    for i, name in ((1, "norm1_g_2"), (2, "norm2_g_2")):
                        gp.dma_start(ln_g[:, i, :], a[name][0].rearrange("(p k) -> p k", k=KT)).then_inc(small, 16)
                    gp.dma_start(c_col[:, 0, :], a["c_2"][0].rearrange("(p k) -> p k", k=KT)).then_inc(small, 16)
                    gp.dma_start(b_ada[:, :, :], a["b_ada_2"][0].rearrange("(s p k) -> p s k", s=6, k=KT)).then_inc(small, 16)
                    for h in range(2):
                        gp.dma_start(qk_g[HD * h:HD * h + HD, :], a["qk_g"][0].rearrange("g d -> d g")).then_inc(small, 16)
                    gp.dma_start(sinks[:, :], a["sinks"].to_broadcast([P, 8])).then_inc(small, 16)
                    for i, name in enumerate(("q_norm_g_2", "k_norm_g_2", "kidx_norm_g_2")):
                        gp.dma_start(g2[:, i, :], a[name].to_broadcast([P, HD])).then_inc(small, 16)
                    for i, s in enumerate((2, 5)):
                        gp.dma_start(gate_bc[:, i, :], a["b_ada_2"][0:1, s * DM:(s + 1) * DM].to_broadcast([P, DM])).then_inc(small, 16)
                if it == ("norm", 0):
                    bank_taken(gp, USE["out1", 1, 1])
                    late = S("late_loaded")
                    gp.dma_start(pos_i[:, :], a["positions_2"][0].rearrange("(t p) -> p t", p=P)).then_inc(late, 16)
                    for j in range(3):
                        gp.dma_start(conv_w[:, j, :], a["conv_w_2"][0, j].rearrange("(k p) -> p k", p=P)).then_inc(late, 16)
                    gp.dma_start(w_router[:, :, :], a["w_router_2"][0].rearrange("(p k) n -> p k n", k=KT)).then_inc(late, 16)
                    gp.dma_start(rbias[:, :], a["router_bias_2"].to_broadcast([P, N_EXP])).then_inc(late, 16)
                if it in NTH_NORM:
                    kind = CHUNKS[it[1]][0] if it[0] == "proj" else CHUNKS2[it[1]][0]
                    inverse_root({"kv": 2, "kiwi": 1}.get(kind, 8), HD, "head_sums", NTH_NORM[it] + 1, "head_rstd")
        @block.scalar
        def _(act):
            def x_square(x, t, nth):
                if nth >= 1:
                    act.wait_ge(S("x_rstd"), nth)
                    act.wait_ge(S("x_scaled"), nth)
                act.activation(spare[:, 0:DM], x[:, t, :], ACT.Square, accum_out=msum[:, 0:1]).then_inc(S("x_squared"), 1)

            def round_turned_x(it):
                for t in range(NT):
                    for q in range(2):
                        n = 2 * t + q
                        act.wait_ge(S("turn_free"), TURN[it + (t, q)] + 1)
                        act.activation(a_parts[0][:, 4 * q:4 * q + 4, t * P:(t + 1) * P],
                                       turned_x[n % 2].rearrange("p (b n) -> p b n", b=4), ACT.Copy)\
                           .then_inc(S("a_hi"), 1)

            act.dma_start(consts[:, :], a["c_square"]).then_inc(S("consts_loaded"), 16)
            act.dma_start(ln_g[:, 0, :], a["ln_g"][0].rearrange("(p k) -> p k", k=KT)).then_inc(S("ln_g_loaded"), 16)
            nx = 0
            for it in RESULTS:
                if it[0] == "start":
                    for t in range(NT):
                        act.wait_ge(S(f"x_loaded_{t}"), 16)
                        x_square(G, t, nx)
                        nx += 1
                    round_turned_x(it)
                if it[0] == "small":
                    act.wait_ge(S("small_loaded"), 16 * N_SMALL)
                    act.activation(c_col[:, 1, :], c_col[:, 0, :], ACT.Exp, scale=-1.0).then_inc(S("c_exp"), 1)
                if it[0] == "norm":
                    for t in range(NT):
                        bank_taken(act, USE[("out1" if it[1] == 0 else "out2", 1, t)])
                        x_square(x, t, nx)
                        nx += 1
                    if it[1] == 0:
                        round_turned_x(it)
                if it[0] == "split":
                    _, name, arg, p = it
                    m = SPLITS.index(it[1:3])
                    j = JOB[it[1:3]]
                    kind, w = split_kind(name, arg)
                    if p == 0:
                        job_ready(act, j)
                    if m >= 1 and p < PIECES - 1:
                        act.wait_ge(S("w_used"), (PIECES - 1) * (m - 1) + p + 1)
                    elif m >= 1:
                        act.wait_ge(S("bank_full"), LAST_USE[SPLITS[m - 1]] + 1)
                    act.activation(w_parts[0][:, 2 * p:2 * p + 2, 0:w], view(j, kind)[:, 2 * p:2 * p + 2, :], ACT.Copy)\
                       .then_inc(S("w_hi"), 1)
                if it[0] == "mix_conv":
                    for c in range(2):
                        bank_taken(act, USE["proj2", 7, c])
                        act.activation(a_parts[0][:, 2 * c:2 * c + 2, :], convT[:, 2 * c:2 * c + 2, :], ACT.Copy)\
                           .then_inc(S("a_hi"), 1)
                if it[0] in ("proj", "proj2"):
                    n = USE[it]
                    kind, _, w, dst = (CHUNKS if it[0] == "proj" else CHUNKS2)[it[1]]
                    ps = proj_b[n % 2]
                    if it in NTH_NORM:
                        m = NTH_NORM[it]
                        w = {"kv": 128, "kiwi": 64}.get(kind, 512)
                        act.wait_ge(S("bank_full"), n + 1)
                        if m >= 1:
                            act.wait_ge(S("head_sums"), m)
                        act.activation(sq[:, 0:w], ps[:, 0:w], ACT.Square).then_inc(S("squared"), 1)
                    if kind in ("v", "v2", "xc"):
                        t = it[2]
                        o = {"v": lambda: V[:, t, dst:dst + 512], "v2": lambda: V2[:, t, :],
                             "xc": lambda: xcT[:, 2 * t:2 * t + 2, :].rearrange("p c n -> p (c n)")}[kind]()
                        act.wait_ge(S("bank_full"), n + 1)
                        act.activation(o, ps[:, :], ACT.Copy).then_inc(S(f"bank_free_{n % 2}"), 1)
                    if kind in ("silu", "gate"):
                        act.wait_ge(S("bank_full"), n + 1)
                        if kind == "gate":
                            m = SIGMOIDS.index(it)
                            if m >= 2:
                                bank_taken(act, USE[BRANCHED[m - 2]])
                            act.activation(gates[:, m % 2, :], ps[:, :], ACT.Tanh, scale=0.5)\
                               .then_inc(S(f"bank_free_{n % 2}"), 1)
                        else:
                            m = NTH_GATE[it]
                            if m >= 1:
                                bank_taken(act, USE[GATED[m - 1]])
                            act.activation(egate[:, :], ps[:, :], ACT.Tanh, scale=0.5).then_inc(S("gate_tanh"), 1)
                if it[0] == "turn":
                    k = TURN[it]
                    kind, _, _, dst = CHUNKS[it[1]]
                    t = it[2]
                    act.wait_ge(S("turned"), k + 1)
                    src = turn_b[:, :].rearrange("p (b n) -> p b n", b=4)
                    if kind == "q":
                        br = 0 if dst < 4 else (1 if dst < 16 else 2)
                        act.wait_ge(S("q_scale_ready"), 2)
                        act.activation(qT[:, dst:dst + 4, t * P:(t + 1) * P], src, ACT.Copy,
                                       scale=q_scale[:, br:br + 1]).then_inc(S("turn_free"), 1)
                    elif kind == "k":
                        act.activation(kT[:, dst:dst + 4, t * P:(t + 1) * P], src, ACT.Copy).then_inc(S("turn_free"), 1)
                    else:
                        act.activation(kT[:, dst:dst + 2, t * P:(t + 1) * P], src[:, 0:2], ACT.Copy)\
                           .then_inc(S("turn_free"), 1)
                if it[0] == "turn_branch":
                    i = it[1]
                    dst = OT if i < 3 else a_parts[0][:, WK:2 * WK, :]
                    for t in range(NT):
                        k = TURN[it + (t,)]
                        act.wait_ge(S("turned"), k + 1)
                        if i in (1, 2) and t == 0:
                            act.wait_ge(S("bank_full"), USE[("branch", i - 1, 1, 1)] + 1)
                        act.activation(dst[:, :, t * P:(t + 1) * P],
                                       turn_b[:, :].rearrange("p (b n) -> p b n", b=4), ACT.Copy,
                                       scale=0.5 if i < 3 else 1.0).then_inc(S("turn_free" if i < 3 else "a_hi"), 1)
                if it[0] == "turn_merged":
                    for t in range(NT):
                        for q in range(2):
                            act.wait_ge(S("turned"), TURN[it + (t, q)] + 1)
                            act.activation(a_parts[0][:, 4 * q:4 * q + 4, t * P:(t + 1) * P],
                                           wide_b[q][:, :].rearrange("p (b n) -> p b n", b=4), ACT.Copy, scale=0.5)\
                               .then_inc(S("a_hi"), 1)
                if it[0] == "turn2":
                    for g in range(4):
                        for t in range(NT):
                            act.wait_ge(S("turned"), TURN[it + (g, t)] + 1)
                            nb = 4 if g < 3 else 1
                            act.activation(T2[:, 4 * g:4 * g + nb, t * P:(t + 1) * P],
                                           turn_b[:, 0:P * nb].rearrange("p (b n) -> p b n", b=nb), ACT.Copy,
                                           scale=SCALE if g == 0 else 1.0).then_inc(S("turn_free"), 1)
                if it[0] == "angles":
                    act.wait_ge(S("angles_ready"), 1)
                    act.activation(trig[:, :, :, :], ang[:, :, :, :], ACT.Sin).then_inc(S("trig_ready"), 1)
                if it[0] == "index":
                    h = it[1]
                    act.wait_ge(S("index_product"), h + 1)
                    if h >= 2:
                        act.wait_ge(S("index_added"), h - 1)
                    act.activation(relu[:, h % 2, :], score_b[h % 2][:, 0:384], ACT.Relu).then_inc(S("relu_done"), 1)
                if it[0] == "score_rest":
                    n = it[1]
                    ng = len(units_of(n)) if n < 24 else 1
                    sink = 1 if 16 <= n < 24 else 0
                    i = HEADS.index(n)
                    act.wait_ge(S("maxed"), 2 * i + 2)
                    for t in range(NT):
                        lo, w = (0, P + sink) if t == 0 else (P + 1, 2 * P + sink)
                        v = L[:, i % 2, 0:ng, lo:lo + w]
                        act.activation(v, v, ACT.Exp, bias=nmax[:, i % 2, t:t + 1],
                                       accum_out=den[:, i % 2, t:t + 1]).then_inc(S("probs"), 1)
                if it[0] == "flip":
                    n = it[1]
                    ng = len(units_of(n)) if n < 24 else 1
                    i = HEADS.index(n)
                    for g in range(ng):
                        u = UNIT[n, g]
                        act.wait_ge(S("flipped"), u + 1)
                        if i >= 2:
                            act.wait_ge(S("value_product"), 2 * (i - 1))
                        act.activation(PT[:, i % 2, g, :], flip_b[u % 2][:, 0:384], ACT.Copy).then_inc(S("probsT"), 1)
                if it[0] == "router":
                    act.wait_ge(S("router_args"), 2)
                    act.activation(rexp[:, :, :, :], rarg[:, :, :, :], ACT.Exp).then_inc(S("router_exp"), 1)

            for f in range(FT):
                act.wait_ge(S(f"shared_up_{f}"), 1)
                act.activation(hs[:, f, :], up_b[f][:, 0:TOK], ACT.Silu).then_inc(S(f"shared_silu_{f}"), 1)
            for k in range(KT // 2):
                for t in range(NT):
                    n = 2 * k + t
                    act.wait_ge(S("h2_turned"), n + 1)
                    act.activation(x_hi[:, t, 2 * k:2 * k + 2, :],
                                   y_b[t][:, 0:2 * P].rearrange("p (b n) -> p b n", b=2), ACT.Copy)\
                       .then_inc(S("x_hi_ready"), 1)
            def copy_block(nth, q, z):
                act.wait_ge(S(f"gathered_{q}{z}"), nth)
                act.activation((xe_hi, xe_lo)[z][:, 4 * q:4 * q + 4, :],
                               gather_b[2 * q + z][:, :].rearrange("p (b n) -> p b n", b=4), ACT.Copy)\
                   .then_inc(S(f"block_ready_{q}{z}"), 1)

            def round_up_weights(r, kh, m):
                act.activation(up_hi[:, r % 2, 4 * kh:4 * kh + 4, m, :], raw_up(raw[:, r % 2, :], kh, m), ACT.Copy)\
                   .then_inc(S("up_hi"), 1)

            act.wait_ge(S("up_loaded_0"), 32)
            for kh in range(2):
                for m in range(2):
                    round_up_weights(0, kh, m)
            for q in range(2):
                for z in range(2):
                    copy_block(1, q, z)
            act.wait_ge(S("work_ready"), 2)
            n_work = act.value_load(work[0:1, 0:1], min_val=0, max_val=MAX_WORK)
            with act.Fori(0, -(-MAX_WORK // BODY)) as m4, act.If(n_work > m4 * BODY):
                for r in range(BODY):
                    i = m4 * BODY + r
                    with act.If(n_work > i):
                        act.wait_ge(S("block_done"), i + 1)
                        act.wait_ge(S(f"down_loaded_{r}"), 16 * (m4 + 1))
                        for f in range(FT):
                            act.activation(down_hi[:, f, :], raw[:, r % 2][:, UP + f * DM:UP + (f + 1) * DM], ACT.Copy)\
                               .then_inc(S("down_hi"), 1)
                        nxt = (r + 1) % BODY
                        act.wait_ge(S(f"up_loaded_{nxt}"), 32 * (m4 + 1 + (r + 1) // BODY))
                        for m in range(2):
                            round_up_weights(nxt, 0, m)
                        act.wait_ge(S("up_done"), i + 1)
                        act.activation(hs[:, 0, :], hidden_b[:, 0:ED], ACT.Silu).then_inc(S("silu_done"), 1)
                        copy_block(i + 2, 0, 0)
                        copy_block(i + 2, 0, 1)
                        act.wait_ge(S("h_turned"), i + 1)
                        act.activation(h_hi[:, :, :], turned_b[:, 0:ED].rearrange("p (f n) -> p f n", f=FT), ACT.Copy)\
                           .then_inc(S("h_hi_ready"), 1)
                        copy_block(i + 2, 1, 0)
                        round_up_weights(nxt, 1, 0)
                        act.wait_ge(S("gates_ready"), i + 1)
                        for hf in range(2):
                            act.wait_ge(S(f"down_{hf}"), i + 1)
                            act.activation(y_hi[:, hf * CH:(hf + 1) * CH], y_b[hf][:, :], ACT.Copy, scale=gcol[:, 0:1])\
                               .then_inc(S(f"y_hi_{hf}"), 1)
                        copy_block(i + 2, 1, 1)
                        round_up_weights(nxt, 1, 1)

        @block.vector
        def _(dve):
            n_scaled = 0

            def x_scale(x, t):
                nonlocal n_scaled
                dve.wait_ge(S("x_rstd"), n_scaled + 1)
                dve.tensor_scalar(xn, x[:, t, :], rstd[:, 0:1], None, ALU.mult).then_inc(S("x_scaled"), 1)
                n_scaled += 1

            def bc(ap2, n):
                return ap2.unsqueeze(2).to_broadcast([ap2.shape[0], ap2.shape[1], n])

            n_gt = 0
            for it in RESULTS:
                kind0 = it[0]
                if kind0 in ("start", "norm"):
                    w = 0 if kind0 == "start" else 1 + it[1]
                    if kind0 == "start":
                        dve.wait_ge(S("ln_g_loaded"), 16)
                    if kind0 == "norm":
                        m = it[1]
                        dve.wait_ge(S("turn_free"), TURN["ada_out", N_ADA - 1] + 1)
                        dve.tensor_tensor(mod[:, 2 * m + 1, :], mod[:, 2 * m + 1, :], ln_g[:, w, :], ALU.mult)\
                           .then_inc(S("mod_ready"), 1)
                    def rest_of_x(n):
                        t, q = n // 2, n % 2
                        dve.wait_ge(S("a_hi"), (0 if kind0 == "start" else 8) + n + 1)
                        sl = (slice(None), slice(4 * q, 4 * q + 4), slice(t * P, (t + 1) * P))
                        dve.tensor_tensor(a_parts[1][sl], turned_x[n % 2].rearrange("p (b n) -> p b n", b=4),
                                          a_parts[0][sl].bitcast(F32), ALU.subtract).then_inc(S("a_lo"), 1)

                    split = it != ("norm", 1)
                    for t in range(NT):
                        x_scale(G if kind0 == "start" else x, t)
                        for q in range(2):
                            n = 2 * t + q
                            dve.wait_ge(S("turned"), TURN[it + (t, q)] + 1)
                            src = wide_b[n % 2][:, :].rearrange("p (b n) -> p b n", b=4)
                            if split:
                                o = turned_x[n % 2].rearrange("p (b n) -> p b n", b=4)
                                if n >= 2:
                                    dve.wait_ge(S("a_lo"), (0 if kind0 == "start" else 4) + n - 1)
                            else:
                                o = xT[:, 4 * q:4 * q + 4, t * P:(t + 1) * P]
                            if kind0 == "start":
                                dve.tensor_tensor(o, src, bc(ln_g[:, 0, 4 * q:4 * q + 4], P), ALU.mult)\
                                   .then_inc(S("turn_free"), 1)
                            else:
                                dve.wait_ge(S("mod_ready"), m + 1)
                                for b in range(4):
                                    k = 4 * q + b
                                    last = dve.tensor_scalar(o[:, b], src[:, b], mod[:, 2 * m + 1, k:k + 1],
                                                             mod[:, 2 * m, k:k + 1], ALU.mult, ALU.add)
                                last.then_inc(S("turn_free"), 1)
                            if split and n:
                                rest_of_x(n - 1)
                    if split:
                        rest_of_x(3)
                if kind0 == "small":
                    dve.wait_ge(S("small_loaded"), 16 * N_SMALL)
                    dve.wait_ge(S("c_exp"), 1)
                    dve.tensor_scalar(c_col[:, 1, :], c_col[:, 1, :], 1.0, None, ALU.add).then_inc(S("c_step"), 1)
                    dve.wait_ge(S("c_step"), 1)
                    dve.reciprocal(c_col[:, 2, :], c_col[:, 1, :]).then_inc(S("c_step"), 1)
                    dve.wait_ge(S("c_step"), 2)
                    dve.tensor_tensor(c_col[:, 1, :], c_col[:, 0, :], c_col[:, 2, :], ALU.mult).then_inc(S("c_step"), 1)
                    gains = qk_g[:, :].rearrange("p (b two) -> p b two", two=2)
                    dve.tensor_tensor(q_scale[:, :], gains[:, :, 0], gains[:, :, 1], ALU.mult).then_inc(S("q_scale_ready"), 1)
                    dve.wait_ge(S("q_scale_ready"), 1)
                    dve.tensor_scalar(q_scale[:, :], q_scale[:, :], SCALE, None, ALU.mult).then_inc(S("q_scale_ready"), 1)
                    dve.wait_ge(S("rel_product"), 1)
                    dve.tensor_tensor(relrow, bank[6][0:40, 0:NREL_PAD], relmask, ALU.add)\
                       .then_inc(S("rel_ready"), 1)
                if kind0 == "split":
                    _, name, arg, p = it
                    m = SPLITS.index(it[1:3])
                    kind, w = split_kind(name, arg)
                    dve.wait_ge(S("w_hi"), PIECES * m + p + 1)
                    dve.tensor_tensor(w_parts[1][:, 2 * p:2 * p + 2, 0:w], view(JOB[it[1:3]], kind)[:, 2 * p:2 * p + 2, :],
                                      w_parts[0][:, 2 * p:2 * p + 2, 0:w].bitcast(F32), ALU.subtract)\
                       .then_inc(S("w_lo"), 1)
                if kind0 == "turn_merged":
                    for n in range(4):
                        t, q = n // 2, n % 2
                        dve.wait_ge(S("a_hi"), 4 + n + 1)
                        sl = (slice(None), slice(4 * q, 4 * q + 4), slice(t * P, (t + 1) * P))
                        dve.scalar_tensor_tensor(out=a_parts[1][sl], in0=wide_b[n % 2][:, :].rearrange("p (b n) -> p b n", b=4),
                                                 scalar=0.5, in1=a_parts[0][sl].bitcast(F32),
                                                 op0=ALU.mult, op1=ALU.subtract).then_inc(S("turn_free"), 1)
                if kind0 == "mix_conv":
                    for c in range(2):
                        dve.wait_ge(S("a_hi"), 12 + c + 1)
                        dve.tensor_tensor(a_parts[1][:, 2 * c:2 * c + 2, :], convT[:, 2 * c:2 * c + 2, :],
                                          a_parts[0][:, 2 * c:2 * c + 2, :].bitcast(F32), ALU.subtract)\
                           .then_inc(S("a_lo"), 1)
                if it == ("turn_branch", 3):
                    for t in range(NT):
                        dve.wait_ge(S("a_hi"), 14 + t + 1)
                        sl = (slice(None), slice(WK, 2 * WK), slice(t * P, (t + 1) * P))
                        dve.tensor_tensor(a_parts[1][sl], turn_b[:, :].rearrange("p (b n) -> p b n", b=4),
                                          a_parts[0][sl].bitcast(F32), ALU.subtract).then_inc(S("turn_free"), 1)
                if kind0 in ("proj", "proj2"):
                    n, t = USE[it], it[2]
                    kind, _, w, dst = (CHUNKS if kind0 == "proj" else CHUNKS2)[it[1]]
                    ps = proj_b[n % 2]
                    free = S(f"bank_free_{n % 2}")
                    if it in NTH_NORM:
                        m = NTH_NORM[it]
                        nh = {"kv": 2, "kiwi": 1}.get(kind, 8)
                        dve.wait_ge(S("squared"), m + 1)
                        if m >= 1:
                            dve.wait_ge(S("head_rstd"), m)
                        dve.tensor_reduce(msum[:, 0:nh], sq[:, 0:nh * HD].rearrange("p (h d) -> p h d", d=HD),
                                          AX.X, ALU.add).then_inc(S("head_sums"), 1)
                        dve.wait_ge(S("head_rstd"), m + 1)
                        heads = ps[:, 0:nh * HD].rearrange("p (h d) -> p h d", d=HD)
                        r8 = bc(rstd[:, 0:nh], HD)
                        if kind in ("q", "k"):
                            if m >= 2:
                                dve.wait_ge(S("turned"), TURN[("turn",) + NORMED[m - 2][1:]] + 1)
                            dve.tensor_tensor(qn[:, m % 2, :].rearrange("p (h d) -> p h d", d=HD), heads, r8, ALU.mult)\
                               .then_inc(free, 1)
                        elif kind == "kv":
                            dve.wait_ge(S("turned"), TURN[("turn",) + NORMED[m - 2][1:]] + 1)
                            o = qn[:, m % 2, 0:256].rearrange("p (g c d) -> p g c d", g=2, c=2)
                            for c in range(2):
                                dve.tensor_tensor(o[:, :, c, :], heads, r8, ALU.mult).then_inc(S("kv_step"), 1)
                            dve.tensor_copy(V[:, t, 2048:2176], ps[:, 128:256]).then_inc(free, 1)
                        else:
                            gi = {"q2": 0, "k2": 1, "kiwi": 2}[kind]
                            o = R[:, t, dst:dst + nh, :]
                            dve.tensor_tensor(o, heads, r8, ALU.mult).then_inc(S("r2_step"), 1)
                            n_gt += 1
                            dve.wait_ge(S("r2_step"), n_gt)
                            gains = g2[:, gi:gi + 1, :].to_broadcast([P, nh, HD])
                            if kind == "kiwi":
                                dve.tensor_copy(wi[:, t, :], ps[:, 64:72]).then_inc(S("wi_ready"), 1)
                            dve.tensor_tensor(o, o, gains, ALU.mult).then_inc(free, 1)
                    elif kind in ("v", "v2", "xc"):
                        pass
                    elif kind == "qi":
                        dve.wait_ge(S("bank_full"), n + 1)
                        dve.tensor_copy(R[:, t, dst:dst + 8, :], ps[:, :].rearrange("p (h d) -> p h d", d=HD))\
                           .then_inc(free, 1)
                    elif kind == "gate":
                        pass
                    elif kind == "silu":
                        dve.wait_ge(S("gate_tanh"), NTH_GATE[it] + 1)
                        if dst == 2:
                            dve.wait_ge(S("turned"), TURN["turn_branch", 0, t] + 1)
                        dve.scalar_tensor_tensor(out=O[:, dst % 2, t, :], in0=egate[:, :], scalar=1.0, in1=ps[:, :],
                                                 op0=ALU.add, op1=ALU.mult).then_inc(free, 1)
                    else:
                        v = ps[:, :].rearrange("p (c n) -> p c n", c=2)
                        dve.wait_ge(S("bank_full"), n + 1)
                        if kind == "cg":
                            bank_taken(dve, USE["proj2", it[1] - 1, t])
                            if t == 0:
                                dve.memset(uT[:, :, 0:2], 0.0).then_inc(S("u_pad"), 1)
                            dve.tensor_tensor(uT[:, 2 * t:2 * t + 2, 2:TOK + 2], v, xcT[:, 2 * t:2 * t + 2, :], ALU.mult)\
                               .then_inc(free, 1)
                        else:
                            bank_taken(dve, USE["proj2", it[1] - 1, t])
                            dve.wait_ge(S("late_loaded"), 16 * N_LATE)
                            dve.wait_ge(S("u_pad"), 1)
                            for c in range(2):
                                ct = 2 * t + c
                                s0 = 4 * ct - ct // 2
                                if ct % 2:
                                    dve.wait_ge(S("conv_step"), s0)
                                elif t:
                                    bank_taken(dve, n - 1)
                                dve.tensor_scalar(cv[:, :], uT[:, ct, 0:TOK], conv_w[:, 0, ct:ct + 1], None, ALU.mult)\
                                   .then_inc(S("conv_step"), 1)
                                for j in (1, 2):
                                    dve.wait_ge(S("conv_step"), s0 + j)
                                    dve.scalar_tensor_tensor(out=cv[:, :], in0=uT[:, ct, j:TOK + j],
                                                             scalar=conv_w[:, j, ct:ct + 1], in1=cv[:, :],
                                                             op0=ALU.mult, op1=ALU.add).then_inc(S("conv_step"), 1)
                                dve.wait_ge(S("conv_step"), s0 + 3)
                                dve.tensor_tensor(convT[:, ct, :], v[:, c], cv[:, :], ALU.mult)\
                                   .then_inc(free if c else S("conv_step"), 1)
                if kind0 == "branch":
                    _, i, hf, t = it
                    n = USE[it]
                    g0 = G[:, t, hf * CH:hf * CH + CH]
                    m = BRANCHED.index(it)
                    g = gates[:, m % 2, :]
                    dve.wait_ge(S("bank_full"), n + 1)
                    bank_taken(dve, USE[SIGMOIDS[m]])
                    done = S("merge_step" if i else f"bank_free_{n % 2}")
                    dve.scalar_tensor_tensor(out=g if i else g0, in0=g, scalar=1.0, in1=proj_b[n % 2][:, :],
                                             op0=ALU.add, op1=ALU.mult).then_inc(done, 1)
                    if i:
                        dve.wait_ge(S("merge_step"), 4 * (i - 1) + 2 * hf + t + 1)
                        bank_taken(dve, USE["branch", i - 1, hf, t])
                        dve.tensor_tensor(g0, g0, g, ALU.add).then_inc(S(f"bank_free_{n % 2}"), 1)
                if kind0 == "out1":
                    _, hf, t = it
                    n = USE[it]
                    o = x[:, t, hf * CH:hf * CH + CH]
                    dve.wait_ge(S("bank_full"), n + 1)
                    dve.wait_ge(S(f"x_loaded_{t}"), 32)
                    dve.tensor_tensor(o, o, proj_b[n % 2][:, :], ALU.add).then_inc(S(f"bank_free_{n % 2}"), 1)
                if kind0 == "out2":
                    _, hf, t = it
                    n = USE[it]
                    o = x[:, t, hf * CH:hf * CH + CH]
                    tmp = qn[:, n % 2, :]
                    dve.wait_ge(S("bank_full"), n + 1)
                    dve.tensor_tensor(tmp, proj_b[n % 2][:, :], gate_bc[:, 0, hf * CH:hf * CH + CH], ALU.mult)\
                       .then_inc(S("mix_step"), 1)
                    dve.wait_ge(S("mix_step"), 2 * hf + t + 1)
                    dve.tensor_tensor(o, o, tmp, ALU.add).then_inc(S(f"bank_free_{n % 2}"), 1)
                if kind0 == "ada":
                    _, c, part = it
                    j = JOB["w_ada", c]
                    o = ada_acc[:, c % 2, :]
                    w = view(j, "k8")
                    if part == 0:
                        job_ready(dve, j)
                        if c >= 2:
                            dve.wait_ge(S("turned"), TURN["ada_out", c - 2] + 1)
                        if c == 0:
                            dve.wait_ge(S("c_step"), 3)
                        dve.tensor_scalar(o, w[:, 0], c_col[:, 1, 0:1], None, ALU.mult).then_inc(S("ada_step"), 1)
                    for k in range(max(1, 2 * part), 2 * part + 2):
                        dve.wait_ge(S("ada_step"), (KT - 1) * c + k)
                        dve.scalar_tensor_tensor(out=o, in0=w[:, k], scalar=c_col[:, 1, k:k + 1], in1=o,
                                                 op0=ALU.mult, op1=ALU.add)\
                           .then_inc(S("ada_step" if k < KT - 1 else "ada_summed"), 1)
                if kind0 == "ada_out":
                    c = it[1]
                    s, hf = c // 2, c % 2
                    k = TURN[it]
                    dve.wait_ge(S("turned"), k + 1)
                    dve.wait_ge(S("small_loaded"), 16 * N_SMALL)
                    if s in (2, 5):
                        o = gate_bc[:, s // 3, hf * CH:(hf + 1) * CH]
                        dve.tensor_tensor(o, o, turn_b[:, :], ALU.add).then_inc(S("turn_free"), 1)
                    else:
                        m = {0: 0, 1: 1, 3: 2, 4: 3}[s]
                        rows = slice(HD * hf, HD * hf + HD)
                        dve.scalar_tensor_tensor(out=mod[rows, m, :], in0=turn_b[rows, 0:KT], scalar=float(s in (1, 4)),
                                                 in1=b_ada[rows, s, :], op0=ALU.add, op1=ALU.add)\
                           .then_inc(S("turn_free"), 1)
                if kind0 in ("score", "score_rest"):
                    n = it[1]
                    i = HEADS.index(n)
                    ng = len(units_of(n)) if n < 24 else 1
                    sink = 1 if 16 <= n < 24 else 0
                    buf = L[:, i % 2]
                    for g in range(0 if kind0 == "score" else 2, min(2, ng) if kind0 == "score" else ng):
                        u = UNIT[n, g]
                        if i >= 2 and g == 0:
                            dve.wait_ge(S("flipped"), UNIT[HEADS[i - 2], 0] + (len(units_of(HEADS[i - 2])) if HEADS[i - 2] < 24 else 1))
                        dve.wait_ge(S("scored"), u + 1)
                        if n < 24:
                            dve.wait_ge(S(f"bias_loaded_{u % BIAS_SLOTS}"), 16 * (u // BIAS_SLOTS + 1))
                            back = bias[:, u % BIAS_SLOTS, ::-1]
                            add = [back[:, P:2 * P], back]
                        else:
                            dve.wait_ge(S("selmask_ready"), 1)
                            add = [selmask[:, 0:P], selmask[:, P:3 * P]]
                        ps = score_b[u % 2]
                        dve.tensor_tensor(buf[:, g, 0:P], ps[:, 0:P], add[0], ALU.add).then_inc(S("logits_half"), 1)
                        dve.tensor_tensor(buf[:, g, P + 1:3 * P + 1], ps[:, P:3 * P], add[1], ALU.add)\
                           .then_inc(S("logits"), 1)
                if kind0 == "score_rest":
                    if sink:
                        h = n - 16
                        for t in range(NT):
                            at = (P, 3 * P + 1)[t]
                            dve.tensor_copy(buf[:, 0, at:at + 1], sinks[:, h:h + 1]).then_inc(S("sink_set"), 1)
                        dve.wait_ge(S("sink_set"), 2 * h + 2)
                    dve.wait_ge(S("logits"), UNIT[n, ng - 1] + 1)
                    if i >= 2:
                        dve.wait_ge(S("probs"), 2 * i - 2)
                    for t in range(NT):
                        lo, w = (0, P + sink) if t == 0 else (P + 1, 2 * P + sink)
                        dve.tensor_reduce(nmax[:, i % 2, t:t + 1], buf[:, 0:ng, lo:lo + w],
                                          AX.XY, ALU.max, negate=True).then_inc(S("maxed"), 1)
                if kind0 == "flip":
                    i = HEADS.index(it[1])
                    dve.wait_ge(S("probs"), 2 * i + 2)
                    if i >= 2:
                        dve.wait_ge(S("valued"), 2 * i - 2)
                    dve.reciprocal(rden[:, i % 2, :], den[:, i % 2, :]).then_inc(S("rden_ready"), 1)
                if kind0 == "value":
                    n = it[1]
                    i = HEADS.index(n)
                    dve.wait_ge(S("rden_ready"), i + 1)
                    for t in range(NT):
                        dve.wait_ge(S("value_product"), 2 * i + 2)
                        ps = value_b[:, 128 * (i % 2) + 64 * t:128 * (i % 2) + 64 * t + 64]
                        if n < 24:
                            o = O[:, n // 8 % 2, t, HD * (n % 8):HD * (n % 8) + HD]
                            if n % 8 == 0 and t == 0:
                                c = [k for k, ch in enumerate(CHUNKS) if ch[0] == "silu"][n // 8]
                                bank_taken(dve, USE["proj", c, 1])
                            dve.scalar_tensor_tensor(out=o, in0=ps, scalar=rden[:, i % 2, t:t + 1], in1=o,
                                                     op0=ALU.mult, op1=ALU.mult).then_inc(S("valued"), 1)
                        else:
                            o = O2[:, t, HD * (n - 24):HD * (n - 24) + HD]
                            dve.tensor_scalar(o, ps, rden[:, i % 2, t:t + 1], None, ALU.mult).then_inc(S("valued"), 1)
                if kind0 in ("angles", "rope"):
                    step = S(kind0 + "_step")
                    k = 0

                    def chain(ins):
                        nonlocal k
                        ins.then_inc(step, 1)
                        k += 1
                        dve.wait_ge(step, k)

                if kind0 == "angles":
                    dve.wait_ge(S("late_loaded"), 16 * N_LATE)
                    chain(dve.tensor_copy(pos[:, :], pos_i[:, :]))
                    for t in range(NT):
                        chain(dve.tensor_scalar(ang[:, t, 1, :], consts[:, C_FREQ:C_FREQ + 8], pos[:, t:t + 1], None,
                                                ALU.mult))
                    chain(dve.tensor_scalar(turns_f[:, :, 1, :], ang[:, :, 1, :], 1.0 / (2 * math.pi), None, ALU.mult))
                    chain(dve.tensor_scalar(turns_f[:, :, 0, :], turns_f[:, :, 1, :], 0.25, None, ALU.add))
                    chain(dve.tensor_copy(turns_i[:, :, :, :], turns_f[:, :, :, :]))
                    chain(dve.tensor_copy(turns_f[:, :, :, :], turns_i[:, :, :, :]))
                    chain(dve.tensor_copy(ang[:, :, 0, :], ang[:, :, 1, :]))
                    c1 = 6.28125
                    c2 = float(np.float32(np.floor((2 * math.pi - c1) * 2 ** 20) / 2 ** 20))
                    c3 = 2 * math.pi - c1 - c2
                    for c in (c1, c2, c3):
                        chain(dve.scalar_tensor_tensor(out=ang[:, :, :, :], in0=turns_f[:, :, :, :], scalar=-c,
                                                       in1=ang[:, :, :, :], op0=ALU.mult, op1=ALU.add))
                    chain(dve.tensor_scalar(ang[:, :, 0, :], ang[:, :, 0, :], math.pi / 2, None, ALU.add))
                    for op, lim, sign in ((ALU.is_gt, math.pi, -1.0), (ALU.is_lt, -math.pi, 1.0)):
                        chain(dve.tensor_scalar(wrap[:, :, :, :], ang[:, :, :, :], lim, sign * 2 * math.pi, op, ALU.mult))
                        chain(dve.tensor_tensor(ang[:, :, :, :], ang[:, :, :, :], wrap[:, :, :, :], ALU.add))
                    dve.tensor_scalar(ang[:, :, :, :], ang[:, :, :, :], 3.1415925, -3.1415925, ALU.min, ALU.max)\
                       .then_inc(S("angles_ready"), 1)
                if kind0 == "rope":
                    dve.wait_ge(S("trig_ready"), 1)
                    bank_taken(dve, USE["proj2", 3, 1])
                    for t in range(NT):
                        lo, hi = R[:, t, 0:25, 0:8], R[:, t, 0:25, 8:16]
                        cos = trig[:, t, 0:1, :].to_broadcast([P, 25, 8])
                        sin = trig[:, t, 1:2, :].to_broadcast([P, 25, 8])
                        for b, (src, f) in enumerate(((lo, cos), (hi, sin), (hi, cos), (lo, sin))):
                            chain(dve.tensor_tensor(rt[:, b], src, f, ALU.mult))
                        chain(dve.tensor_tensor(lo, rt[:, 0], rt[:, 1], ALU.subtract))
                        chain(dve.tensor_tensor(hi, rt[:, 2], rt[:, 3], ALU.add))
                        dve.tensor_copy(R[:, t, 25, :], R[:, t, 24, :]).then_inc(S("rows_ready"), 1)
                if kind0 == "index":
                    h = it[1]
                    dve.wait_ge(S("relu_done"), h + 1)
                    dve.wait_ge(S("wi_ready"), 2)
                    for t, (lo, w) in enumerate(((0, P), (P, 2 * P))):
                        o = score[:, lo:lo + w]
                        r = relu[:, h % 2, lo:lo + w]
                        done = S("index_half" if t == 0 else "index_added")
                        if h == 0:
                            dve.tensor_scalar(o, r, wi[:, t, h:h + 1], None, ALU.mult).then_inc(done, 1)
                        else:
                            dve.wait_ge(done, h)
                            dve.scalar_tensor_tensor(out=o, in0=r, scalar=wi[:, t, h:h + 1], in1=o,
                                                     op0=ALU.mult, op1=ALU.add).then_inc(done, 1)
                if kind0 == "topk":
                    step = S("topk_step")
                    k = TOPK_STEPS * it[1]

                    def chain(ins):
                        nonlocal k
                        ins.then_inc(step, 1)
                        k += 1
                        dve.wait_ge(step, k)

                    caus = [consts[:, C_CAUS + P:C_CAUS + 2 * P], consts[:, C_CAUS:C_CAUS + 2 * P]]
                    dve.wait_ge(S("index_added"), 8)
                    for t, lo, w in (((0, 0, P), (1, P, 2 * P))[it[1]],):
                        o = score[:, lo:lo + w]
                        chain(dve.scalar_tensor_tensor(out=o, in0=o, scalar=IDX_SCALE, in1=caus[t],
                                                       op0=ALU.mult, op1=ALU.add))
                        for _ in range(TOP_KEYS // 8):
                            chain(dve.max(top8[:, t, :], o))
                            chain(dve.match_replace(out=o, in_to_replace=top8[:, t, :], in_values=o, imm_value=TAKEN))
                        chain(dve.tensor_scalar(o, o, TAKEN / 2, NEG, ALU.is_gt, ALU.mult))
                        last = dve.tensor_tensor(selmask[:, lo:lo + w], o, caus[t], ALU.add)
                        if t == 0:
                            chain(last)
                        else:
                            last.then_inc(S("selmask_ready"), 1)
                if kind0 == "router":
                    step = S("router_step")
                    k = 0

                    def chain(ins):
                        nonlocal k
                        ins.then_inc(step, 1)
                        k += 1
                        dve.wait_ge(step, k)

                    dve.wait_ge(S("router_product"), 1)
                    z = turn_b[:, 0:NT * N_EXP].rearrange("p (t e) -> p t e", t=NT)
                    dve.tensor_scalar(rarg[:, 0], z, 0.0, None, ALU.min).then_inc(S("router_args"), 1)
                    dve.wait_ge(S("router_args"), 1)
                    dve.scalar_tensor_tensor(out=rarg[:, 1], in0=rarg[:, 0], scalar=2.0, in1=z, op0=ALU.mult,
                                             op1=ALU.subtract)\
                       .then_inc(S("router_args"), 1)
                    dve.wait_ge(S("router_exp"), 1)
                    chain(dve.tensor_scalar(rexp[:, 1], rexp[:, 1], 1.0, None, ALU.add))
                    chain(dve.reciprocal(rexp[:, 1], rexp[:, 1]))
                    chain(dve.tensor_tensor(sig[:, :, :], rexp[:, 0], rexp[:, 1], ALU.mult))
                    chain(dve.tensor_tensor(sel[:, :, :], sig[:, :, :],
                                            rbias[:, :].unsqueeze(1).to_broadcast([P, NT, N_EXP]), ALU.add))
                    for t in range(NT):
                        chain(dve.max(top8[:, t, :], sel[:, t, :]))
                        chain(dve.match_replace(out=sel[:, t, :], in_to_replace=top8[:, t, :], in_values=sel[:, t, :],
                                                imm_value=TAKEN))
                    chain(dve.tensor_scalar(sel[:, :, :], sel[:, :, :], TAKEN / 2, None, ALU.is_lt))
                    chain(dve.tensor_tensor(sig[:, :, :], sig[:, :, :], sel[:, :, :], ALU.mult))
                    chain(dve.tensor_reduce(gsum[:, :], sig[:, :, :], AX.X, ALU.add))
                    chain(dve.reciprocal(gsum[:, :], gsum[:, :]))
                    for j in range(2):
                        ins = dve.tensor_copy(taken[:, :, N_EXP * j:N_EXP * j + N_EXP], sel[:, :, :])
                        ins.then_inc(S("taken_ready"), 1)
                    for t in range(NT):
                        for j in range(2):
                            chain(dve.tensor_scalar(pcol[:, N_EXP * j:N_EXP * j + N_EXP, NT + t], sig[:, t, :],
                                                    gsum[:, t:t + 1], ROUTED, ALU.mult, ALU.mult))
                    dve.wait_ge(S("ranked"), 1)
                    counted = y_b[0][:, 2 * NV:2 * NV + 1]
                    dve.tensor_scalar(used[:, :], counted, consts[:, C_THR:C_THR + 1], None, ALU.is_gt)\
                       .then_inc(S("used_ready"), 1)
                    for t in range(NT):
                        chain(dve.tensor_tensor(ranks[:, t, :], y_b[0][:, NV * t:NV * t + NV],
                                                consts[:, C_THR_ROW:C_THR_ROW + NV], ALU.subtract))
                        chain(dve.tensor_tensor(ranks[:, t, :], ranks[:, t, :], taken[:, t, :], ALU.mult))
                        dve.tensor_scalar(ranks[:, t, :], ranks[:, t, :], -FAR, None, ALU.add)\
                           .then_inc(S("ranks_ready"), 1)
                    dve.wait_ge(S("places_counted"), 1)
                    chain(dve.tensor_copy(place[:, :], y_b[1][:, 0:1]))
                    dve.wait_ge(S("used_ready"), 1)
                    dve.tensor_scalar(order[:, :], consts[:, C_IOTA:C_IOTA + NV], place[:, 0:1],
                                      used[:, 0:1], ALU.is_equal, ALU.mult).then_inc(S("order_ready"), 1)
                    dve.wait_ge(S("ranks_ready"), NT)
                    for t in range(NT):
                        chain(dve.tensor_copy(pcol[:, :, t], ranks[:, t, :]))
                    dve.wait_ge(S("ranks_turned"), 1)
                    dve.tensor_copy(prow[:, :], y_b[0][:, 0:TOK]).then_inc(S("rows_turned"), 1)
                    dve.wait_ge(S("list_product"), 1)
                    dve.tensor_copy(work[0:1, 1:1 + 2 * NV], y_b[1][0:1, 0:2 * NV]).then_inc(S("work_ready"), 1)
                    dve.tensor_copy(work[0:1, 0:1], y_b[1][0:1, 2 * NV:2 * NV + 1]).then_inc(S("work_ready"), 1)

            for f in range(FT):
                dve.wait_ge(S(f"shared_silu_{f}"), 1)
                dve.tensor_tensor(hT[:, f, :], hs[:, f, :], up_b[f][:, TOK:2 * TOK], ALU.mult)\
                   .then_inc(S(f"shared_h_{f}"), 1)

            for k in range(KT // 2):
                for t in range(NT):
                    n = 2 * k + t
                    dve.wait_ge(S("x_hi_ready"), n + 1)
                    sl = x_hi[:, t, 2 * k:2 * k + 2, :]
                    dve.tensor_tensor(x_lo[:, t, 2 * k:2 * k + 2, :],
                                      y_b[t][:, 0:2 * P].rearrange("p (b n) -> p b n", b=2), sl.bitcast(F32),
                                      ALU.subtract).then_inc(S("x_lo_ready"), 1)
            def make_picks(r, loads):
                dve.wait_ge(S(f"places_loaded_{r}"), loads)
                dve.tensor_tensor(pick[:, r % 2], consts[:, C_IOTA:C_IOTA + P].unsqueeze(1).to_broadcast([P, NT, P]),
                                  bc(col4[:, r, 0:NT], P), ALU.is_equal).then_inc(S("pick_ready"), 1)
                dve.tensor_scalar(put[:, r % 2, :], row4[:, r, :], consts[:, C_COL:C_COL + 1], None, ALU.is_equal)\
                   .then_inc(S("put_ready"), 1)

            def rest_of_up_weights(i, r, kh, m):
                dve.wait_ge(S("up_hi"), 4 * i + 2 * kh + m + 1)
                dve.tensor_tensor(up_lo[:, r % 2, 4 * kh:4 * kh + 4, m, :], raw_up(raw[:, r % 2, :], kh, m),
                                  up_hi[:, r % 2, 4 * kh:4 * kh + 4, m, :].bitcast(F32), ALU.subtract)\
                   .then_inc(S("up_lo"), 1)

            make_picks(0, 32)
            for kh in range(2):
                for m in range(2):
                    rest_of_up_weights(0, 0, kh, m)
            dve.wait_ge(S("work_ready"), 2)
            n_work = dve.value_load(work[0:1, 0:1], min_val=0, max_val=MAX_WORK)
            with dve.Fori(0, -(-MAX_WORK // BODY)) as m4, dve.If(n_work > m4 * BODY):
                for r in range(BODY):
                    i = m4 * BODY + r
                    with dve.If(n_work > i):
                        nxt = (r + 1) % BODY
                        for f in range(FT):
                            dve.wait_ge(S("down_hi"), 2 * i + f + 1)
                            dve.tensor_tensor(down_lo[:, f, :], raw[:, r % 2][:, UP + f * DM:UP + (f + 1) * DM],
                                              down_hi[:, f, :].bitcast(F32), ALU.subtract).then_inc(S("down_lo"), 1)
                        dve.wait_ge(S("block_done"), i + 1)
                        make_picks(nxt, 32 * (m4 + 1 + (r + 1) // BODY))
                        for m in range(2):
                            rest_of_up_weights(i + 1, nxt, 0, m)
                        dve.wait_ge(S("gates_gathered"), i + 1)
                        dve.tensor_copy(gcol[:, :], turned_b[:, ED:ED + 1]).then_inc(S("gates_ready"), 1)
                        dve.wait_ge(S("silu_done"), i + 1)
                        dve.tensor_tensor(he, hs[:, 0, :], hidden_b[:, ED:2 * ED], ALU.mult).then_inc(S("h_done"), 1)
                        dve.wait_ge(S("h_hi_ready"), i + 1)
                        dve.tensor_tensor(h_lo[:, :, :], turned_b[:, 0:ED].rearrange("p (f n) -> p f n", f=FT),
                                          h_hi[:, :, :].bitcast(F32), ALU.subtract).then_inc(S("h_lo_ready"), 1)
                        rest_of_up_weights(i + 1, nxt, 1, 0)
                        dve.wait_ge(S("gates_ready"), i + 1)
                        for hf in range(2):
                            dve.wait_ge(S(f"y_hi_{hf}"), i + 1)
                            c = slice(hf * CH, (hf + 1) * CH)
                            dve.scalar_tensor_tensor(out=y_lo[:, c], in0=y_b[hf][:, :], scalar=gcol[:, 0:1],
                                                     in1=y_hi[:, c].bitcast(F32), op0=ALU.mult, op1=ALU.subtract)\
                               .then_inc(S(f"y_lo_{hf}"), 1)
                        rest_of_up_weights(i + 1, nxt, 1, 1)
            dve.wait_ge(S("experts_summed"), 1)
            for t in range(NT):
                for hf in range(2):
                    tmp = qn[:, hf, :]
                    o = x[:, t, hf * CH:hf * CH + CH]
                    dve.tensor_tensor(tmp, acc_b[2 * t + hf][:, :], gate_bc[:, 1, hf * CH:hf * CH + CH], ALU.mult)\
                       .then_inc(S("final_step"), 1)
                    dve.wait_ge(S("final_step"), 2 * t + hf + 1)
                    dve.tensor_tensor(o, o, tmp, ALU.add).then_inc(S("out_ready"), 1)

        @block.tensor
        def _(pe):
            PASSES = ((0, 0), (0, 1), (1, 0))

            def turn_bank(k):
                if k >= 1:
                    pe.wait_ge(S("turn_free"), k)

            def wide_bank(k, n):
                if k >= 1 and (n == 0 or k >= 2):
                    pe.wait_ge(S("turn_free"), k if n == 0 else k - 1)

            def use_bank(n):
                if n >= 2:
                    bank_taken(pe, n - 2)
                return proj_b[n % 2]

            for it in SCHEDULE:
                kind0 = it[0]
                if kind0 == "start":
                    pe.wait_ge(S("consts_loaded"), 16)
                    pe.wait_ge(S("ones_set"), 1)
                if kind0 in ("start", "norm"):
                    base = {("start",): 0, ("norm", 0): NT, ("norm", 1): 2 * NT}[it]
                    for t in range(NT):
                        pe.wait_ge(S("x_scaled"), base + t + 1)
                        for q in range(2):
                            n = 2 * t + q
                            wide_bank(TURN[it + (t, q)], n)
                            for b in range(4):
                                k = 4 * q + b
                                mm = pe.transpose(wide_b[n % 2][:, b * P:(b + 1) * P], xn[:, k:DM:KT], ident)
                            mm.then_inc(S("turned"), 1)
                if kind0 == "small":
                    pe.wait_ge(S("small_loaded"), 16 * N_SMALL)
                    pe.matmul(bank[6][0:40, 0:NREL_PAD], tabT[:, :], hot, start=True, stop=True)\
                      .then_inc(S("rel_product"), 1)
                if kind0 in SPLIT_OF:
                    name, arg, t = SPLIT_OF[kind0], it[1], it[2]
                    n = USE[it]
                    m = SPLITS.index((name, arg))
                    kind, w = split_kind(name, arg)
                    ps = use_bank(n)
                    if n == 0 or (t == 0 and arg == 0):
                        if kind0 == "proj":
                            pe.wait_ge(S("a_lo"), 4)
                        if kind0 == "out1":
                            pe.wait_ge(S("turn_free"), TURN["turn_merged", 1, 1] + 1)
                        if kind0 == "proj2":
                            pe.wait_ge(S("a_lo"), 8)
                        if kind0 == "out2":
                            pe.wait_ge(S("a_lo"), 10)
                            pe.wait_ge(S("turn_free"), TURN["turn_branch", 3, 1] + 1)
                    conv = kind0 == "proj2" and CHUNKS2[arg][0] in ("xc", "cg", "bg")
                    for q in range(2 if conv else 1):
                        ct = 2 * t + q
                        for k in range(KT):
                            if t == 0 and q == 0 and k % 2 == 0:
                                pe.wait_ge(S("w_lo"), PIECES * m + k // 2 + 1)
                            for z, (za, zw) in enumerate(PASSES):
                                start, stop = (k == 0 and z == 0), (k == KT - 1 and z == 2)
                                if conv:
                                    mm = pe.matmul(ps[:, q * TOK:(q + 1) * TOK], w_parts[zw][:, k, ct * P:(ct + 1) * P],
                                                   a_parts[za][:, k, :], start=start, stop=stop)
                                else:
                                    mm = pe.matmul(ps[:, 0:w], a_parts[za][:, k, t * P:(t + 1) * P],
                                                   w_parts[zw][:, k, 0:w], start=start, stop=stop)
                            if t == 1 and q == int(conv) and k % 2 and k < KT - 1:
                                mm.then_inc(S("w_used"), 1)
                    mm.then_inc(S("bank_full"), 1)
                if kind0 == "branch":
                    n = USE[it]
                    ps = use_bank(n)
                    _, i, hf, t = it
                    j = JOB["w_branch", i]
                    if hf == 0 and t == 0:
                        job_ready(pe, j)
                        pe.wait_ge(S("turn_free"), TURN["turn_branch", i, 1] + 1)
                    wv = view(j, "k4")
                    for k in range(WK):
                        mm = pe.matmul(ps[:, :], OT[:, k, t * P:(t + 1) * P], wv[:, k, hf * CH:hf * CH + CH],
                                       start=(k == 0), stop=(k == WK - 1))
                    mm.then_inc(S("bank_full"), 1)
                if kind0 == "turn":
                    _, c, t = it
                    k = TURN[it]
                    m = NTH_NORM["proj", c, t]
                    bank_taken(pe, USE["proj", c, t])
                    turn_bank(k)
                    nb = 2 if CHUNKS[c][0] == "kv" else 4
                    for b in range(nb):
                        mm = pe.transpose(turn_b[:, b * P:(b + 1) * P], qn[:, m % 2, b * P:(b + 1) * P], ident)
                    mm.then_inc(S("turned"), 1)
                if kind0 == "turn_branch":
                    i = it[1]
                    pe.wait_ge(S("valued"), 2 * (8 * i + 8))
                    for t in range(NT):
                        turn_bank(TURN[it + (t,)])
                        for b in range(4):
                            src = O[:, i % 2, t, b * P:(b + 1) * P] if i < 3 else O2[:, t, b * P:(b + 1) * P]
                            mm = pe.transpose(turn_b[:, b * P:(b + 1) * P], src, ident)
                        mm.then_inc(S("turned"), 1)
                if kind0 == "turn_merged":
                    bank_taken(pe, USE["branch", 2, 1, 0])
                    bank_taken(pe, USE["branch", 2, 1, 1])
                    for t in range(NT):
                        for q in range(2):
                            n = 2 * t + q
                            wide_bank(TURN[it + (t, q)], n)
                            for b in range(4):
                                k = 4 * q + b
                                mm = pe.transpose(wide_b[n % 2][:, b * P:(b + 1) * P], G[:, t, k * P:(k + 1) * P], ident)
                            mm.then_inc(S("turned"), 1)
                if kind0 == "turn2":
                    pe.wait_ge(S("rows_ready"), NT)
                    for g in range(4):
                        for t in range(NT):
                            turn_bank(TURN[it + (g, t)])
                            for b in range(4 if g < 3 else 1):
                                r0 = 8 * g + 2 * b
                                mm = pe.transpose(turn_b[:, b * P:(b + 1) * P],
                                                  R[:, t, r0:r0 + 2, :].rearrange("p h d -> p (h d)"), ident)
                            mm.then_inc(S("turned"), 1)
                if kind0 == "ada_out":
                    c = it[1]
                    s, hf = c // 2, c % 2
                    pe.wait_ge(S("ada_summed"), c + 1)
                    turn_bank(TURN[it])
                    acc = ada_acc[:, c % 2, :]
                    if s in (2, 5):
                        mm = pe.matmul(turn_b[:, :], ones[:, :], acc, start=True, stop=True)
                    else:
                        for k in range(KT):
                            mm = pe.matmul(turn_b[HD * hf:HD * hf + HD, k:k + 1], acc[:, k:CH:KT], ones[:, 0:1],
                                           start=True, stop=True)
                    mm.then_inc(S("turned"), 1)
                if kind0 in ("score", "score_rest"):
                    n = it[1]
                    ng = len(units_of(n)) if n < 24 else 1
                    for g in range(0 if kind0 == "score" else 2, min(2, ng) if kind0 == "score" else ng):
                        u = UNIT[n, g]
                        if u >= 2:
                            pe.wait_ge(S("logits"), u - 1)
                        if n < 24:
                            qp, kp, half, _, _ = units_of(n)[g]
                            q, kk = qT[HD * half:HD * half + HD, qp, :], kT[HD * half:HD * half + HD, kp, :]
                            if n % 8 == 0 and g == 0:
                                c = {0: 1, 1: 9, 2: 15}[n // 8]
                                pe.wait_ge(S("turn_free"), TURN["turn", c, 1] + 1)
                        else:
                            h = n - 24
                            half = h % 2
                            q, kk = T2[HD * half:HD * half + HD, h // 2, :], T2[HD * half:HD * half + HD, 4 + h // 2, :]
                            if h == 0:
                                pe.wait_ge(S("relu_done"), 8)
                        ps = score_b[u % 2]
                        pe.matmul(ps[:, 0:P], q[:, 0:P], kk[:, 0:P], start=True, stop=True)
                        pe.matmul(ps[:, P:3 * P], q[:, P:2 * P], kk, start=True, stop=True).then_inc(S("scored"), 1)
                if kind0 == "index":
                    h = it[1]
                    half = h % 2
                    if h == 0:
                        pe.wait_ge(S("turn_free"), TURN["turn2", 3, 1] + 1)
                        pe.wait_ge(S("logits"), N_BIAS)
                    if h >= 2:
                        pe.wait_ge(S("relu_done"), h - 1)
                    q, kk = T2[HD * half:HD * half + HD, 8 + h // 2, :], T2[HD * half:HD * half + HD, 12, :]
                    ps = score_b[h % 2]
                    pe.matmul(ps[:, 0:P], q[:, 0:P], kk[:, 0:P], start=True, stop=True)
                    pe.matmul(ps[:, P:3 * P], q[:, P:2 * P], kk, start=True, stop=True).then_inc(S("index_product"), 1)
                if kind0 == "flip":
                    n = it[1]
                    i = HEADS.index(n)
                    for g in range(len(units_of(n)) if n < 24 else 1):
                        u = UNIT[n, g]
                        pe.wait_ge(S("probs"), 2 * i + 2)
                        if u >= 2:
                            pe.wait_ge(S("probsT"), u - 1)
                        for b, lo in enumerate((0, P + 1, 2 * P + 1)):
                            mm = pe.transpose(flip_b[u % 2][:, b * P:(b + 1) * P], L[:, i % 2, g, lo:lo + P], ident)
                        mm.then_inc(S("flipped"), 1)
                if kind0 == "value":
                    n = it[1]
                    i = HEADS.index(n)
                    ng = len(units_of(n)) if n < 24 else 1
                    pe.wait_ge(S("probsT"), UNIT[n, ng - 1] + 1)
                    if n in (0, 8, 16):
                        c = {0: 2, 8: 12, 16: 15}[n]
                        bank_taken(pe, USE["proj", c, 1])
                    if n == 0:
                        pe.wait_ge(S("rel_ready"), 1)
                    if n == 24:
                        bank_taken(pe, USE["proj2", 4, 1])
                    if i >= 1:
                        pe.wait_ge(S("valued"), 2 * i)
                    for t in range(NT):
                        o = value_b[:, 128 * (i % 2) + 64 * t:128 * (i % 2) + 64 * t + 64]
                        parts = [(g, kb) for g in range(ng) for kb in range(t + 1)]
                        for z, (g, kb) in enumerate(parts):
                            v = V[:, kb, units_of(n)[g][3]:units_of(n)[g][3] + HD] if n < 24 \
                                else V2[:, kb, HD * (n - 24):HD * (n - 24) + HD]
                            lo = 0 if t == 0 else P + P * kb
                            mm = pe.matmul(o, PT[:, i % 2, g, lo:lo + P], v, start=(z == 0), stop=(z == len(parts) - 1))
                        mm.then_inc(S("value_product"), 1)
                if kind0 == "router":
                    pe.wait_ge(S("turn_free"), TURN["norm", 1, 1, 1] + 1)
                    pe.wait_ge(S("late_loaded"), 16 * N_LATE)
                    for t in range(NT):
                        for k in range(KT):
                            mm = pe.matmul(turn_b[:, N_EXP * t:N_EXP * t + N_EXP], xT[:, k, t * P:(t + 1) * P], w_router[:, k, :],
                                           start=(k == 0), stop=(k == KT - 1))
                    mm.then_inc(S("router_product"), 1)

            def up(w1, w3, f):
                for m, w in enumerate((w1, w3)):
                    for k in range(KT):
                        mm = pe.matmul(up_b[f][:, m * TOK:(m + 1) * TOK], w[:, k, f:ED:FT], xT[:, k, :],
                                       start=(k == 0), stop=(k == KT - 1))
                mm.then_inc(S(f"shared_up_{f}"), 1)

            def down(w2, f, first_of_all):
                for t in range(NT):
                    for hf in range(2):
                        mm = pe.matmul(acc_b[2 * t + hf][:, :], hT[:, f, t * P:(t + 1) * P], w2[:, f, hf * CH:hf * CH + CH],
                                       start=first_of_all, stop=False, skip_group_check=True)
                return mm

            j = JOB["shared_up",]
            job_ready(pe, j)
            pe.wait_ge(S("probsT"), len(UNITS))
            wv = view(j, "up")
            for f in range(FT):
                up(wv[:, 0], wv[:, 1], f)
            for n in (1, 2):
                bank_taken(pe, len(BANKED) - n)
            pe.wait_ge(S("logits"), len(UNITS))
            pe.wait_ge(S("taken_ready"), 2)
            pe.wait_ge(S("valued"), 64)
            tri = consts[:, C_TRI:C_TRI + P]
            pe.matmul(y_b[0][:, 0:NV], tri, taken[:, 0, :], start=True, stop=True)
            pe.matmul(y_b[0][:, NV:2 * NV], ones[:, :], taken[:, 0, :], start=True, stop=False)
            pe.matmul(y_b[0][:, NV:2 * NV], tri, taken[:, 1, :], start=False, stop=True)
            for t in range(NT):
                mm = pe.matmul(y_b[0][:, 2 * NV:2 * NV + 1], taken[:, t, :], ones[:, 0:1], start=(t == 0), stop=(t == 1))
            mm.then_inc(S("ranked"), 1)
            pe.wait_ge(S("used_ready"), 1)
            pe.wait_ge(S("router_exp"), 1)
            pe.matmul(y_b[1][:, 0:1], tri, used[:, :], start=True, stop=True).then_inc(S("places_counted"), 1)
            pe.wait_ge(S("ranks_ready"), NT)
            for t in range(NT):
                mm = pe.transpose(y_b[0][:, t * P:(t + 1) * P], ranks[:, t, :], ident)
            mm.then_inc(S("ranks_turned"), 1)
            pe.wait_ge(S("order_ready"), 1)
            pe.matmul(y_b[1][0:1, 0:NV], consts[:, C_EXP:C_EXP + 1], order[:, :], start=True, stop=True)
            pe.matmul(y_b[1][0:1, NV:2 * NV], consts[:, C_COL:C_COL + 1], order[:, :], start=True, stop=True)
            pe.matmul(y_b[1][0:1, 2 * NV:2 * NV + 1], used[:, :], ones[:, 0:1], start=True, stop=True)\
              .then_inc(S("list_product"), 1)
            pe.wait_ge(S("work_ready"), 2)
            for k in range(KT // 2):
                for t in range(NT):
                    if k >= 1:
                        pe.wait_ge(S("x_lo_ready"), 2 * (k - 1) + t + 1)
                    for b in range(2):
                        mm = pe.transpose(y_b[t][:, b * P:(b + 1) * P], xT[:, 2 * k + b, t * P:(t + 1) * P], ident)
                    mm.then_inc(S("h2_turned"), 1)
            j = JOB["shared_down",]
            job_ready(pe, j)
            for f in range(FT):
                pe.wait_ge(S(f"shared_h_{f}"), 1)
                mm = down(view(j, "down"), f, f == 0)
            mm.then_inc(S("block_done"), 1)

            def gather(r, q, z):
                for b in range(4):
                    for t in range(NT):
                        mm = pe.matmul(gather_b[2 * q + z][:, b * P:(b + 1) * P], (x_hi, x_lo)[z][:, t, 4 * q + b, :],
                                       pick[:, r % 2, t, :], start=(t == 0), stop=(t == 1))
                mm.then_inc(S(f"gathered_{q}{z}"), 1)

            DOWN_PASSES = [(f, 0, z) for f in range(FT) for z in range(2)] + [(f, 1, 0) for f in range(FT)]
            pe.wait_ge(S("x_lo_ready"), KT)
            pe.wait_ge(S("pick_ready"), 1)
            for q in range(2):
                for z in range(2):
                    gather(0, q, z)
            n_work = pe.value_load(work[0:1, 0:1], min_val=0, max_val=MAX_WORK)
            with pe.Fori(0, -(-MAX_WORK // BODY)) as m4, pe.If(n_work > m4 * BODY):
                for r in range(BODY):
                    i = m4 * BODY + r
                    nxt = (r + 1) % BODY
                    with pe.If(n_work > i):
                        pe.wait_ge(S("block_ready_11"), i + 1)
                        for t in range(NT):
                            mm = pe.matmul(turned_b[:, ED:ED + 1], pick[:, r % 2, t, :].bitcast(F32),
                                           col4[:, r, NT + t:NT + t + 1], start=(t == 0), stop=(t == 1))
                        mm.then_inc(S("gates_gathered"), 1)
                        for k in range(KT):
                            if k % 4 == 0:
                                pe.wait_ge(S("up_lo"), 4 * i + k // 2 + 2)
                            for n, (zx, zw) in enumerate(PASSES):
                                mm = pe.matmul(hidden_b[:, :], (xe_hi, xe_lo)[zx][:, k, :],
                                               (up_hi, up_lo)[zw][:, r % 2, k].rearrange("p m n -> p (m n)"),
                                               start=(k == 0 and n == 0), stop=(k == KT - 1 and n == 2))
                        mm.then_inc(S("up_done"), 1)
                        pe.wait_ge(S("pick_ready"), i + 2)
                        gather(nxt, 0, 0)
                        gather(nxt, 0, 1)
                        pe.wait_ge(S("h_done"), i + 1)
                        pe.wait_ge(S("gates_ready"), i + 1)
                        for f in range(FT):
                            mm = pe.transpose(turned_b[:, f * P:(f + 1) * P], he[:, f:ED:FT], ident)
                        mm.then_inc(S("h_turned"), 1)
                        gather(nxt, 1, 0)
                        pe.wait_ge(S("h_hi_ready"), i + 1)
                        pe.wait_ge(S("down_lo"), 2 * i + 2)
                        for hf in range(2):
                            pe.wait_ge(S(f"block_ready_0{hf}"), i + 2)
                            for n, (f, zh, zw) in enumerate(DOWN_PASSES):
                                if hf == 0 and n == 2 * FT:
                                    pe.wait_ge(S("h_lo_ready"), i + 1)
                                mm = pe.matmul(y_b[hf][:, :], (h_hi, h_lo)[zh][:, f, :],
                                               (down_hi, down_lo)[zw][:, f, hf * CH:hf * CH + CH],
                                               start=(n == 0), stop=(n == len(DOWN_PASSES) - 1))
                            mm.then_inc(S(f"down_{hf}"), 1)
                        gather(nxt, 1, 1)
                        pe.wait_ge(S("put_ready"), i + 1)
                        for hf in range(2):
                            pe.wait_ge(S(f"y_lo_{hf}"), i + 1)
                            for t in range(NT):
                                for part in (y_hi, y_lo):
                                    mm = pe.matmul(acc_b[2 * t + hf][:, :], put[:, r % 2, t * P:(t + 1) * P],
                                                   part[:, hf * CH:hf * CH + CH], start=False, stop=False,
                                                   skip_group_check=True)
                        mm.then_inc(S("block_done"), 1)
            pe.matmul(y_b[0][0:1, 0:1], ones[:, 0:1], ones[:, 0:1], start=True, stop=True).then_inc(S("experts_summed"), 1)


def rel_bucket(dist):
    dist = np.maximum(dist, 0)
    ratio = (np.log(np.maximum(dist, 1).astype(np.float32) / np.float32(16)) / np.float32(math.log(2048 / 16)))
    large = np.minimum(16 + (ratio * np.float32(16)).astype(np.int32), 31)
    return np.where(dist < 16, dist, large)


def shape_constants():
    sq = np.zeros((P, C_N), np.float32)
    p = np.arange(P)[:, None]
    sq[:, C_ID:C_ID + P] = np.eye(P)
    sq[:, C_CAUS:C_CAUS + 2 * P] = np.where(P + p - np.arange(2 * P)[None, :] >= 0, 0.0, NEG)
    sq[:, C_FREQ:C_FREQ + 8] = (np.float32(500000.0) ** (-np.arange(8, dtype=np.float32) / np.float32(8)))[None, :]
    sq[:, C_TRI:C_TRI + P] = p < np.arange(P)[None, :]
    sq[:, C_IOTA:C_IOTA + P] = np.arange(P)[None, :]
    sq[:, C_THR_ROW:C_THR_ROW + NV] = P * (np.arange(NV)[None, :] // N_EXP) - FAR
    sq[:, C_COL] = np.arange(P)
    sq[:, C_EXP] = np.arange(P) % N_EXP
    sq[:, C_THR] = P * (np.arange(P) // N_EXP)
    dist = np.arange(NREL_PAD) - 127
    hot = (np.arange(32)[:, None] == rel_bucket(dist)[None, :]).astype(np.float32)
    mask = np.zeros((40, NREL_PAD), np.float32)
    for row in range(40):
        ok = dist >= 0
        if 8 <= row < 32:
            w, d = ((128, 1), (512, 4), (2048, 16))[(row - 8) // 8]
            ok = ok & (dist <= w) & (dist % d == 0)
        if row >= 32:
            ok = ok & (dist < 128)
        mask[row] = np.where(ok, 0.0, NEG)
    return {"c_square": sq, "c_hot": hot, "c_mask": mask}


_INS = ["x", "ln_g", "w_in", "qk_g", "sinks", "w_branch", "w_out", "rel_bias", "c_2", "positions_2", "norm1_g_2",
        "norm2_g_2", "w_ada_2", "b_ada_2", "w_in_2", "conv_w_2", "q_norm_g_2", "k_norm_g_2", "kidx_norm_g_2",
        "w_out_2", "w_router_2", "router_bias_2", "w1_2", "w3_2", "w2_2", "ws1_2", "ws3_2", "ws2_2"]


def kernel(**inputs):
    import concourse.bacc as _bacc
    from concourse.bass_utils import run_bass_kernel_spmd as _run

    nc = _bacc.Bacc("TRN2", target_bir_lowering=False, num_devices=1)
    arrays, args = {}, {}
    given = {name: inputs[name] for name in _INS}
    given.update(shape_constants())
    for name, value in given.items():
        v = np.ascontiguousarray(value)
        arrays[f"in_{name}_dram"] = v
        args[name] = nc.dram_tensor(f"in_{name}_dram", v.shape, mybir.dt.from_np(v.dtype), kind="ExternalInput").ap()
    out = nc.dram_tensor("out_0_dram", (1, TOK, DM), F32, kind="ExternalOutput").ap()
    build(nc, args, out)
    r = _run(nc, [arrays], core_ids=[0])
    return r.results[0]["out_0_dram"]
```
